# Optimizing a Trainium2 kernel written in Bass

```python
import math
import jax
import jax.numpy as jnp
from jax import lax
import numpy as np

D_MODEL = 1024
BATCH = 1
SEQ = 256
DEPTH = 2

N_MEM = 256
HEAD_DIM = 64
EPS = 1e-6
MASK_VALUE = -1e9
LB_FLOOR = 1e-30
FOX_W = D_MODEL // 4
FOX_H = FOX_W // HEAD_DIM
FOX_BLOCK = 128
HG_W = D_MODEL // 4
HG_H = HG_W // HEAD_DIM
HG_K = HEAD_DIM
HG_V = HEAD_DIM
HG_CHUNK = 64
M2_W = D_MODEL // 2
M2_P = HEAD_DIM
M2_H = M2_W // M2_P
M2_G = 2
M2_N = 128
M2_CONV = 4
M2_CHUNK = 128
M2_CONV_CH = M2_W + 2 * M2_G * M2_N
D_MIX = FOX_W + HG_W + M2_W
IN_SPLITS = (FOX_W, FOX_W, FOX_W, FOX_H, HG_W, HG_W, HG_W, HG_W, M2_W, M2_CONV_CH, M2_H)
D_IN = 3 * FOX_W + FOX_H + 4 * HG_W + M2_W + M2_CONV_CH + M2_H
XA_H = 4
XA_D = D_MODEL // XA_H
D_FF = 128 * ((8 * D_MODEL // 3 + 127) // 128)
N_EXPERTS = 8
TOP_K = 2
MOE_BLOCK = 128
N_DENSE = (DEPTH + 1) // 2
N_MOE = DEPTH // 2

kernel_name = 'hybrid_fox_hgrn2_ssd_moe_trunk'

def rms_norm(x, w):
    xf = x.astype(jnp.float32)
    y = xf * lax.rsqrt(jnp.mean(xf * xf, axis=-1, keepdims=True) + EPS)
    return (y * w.astype(jnp.float32)).astype(x.dtype)

def _causal_mask(n):
    return jnp.tril(jnp.ones((n, n), dtype=bool))

def masked_exp(x, mask):
    return jnp.where(mask, jnp.exp(jnp.where(mask, x, 0.0)), 0.0)

def fox_attention(q, k, v, log_f):
    b, s, h, d = q.shape
    nblk = s // FOX_BLOCK
    scale = d ** -0.5
    c = jnp.cumsum(log_f, axis=1).transpose(0, 2, 1)
    kt = k.transpose(0, 2, 1, 3)
    vt = v.transpose(0, 2, 1, 3)
    qb = q.reshape(b, nblk, FOX_BLOCK, h, d).transpose(1, 0, 3, 2, 4)
    cb = c.reshape(b, h, nblk, FOX_BLOCK).transpose(2, 0, 1, 3)
    kpos = jnp.arange(s)

    def query_block(args):
        q_i, c_i, i = args
        logits = jnp.einsum('bhqd,bhkd->bhqk', q_i, kt, preferred_element_type=jnp.float32) * scale
        logits = logits + c_i[..., :, None] - c[:, :, None, :]
        qpos = i * FOX_BLOCK + jnp.arange(FOX_BLOCK)
        logits = jnp.where(kpos[None, :] <= qpos[:, None], logits, MASK_VALUE)
        p = jax.nn.softmax(logits, axis=-1)
        return jnp.einsum('bhqk,bhkd->bhqd', p.astype(vt.dtype), vt)

    o = lax.map(query_block, (qb, cb, jnp.arange(nblk)))
    return o.transpose(1, 0, 3, 2, 4).reshape(b, s, h, d)

def hgrn2_recurrence(q, k, v, log_f):
    b, s, h, dk = q.shape
    dv = v.shape[-1]
    n = s // HG_CHUNK
    causal = _causal_mask(HG_CHUNK)[:, :, None]

    def to_chunks(t):
        return t.astype(jnp.float32).reshape(b, n, HG_CHUNK, h, t.shape[-1]).transpose(1, 0, 3, 2, 4)

    def chunk_step(state, inp):
        q_c, k_c, v_c, g_c = inp
        cum = jnp.cumsum(g_c, axis=2)
        diff = cum[:, :, :, None, :] - cum[:, :, None, :, :]
        decay = masked_exp(diff, causal)
        scores = jnp.einsum('bhtsk,bhsk->bhts', q_c[:, :, :, None, :] * decay, k_c)
        o = jnp.einsum('bhts,bhsv->bhtv', scores, v_c) + jnp.einsum('bhtk,bhkv->bhtv', q_c * jnp.exp(cum), state)
        last = cum[:, :, -1:, :]
        state = jnp.exp(last[:, :, 0, :, None]) * state + jnp.einsum('bhsk,bhsv->bhkv', k_c * jnp.exp(last - cum), v_c)
        return state, o

    state0 = jnp.zeros((b, h, dk, dv), jnp.float32)
    _, o = lax.scan(chunk_step, state0, (to_chunks(q), to_chunks(k), to_chunks(v), to_chunks(log_f)))
    return o.transpose(1, 0, 3, 2, 4).reshape(b, s, h, dv)

def causal_depthwise_conv(x, w, bias):
    width, ch = w.shape
    y = lax.conv_general_dilated(x, w[:, None, :].astype(x.dtype), window_strides=(1,), padding=[(width - 1, 0)], dimension_numbers=('NWC', 'WIO', 'NWC'), feature_group_count=ch)
    return y + bias.astype(y.dtype)

def ssd_chunked(x, dt, a, bm, cm):
    b, s, h, p = x.shape
    g, nst = bm.shape[-2:]
    e = h // g
    n = s // M2_CHUNK
    ln = M2_CHUNK
    xc = (x.astype(jnp.float32) * dt[..., None]).reshape(b, n, ln, g, e, p)
    bc = bm.astype(jnp.float32).reshape(b, n, ln, g, nst)
    cc = cm.astype(jnp.float32).reshape(b, n, ln, g, nst)
    a_dt = (dt * a).reshape(b, n, ln, g, e).transpose(0, 3, 4, 1, 2)
    a_cum = jnp.cumsum(a_dt, axis=-1)
    seg = a_cum[..., :, None] - a_cum[..., None, :]
    lmat = masked_exp(seg, _causal_mask(ln))
    cb = jnp.einsum('bclgn,bcsgn->bgcls', cc, bc)
    y_diag = jnp.einsum('bgecls,bcsgep->bclgep', cb[:, :, None] * lmat, xc)
    decay_states = jnp.exp(a_cum[..., -1:] - a_cum).transpose(0, 3, 4, 1, 2)
    states = jnp.einsum('bclgn,bclgep->bcgepn', bc, xc * decay_states[..., None])
    cx = jnp.cumsum(jnp.pad(a_cum[..., -1], ((0, 0), (0, 0), (0, 0), (1, 0))), axis=-1)
    decay_chunk = masked_exp(cx[..., :, None] - cx[..., None, :], _causal_mask(n + 1))
    states = jnp.concatenate([jnp.zeros_like(states[:, :1]), states], axis=1)
    new_states = jnp.einsum('bgezc,bcgepn->bzgepn', decay_chunk, states)[:, :-1]
    state_decay_out = jnp.exp(a_cum).transpose(0, 3, 4, 1, 2)
    y_off = jnp.einsum('bclgn,bcgepn->bclgep', cc, new_states) * state_decay_out[..., None]
    return (y_diag + y_off).reshape(b, s, h, p)

def mamba2_group(z, xbc, dt_raw, conv_w, conv_b, dt_bias, a_log, d_skip, norm_w):
    b, s, _ = z.shape
    xbc = jax.nn.silu(causal_depthwise_conv(xbc, conv_w, conv_b))
    xs, bm, cm = jnp.split(xbc, [M2_W, M2_W + M2_G * M2_N], axis=-1)
    xs = xs.reshape(b, s, M2_H, M2_P)
    dt = jax.nn.softplus(dt_raw.astype(jnp.float32) + dt_bias.astype(jnp.float32))
    a = -jnp.exp(a_log.astype(jnp.float32))
    y = ssd_chunked(xs, dt, a, bm.reshape(b, s, M2_G, M2_N), cm.reshape(b, s, M2_G, M2_N))
    y = y + d_skip.astype(jnp.float32)[:, None] * xs.astype(jnp.float32)
    y = y.reshape(b, s, M2_W) * jax.nn.silu(z.astype(jnp.float32))
    y = rms_norm(y.reshape(b, s, M2_G, M2_W // M2_G), norm_w.reshape(M2_G, M2_W // M2_G))
    return y.reshape(b, s, M2_W)

def parallel_mixer(h, norm_w, w_in, fox_f_bias, fox_norm_w, hg_lb, hg_norm_w, conv_w, conv_b, dt_bias, a_log, d_skip, m2_norm_w, w_out):
    b, s, _ = h.shape
    split_at = [int(i) for i in np.cumsum(IN_SPLITS)[:-1]]
    fq, fk, fv, ff, hq, hf, hi, hgate, mz, mxbc, mdt = jnp.split(rms_norm(h, norm_w) @ w_in, split_at, axis=-1)
    fox_log_f = jax.nn.log_sigmoid(ff.astype(jnp.float32) + fox_f_bias.astype(jnp.float32))
    o_fox = fox_attention(fq.reshape(b, s, FOX_H, HEAD_DIM), fk.reshape(b, s, FOX_H, HEAD_DIM), fv.reshape(b, s, FOX_H, HEAD_DIM), fox_log_f)
    o_fox = rms_norm(o_fox, fox_norm_w.reshape(FOX_H, HEAD_DIM)).reshape(b, s, FOX_W)
    lb = hg_lb.reshape(HG_H, HG_K)
    f_raw = hf.astype(jnp.float32).reshape(b, s, HG_H, HG_K)
    hg_log_f = jnp.logaddexp(jnp.log(jnp.maximum(lb, LB_FLOOR)), jnp.log1p(-lb) + jax.nn.log_sigmoid(f_raw))
    hg_k = (1.0 - lb) * jax.nn.sigmoid(-f_raw)
    hg_q = jax.nn.silu(hq.astype(jnp.float32)).reshape(b, s, HG_H, HG_K) * (HG_K ** -0.5)
    o_hg = hgrn2_recurrence(hg_q, hg_k, hi.reshape(b, s, HG_H, HG_V), hg_log_f)
    o_hg = rms_norm(o_hg, hg_norm_w.reshape(HG_H, HG_V)) * jax.nn.silu(hgate.astype(jnp.float32).reshape(b, s, HG_H, HG_V))
    o_hg = o_hg.reshape(b, s, HG_W)
    o_m2 = mamba2_group(mz, mxbc, mdt, conv_w, conv_b, dt_bias, a_log, d_skip, m2_norm_w)
    o = jnp.concatenate([o_fox.astype(h.dtype), o_hg.astype(h.dtype), o_m2.astype(h.dtype)], axis=-1)
    return o @ w_out

def memory_cross_attention(h, mem, norm_w, mem_norm_w, w_q, w_kv, w_o):
    b, s, _ = h.shape
    m = mem.shape[1]
    q = (rms_norm(h, norm_w) @ w_q).reshape(b, s, XA_H, XA_D)
    k, v = jnp.split(rms_norm(mem, mem_norm_w) @ w_kv, 2, axis=-1)
    k = k.reshape(b, m, XA_H, XA_D)
    v = v.reshape(b, m, XA_H, XA_D)
    logits = jnp.einsum('bshd,bmhd->bhsm', q, k, preferred_element_type=jnp.float32) * (XA_D ** -0.5)
    p = jax.nn.softmax(logits, axis=-1)
    o = jnp.einsum('bhsm,bmhd->bshd', p.astype(v.dtype), v).reshape(b, s, XA_H * XA_D)
    return o @ w_o

def swiglu(x, w1, w2):
    gate, up = jnp.split(x @ w1, 2, axis=-1)
    return (jax.nn.silu(gate) * up) @ w2

def moe_ffn(x, router_w, w1, w2):
    b, s, d = x.shape
    xt = x.reshape(-1, d)
    n_tok = xt.shape[0]
    logits = (xt @ router_w).astype(jnp.float32)
    top_logit, top_idx = lax.top_k(logits, TOP_K)
    gates = jax.nn.softmax(top_logit, axis=-1)
    n_assign = n_tok * TOP_K
    e_flat = top_idx.reshape(-1)
    g_flat = gates.reshape(-1)
    t_flat = jnp.arange(n_assign) // TOP_K
    order = jnp.argsort(e_flat)
    e_sorted = e_flat[order]
    counts = jnp.bincount(e_flat, length=N_EXPERTS)
    starts = jnp.cumsum(counts) - counts
    padded = (counts + MOE_BLOCK - 1) // MOE_BLOCK * MOE_BLOCK
    pends = jnp.cumsum(padded)
    pstarts = pends - padded
    dest = pstarts[e_sorted] + (jnp.arange(n_assign) - starts[e_sorted])
    cap = ((n_assign + MOE_BLOCK - 1) // MOE_BLOCK + N_EXPERTS) * MOE_BLOCK
    slot_tok = jnp.zeros((cap,), jnp.int32).at[dest].set(t_flat[order].astype(jnp.int32))
    slot_gate = jnp.zeros((cap,), jnp.float32).at[dest].set(g_flat[order])
    n_blk = cap // MOE_BLOCK
    blk_expert = jnp.minimum(jnp.searchsorted(pends, jnp.arange(n_blk) * MOE_BLOCK, side='right'), N_EXPERTS - 1)
    xb = xt[slot_tok].reshape(n_blk, MOE_BLOCK, d)

    def expert_group(args):
        x_blk, e = args
        return swiglu(x_blk, w1[e], w2[e])

    yb = lax.map(expert_group, (xb, blk_expert)).reshape(cap, d)
    yb = yb * slot_gate[:, None].astype(yb.dtype)
    y = jnp.zeros_like(xt).at[slot_tok].add(yb)
    return y.reshape(b, s, d)

def setup_inputs(seed: int = 0) -> dict:
    key = jax.random.key(seed)
    ks = jax.random.split(key, 27)
    f32 = jnp.float32

    def normal(k, shape, scale):
        return jax.random.normal(k, shape, f32) * scale

    def gain(k, shape):
        return 1.0 + 0.05 * jax.random.normal(k, shape, f32)

    dt0 = jnp.exp(jax.random.uniform(ks[10], (DEPTH, M2_H), f32) * (math.log(0.1) - math.log(0.001)) + math.log(0.001))
    return {
        'x': normal(ks[0], (BATCH, SEQ, D_MODEL), 1.0),
        'mem': normal(ks[1], (BATCH, N_MEM, D_MODEL), 1.0),
        'mix_norm_w': gain(ks[2], (DEPTH, D_MODEL)),
        'w_in': normal(ks[3], (DEPTH, D_MODEL, D_IN), D_MODEL ** -0.5),
        'fox_f_bias': 2.0 + 0.5 * jax.random.normal(ks[4], (DEPTH, FOX_H), f32),
        'fox_norm_w': gain(ks[5], (DEPTH, FOX_W)),
        'hg_lb_raw': normal(ks[6], (DEPTH, HG_W), 0.1),
        'hg_norm_w': gain(ks[7], (DEPTH, HG_W)),
        'm2_conv_w': normal(ks[8], (DEPTH, M2_CONV, M2_CONV_CH), M2_CONV ** -0.5),
        'm2_conv_b': normal(ks[9], (DEPTH, M2_CONV_CH), 0.02),
        'm2_dt_bias': dt0 + jnp.log(-jnp.expm1(-dt0)),
        'm2_a_log': jnp.log(jax.random.uniform(ks[11], (DEPTH, M2_H), f32, minval=1.0, maxval=16.0)),
        'm2_d': 1.0 + 0.1 * jax.random.normal(ks[12], (DEPTH, M2_H), f32),
        'm2_norm_w': gain(ks[13], (DEPTH, M2_W)),
        'w_out': normal(ks[14], (DEPTH, D_MIX, D_MODEL), D_MIX ** -0.5),
        'xa_norm_w': gain(ks[15], (DEPTH, D_MODEL)),
        'xa_mem_norm_w': gain(ks[16], (DEPTH, D_MODEL)),
        'xa_w_q': normal(ks[17], (DEPTH, D_MODEL, XA_H * XA_D), D_MODEL ** -0.5),
        'xa_w_kv': normal(ks[18], (DEPTH, D_MODEL, 2 * XA_H * XA_D), D_MODEL ** -0.5),
        'xa_w_o': normal(ks[19], (DEPTH, XA_H * XA_D, D_MODEL), (XA_H * XA_D) ** -0.5),
        'ffn_norm_w': gain(ks[20], (DEPTH, D_MODEL)),
        'ffn_w1': normal(ks[21], (N_DENSE, D_MODEL, 2 * D_FF), D_MODEL ** -0.5),
        'ffn_w2': normal(ks[22], (N_DENSE, D_FF, D_MODEL), D_FF ** -0.5),
        'moe_router': normal(ks[23], (N_MOE, D_MODEL, N_EXPERTS), D_MODEL ** -0.5),
        'moe_w1': normal(ks[24], (N_MOE, N_EXPERTS, D_MODEL, 2 * D_FF), D_MODEL ** -0.5),
        'moe_w2': normal(ks[25], (N_MOE, N_EXPERTS, D_FF, D_MODEL), D_FF ** -0.5),
        'final_norm_w': gain(ks[26], (D_MODEL,)),
    }

def reference(x, mem, mix_norm_w, w_in, fox_f_bias, fox_norm_w, hg_lb_raw, hg_norm_w, m2_conv_w, m2_conv_b, m2_dt_bias, m2_a_log, m2_d, m2_norm_w, w_out, xa_norm_w, xa_mem_norm_w, xa_w_q, xa_w_kv, xa_w_o, ffn_norm_w, ffn_w1, ffn_w2, moe_router, moe_w1, moe_w2, final_norm_w):
    lb_p = jax.nn.softmax(hg_lb_raw.astype(jnp.float32), axis=0)
    hg_lb = jnp.cumsum(lb_p, axis=0) - lb_p[0]
    h = x
    for layer in range(DEPTH):
        h = h + parallel_mixer(h, mix_norm_w[layer], w_in[layer], fox_f_bias[layer], fox_norm_w[layer], hg_lb[layer], hg_norm_w[layer], m2_conv_w[layer], m2_conv_b[layer], m2_dt_bias[layer], m2_a_log[layer], m2_d[layer], m2_norm_w[layer], w_out[layer])
        h = h + memory_cross_attention(h, mem, xa_norm_w[layer], xa_mem_norm_w[layer], xa_w_q[layer], xa_w_kv[layer], xa_w_o[layer])
        hn = rms_norm(h, ffn_norm_w[layer])
        if layer % 2 == 0:
            h = h + swiglu(hn, ffn_w1[layer // 2], ffn_w2[layer // 2])
        else:
            h = h + moe_ffn(hn, moe_router[layer // 2], moe_w1[layer // 2], moe_w2[layer // 2])
    return rms_norm(h, final_norm_w)


_drawn_inputs = setup_inputs


def setup_inputs(seed=0):
    import zlib

    import numpy as np

    out = dict(_drawn_inputs(seed))
    spreads = {}
    factors = {'hg_lb_raw': 11.419, 'xa_norm_w': 4.615, 'xa_mem_norm_w': 2.735}
    for name, (base, spread) in spreads.items():
        noise = np.random.default_rng([zlib.crc32(name.encode()), seed]).standard_normal(out[name].shape)
        drawn = base * np.exp(spread * noise) if base else spread * noise
        out[name] = jnp.asarray(drawn.astype(out[name].dtype))
    for name, factor in factors.items():
        out[name] = (out[name] * factor).astype(out[name].dtype)
    return out
```

```python
from contextlib import ExitStack

import numpy as np

import concourse.bass as bass
from concourse import mybir

ALU = mybir.AluOpType
ACT = mybir.ActivationFunctionType
F32 = mybir.dt.float32
U32 = mybir.dt.uint32
AX = mybir.AxisListType

P = 128
D = 1024
S = 256
NT = S // P
KT = D // P
DEPTH = 2
DFF = 2816
NF = DFF // P
NE = 8
DH = 64
FOX_H, HG_H, M2_H = 4, 4, 8
EPS = 1e-6
FLOOR = 1e-30
NEG = -1e30
LEVELS = (1, 2, 4, 8, 16, 32, 64)

CW = 2048
RING = 6
LIN = 17
LIN_CHUNKS = 2 * LIN
W1_CHUNKS = NF
W2_CHUNKS = NF // 2
FFN_CHUNKS = W1_CHUNKS + W2_CHUNKS
PROJ = (("hq_hf", "T"), ("gate_small", "R"), ("xbc0", "T"), ("xbc1", "T"), ("fq_fk", "T"), ("fv_hi", "R"),
        ("z", "R"), ("xk0", "T"), ("xk1", "T"), ("xv0", "R"), ("xv1", "R"), ("out0", "R"), ("out1", "R"),
        ("xq0", "T"), ("xq1", "T"), ("xo0", "R"), ("xo1", "R"))
PIDX = {name: i for i, (name, _) in enumerate(PROJ)}
DVE_EVAC = ("out0", "out1", "xo0", "xo1")
assert len(PROJ) == LIN

_PER_LAYER = (("mix_w", 8), ("xa_w", 8), ("mem_w", 8), ("ffn_w", 8), ("out_w", 8), ("conv_w", 32), ("conv_b", 8),
              ("fox_b", 4), ("dt_b", 8), ("a_log", 8), ("m2_d", 8))
PCOL = {}
_n = 0
for _l in range(DEPTH):
    for _name, _w in _PER_LAYER:
        PCOL[_name, _l] = (_n, _n + _w)
        _n += _w
for _name, _w in (("lb_raw", 4), ("router", KT * NE), ("final_w", D)):
    PCOL[_name] = (_n, _n + _w)
    _n += _w
NPAR = _n

CCOL = {}
_n = 0
for _name, _w in (("ident", P), ("neg", P), ("upto", P), ("ones", P), ("after", P), ("m2mask", 3 * P),
                  ("restart", 2 * S), ("iota", NE), ("minus_half", 20)):
    CCOL[_name] = (_n, _n + _w)
    _n += _w
NCONST = _n


def constants():
    r = np.arange(P)
    upto = (r[:, None] <= r[None, :]).astype(np.float32)
    one = np.ones((P, P), np.float32)
    restart = np.broadcast_to((np.arange(2 * S) % 64 != 0).astype(np.float32), (P, 2 * S))
    parts = [np.eye(P, dtype=np.float32), (upto - np.eye(P)) * NEG, upto, one, (r[:, None] > r[None, :]) * 1.0,
             upto, one, upto, restart, np.broadcast_to(np.arange(NE), (P, NE)), np.full((P, 20), -0.5)]
    return np.concatenate([p.astype(np.float32) for p in parts], axis=1)


def level_masks():
    r = np.arange(P)
    masks = [r[:, None] == r[None, :]]
    for half in LEVELS:
        same = (r[:, None] // (2 * half)) == (r[None, :] // (2 * half))
        masks.append(same & ((r[:, None] // half) % 2 == 0) & ((r[None, :] // half) % 2 == 1))
    return np.stack(masks, axis=1).astype(np.uint32).reshape(P, -1)


def build(nc, x, mem, par, con, lvl, lin_w, ffn_w, out):
    groups = []
    for layer in range(DEPTH):
        groups += [(name, layer) for name, _ in PROJ]
        if layer == 0:
            groups += [("w1", j) for j in range(NF // 2)]
    GI = {g: i for i, g in enumerate(groups)}

    def by_dve(g):
        return g[0] == "w1" or g[0] in DVE_EVAC

    def evac_count(g):
        return sum(by_dve(q) == by_dve(g) for q in groups[:GI[g] + 1])

    DVE0 = sum(by_dve(g) for g in groups)

    def chunk0(layer, name=None):
        base = layer * (LIN_CHUNKS + FFN_CHUNKS)
        return base + (LIN_CHUNKS if name is None else 2 * PIDX[name])

    MOE0 = chunk0(1)

    with ExitStack() as ctx:
        def sb(name, shape, dt=F32):
            return ctx.enter_context(nc.sbuf_tensor(name, shape, dt))[:]

        def sem(name):
            return ctx.enter_context(nc.semaphore(name))

        ring = sb("ring", [P, RING, CW])
        h = sb("h", [P, NT, D])
        xn = sb("xn", [P, NT, D])
        xT = sb("xT", [P, KT, S])
        memT = sb("memT", [P, KT, S])
        memTw = sb("memTw", [P, KT, S])
        kX = sb("kX", [P, KT, S])
        vX = sb("vX", [P, NT, D])
        params = sb("params", [P, NPAR])
        consts = sb("consts", [P, NCONST])
        lmask = sb("lmask", [P, len(LEVELS) + 1, P], U32)
        small = sb("small", [P, 512])
        arena = sb("arena", [P, 20480])

        top = [0]

        def small_(n):
            top[0] += n
            assert top[0] <= 512
            return small[:, top[0] - n:top[0]]

        def carve(at, *shape):
            n = int(np.prod(shape))
            assert at + n <= 20480, at + n
            v = arena[:, at:at + n]
            if len(shape) == 1:
                return v
            names = "abcd"[:len(shape)]
            return v.rearrange(f"p ({' '.join(names)}) -> p {' '.join(names)}",
                               **{c: s for c, s in zip(names[1:], shape[1:])})

        def const(name):
            return consts[:, CCOL[name][0]:CCOL[name][1]]

        def par_(name, layer=None):
            a, b = PCOL[name if layer is None else (name, layer)]
            return params[:, a:b]

        hqT = carve(0, 2, S)
        hfT = carve(512, 2, S)
        gate = carve(1024, NT, 256)
        zs = carve(1536, NT, 512)
        fqT = carve(2560, 2, S)
        fkT = carve(3072, 2, S)
        vtok = carve(3584, NT, 512)
        xraw = carve(4608, 8, S + 3)
        xcv = carve(6688, 8, S)
        AUf = carve(8736, NT, FOX_H, P)
        ABf = carve(9760, FOX_H, P)
        Pf = carve(10272, FOX_H, 3 * P)
        PTf = carve(11808, FOX_H, 3, P)
        he = carve(13344, 2 * S)
        hr = carve(13856, 2 * S)
        hk = carve(14368, 2 * S)
        hl = carve(14880, 2 * S)
        hc = carve(15392, 2 * S)
        Dl = carve(15904, 2, 2 * S)
        Ql = carve(16928, 2, 2 * S)
        Kl = carve(17952, 2, 2 * S)
        ScT = carve(18976, FOX_H * NT, P)
        ScO = carve(8736, HG_H, P)
        El = carve(9248, 2, 2 * S)
        CBs = carve(13344, 2, 3 * P)
        xs = carve(14112, NT, 512)
        xcd = carve(15136, NT, 512)
        ALm = carve(16160, NT, M2_H, P)
        ABm = carve(18208, M2_H, P)
        Mm = carve(10272, M2_H, 3 * P)
        ytmp = carve(8736, NT, 512)
        sq = carve(4608, NT, D)
        qX = carve(0, KT, S)
        Px = carve(2048, 4 * NT, S)
        PTx = carve(4096, 4, 2, S)
        hT = carve(8192, NF, S)
        silu = carve(14000, 2, 2, S)

        raw12 = small_(NT * 12).rearrange("p (t c) -> p t c", c=12)
        X12, AX12, EX12, Z12, ZZ12, PO12, SP12, A12 = (
            small_(NT * 12).rearrange("p (t c) -> p t c", c=12) for _ in range(8))
        aexp = small_(8)
        lbe = small_(4)
        lb_s = small_(2)
        lb = small_(4)
        lb1m = small_(4)
        lbfl = small_(4)
        nmax = small_(8)
        rsum = small_(8)
        rinv = small_(8)
        ssq = small_(20)
        rstd = small_(20)
        lg = small_(NT * NE).rearrange("p (t e) -> p t e", e=NE)
        top8 = small_(NT * 8).rearrange("p (t e) -> p t e", e=8)
        idx8 = small_(NT * 8).rearrange("p (t e) -> p t e", e=8)
        idxf = small_(NT * 8).rearrange("p (t e) -> p t e", e=8)
        gd = small_(NT)
        ge = small_(NT)
        gs = small_(NT)
        g12 = small_(2 * NT).rearrange("p (k t) -> p k t", k=2)
        oh = small_(NT * NE).rearrange("p (t e) -> p t e", e=NE)
        gates = small_(NT * NE).rearrange("p (t e) -> p t e", e=NE)

        pb = ctx.enter_context(nc.psum_tensor("pb", [P, 8, 512], F32))[:]

        slot_loaded = [sem(f"slot_loaded{i}") for i in range(RING)]
        w_used = sem("w_used")
        inputs_in = sem("inputs_in")
        tables_in = sem("tables_in")
        out_sent = sem("out_sent")
        xn_ready = sem("xn_ready")
        turned = sem("turned")
        xT_act = sem("xT_act")
        xT_dve = sem("xT_dve")
        ss_ready = sem("ss_ready")
        rs_ready = sem("rs_ready")
        memw_ready = sem("memw_ready")
        lin_act = sem("lin_act")
        lin_dve = sem("lin_dve")
        dve_c = sem("dve_c")
        act_c = sem("act_c")
        pool_c = sem("pool_c")
        conv_ready = sem("conv_ready")
        xcv_ready = sem("xcv_ready")
        x12_ready = sem("x12_ready")
        e12_ready = sem("e12_ready")
        lbx_ready = sem("lbx_ready")
        fa_ready = sem("fa_ready")
        fox_lg = sem("fox_lg")
        fox_max = sem("fox_max")
        fox_p = sem("fox_p")
        fox_pt = sem("fox_pt")
        fox_ptc = sem("fox_ptc")
        fox_o = sem("fox_o")
        fox_ok = sem("fox_ok")
        hg_e = sem("hg_e")
        hg_f = sem("hg_f")
        hg_l = sem("hg_l")
        hg_d = sem("hg_d")
        hg_x = sem("hg_x")
        hg_qk = sem("hg_qk")
        hg_s = sem("hg_s")
        hg_sel = sem("hg_sel")
        hg_o = sem("hg_o")
        hg_ok = sem("hg_ok")
        m2_t = sem("m2_t")
        m2_xs = sem("m2_xs")
        m2_cb = sem("m2_cb")
        m2_a = sem("m2_a")
        m2_seg = sem("m2_seg")
        m2_e = sem("m2_e")
        m2_m = sem("m2_m")
        m2_y = sem("m2_y")
        xa_lg = sem("xa_lg")
        xa_max = sem("xa_max")
        xa_p = sem("xa_p")
        xa_pn = sem("xa_pn")
        xa_pt = sem("xa_pt")
        xa_pta = sem("xa_pta")
        xa_ptd = sem("xa_ptd")
        xa_o = sem("xa_o")
        xa_oc = sem("xa_oc")
        silu_ready = sem("silu_ready")
        ffn_added = sem("ffn_added")
        rt_lg = sem("rt_lg")
        rt_d = sem("rt_d")
        rt_e = sem("rt_e")
        fin_ready = sem("fin_ready")

        def slot(n):
            return ring[:, n % RING, :]

        def loaded(eng, n, later=0):
            eng.wait_ge(slot_loaded[n % RING], (n // RING + 1) * 16 + later)

        def projected(eng, name, layer):
            eng.wait_ge(w_used, chunk0(layer, name) + 2)

        NORMS = 1 + 3 * DEPTH + DEPTH

        def norm_no(layer, what):
            return 1 + 4 * layer + ("mix", "mixed", "xa", "ffn").index(what)

        block = ctx.enter_context(nc.Block())

        @block.sync
        def _(sp):
            sp.dma_start(params[:, :], par).then_inc(tables_in, 16)
            sp.dma_start(consts[:, :], con).then_inc(tables_in, 16)
            sp.dma_start(lmask[:, :, :].rearrange("p a b -> p (a b)"), lvl).then_inc(tables_in, 16)

            def load(n, src, later=0, always=False):
                if n >= RING or always:
                    sp.wait_ge(w_used, n - RING + 1 + later)
                sp.dma_start(slot(n), src).then_inc(slot_loaded[n % RING], 16)

            for layer in range(DEPTH):
                for c in range(LIN_CHUNKS):
                    load(chunk0(layer, PROJ[0][0]) + c, lin_w[layer * LIN_CHUNKS + c])
                if layer == 0:
                    for c in range(FFN_CHUNKS):
                        load(chunk0(0) + c, ffn_w[0, c])
            with sp.Fori(0, NE // 2) as pair:
                for e in range(2):
                    for c in range(FFN_CHUNKS):
                        load(MOE0 + e * FFN_CHUNKS + c, ffn_w[1 + pair * 2 + e, c],
                             later=pair * (2 * FFN_CHUNKS), always=True)
            sp.wait_ge(fin_ready, 1)
            sp.dma_start(out.rearrange("b (t p) d -> p (b t) d", p=P), xn[:, :, :]).then_inc(out_sent, 16)
            sp.wait_ge(out_sent, 16)

        @block.gpsimd
        def _(pool):
            order = []
            order.append(NT)
            for layer in range(DEPTH):
                order += [NT, 20, NT, NT]
            order.append(NT)
            for i, n in enumerate(order):
                pool.wait_ge(ss_ready, i + 1)
                if i == 0:
                    pool.wait_ge(tables_in, 48)
                nc.gpsimd.tensor_tensor(rstd[:, 0:n], ssq[:, 0:n], const("minus_half")[:, 0:n],
                                        ALU.pow).then_inc(rs_ready, 1)

        @block.scalar
        def _(act):
            chain = [0]

            def link(ins):
                chain[0] += 1
                ins.then_inc(act_c, 1)
                act.wait_ge(act_c, chain[0])

            act.dma_start(xn[:, :, :], mem.rearrange("b (t p) d -> p (b t) d", p=P)).then_inc(inputs_in, 16)
            act.dma_start(h[:, :, :], x.rearrange("b (t p) d -> p (b t) d", p=P)).then_inc(inputs_in, 16)
            act.wait_ge(tables_in, 48)

            def turn_out(no, dst, w):
                for b in (0, 2):
                    act.wait_ge(turned, 4 * no + b + 1)
                    for i in range(2):
                        k = 2 * b + i
                        ins = nc.scalar.activation(dst[:, k, :], pb[:, 4 + b, i * S:(i + 1) * S], ACT.Copy,
                                                   scale=1.0 if w is None else w[:, k:k + 1])
                ins.then_inc(xT_act, 1)

            def take(name, layer, *ops):
                g = GI[name, layer]
                projected(act, name, layer)
                b = 2 * (g % 2)
                for dst, a, z, func, scale, banks in ops:
                    if banks is None:
                        src = pb[:, b:b + 2, a:z]
                    else:
                        src = pb[:, b + banks, a:z]
                    ins = nc.scalar.activation(dst, src, func, scale=scale)
                ins.then_inc(lin_act, 1)

            def cols(ap):
                return ap.rearrange("p a s -> p (a s)")

            turn_out(0, memT, None)
            act.wait_ge(lbx_ready, 1)
            nc.scalar.activation(lbe, lbe, ACT.Exp).then_inc(lbx_ready, 1)

            for layer in range(DEPTH):
                turn_out(norm_no(layer, "mix"), xT, par_("mix_w", layer))
                take("hq_hf", layer, (cols(hqT), 0, 512, ACT.Silu, 1.0, 0), (cols(hfT), 0, 512, ACT.Copy, 1.0, 1))
                take("gate_small", layer, (gate, 0, 256, ACT.Silu, 1.0, None),
                     (raw12, 256, 268, ACT.Copy, 1.0, None))
                for i in range(2):
                    g = GI[f"xbc{i}", layer]
                    projected(act, f"xbc{i}", layer)
                    for b in range(2):
                        ins = nc.scalar.activation(
                            xraw[:, 4 * i + 2 * b:4 * i + 2 * b + 2, 3:],
                            pb[:, 2 * (g % 2) + b, :].rearrange("p (a s) -> p a s", a=2), ACT.Copy)
                    ins.then_inc(lin_act, 1)
                take("fq_fk", layer, (cols(fqT), 0, 512, ACT.Copy, DH ** -0.5, 0),
                     (cols(fkT), 0, 512, ACT.Copy, 1.0, 1))
                take("fv_hi", layer, (vtok, 0, 512, ACT.Copy, 1.0, None))
                take("z", layer, (zs, 0, 512, ACT.Silu, 1.0, None))
                act.wait_ge(conv_ready, layer + 1)
                nc.scalar.activation(xcv, xcv, ACT.Silu).then_inc(xcv_ready, 1)
                nc.scalar.preload_act_table_set("natural_log_exp_and_others")
                act.wait_ge(x12_ready, layer + 1)
                nc.scalar.activation(aexp, par_("a_log", layer), ACT.Exp)
                nc.scalar.activation(EX12, AX12, ACT.Exp, scale=-1.0).then_inc(e12_ready, 1)
                nc.scalar.activation(he, hfT.rearrange("p a s -> p (a s)"), ACT.Exp, scale=-1.0).then_inc(hg_e, 1)
                act.wait_ge(fox_max, layer + 1)
                for hd in range(FOX_H):
                    for t in range(NT):
                        a, z = (0, P) if t == 0 else (P, 3 * P)
                        i = t * FOX_H + hd
                        ins = nc.scalar.activation(Pf[:, hd, a:z], pb[:, 4 + hd, a:z], ACT.Exp,
                                                   bias=nmax[:, i:i + 1], accum_out=rsum[:, i:i + 1])
                ins.then_inc(fox_p, 1)
                act.wait_ge(hg_f, layer + 1)
                nc.scalar.activation(hl, hl, ACT.Ln).then_inc(hg_l, 1)
                take("xk0", layer, (kX[:, 0:4, :].rearrange("p (b a) s -> p b (a s)", b=2), 0, 512, ACT.Copy, 1.0, None))
                NL = len(LEVELS) + 1
                for lv in range(NL):
                    n = layer * NL + lv
                    act.wait_ge(hg_d, n + 1)
                    if n >= 2:
                        act.wait_ge(hg_qk, layer * (NL + 1) + 1 + lv - 1 if lv >= 2 else layer * (NL + 1))
                    nc.scalar.activation(El[:, lv % 2, :], Dl[:, lv % 2, :], ACT.Exp).then_inc(hg_x, 1)
                    if lv == 2:
                        take("xk1", layer, (kX[:, 4:8, :].rearrange("p (b a) s -> p b (a s)", b=2), 0, 512,
                                            ACT.Copy, 1.0, None))
                act.wait_ge(m2_t, layer + 1)
                act.wait_ge(hg_ok, layer + 1)
                nc.scalar.activation(xs, pb[:, 6:8, :], ACT.Copy).then_inc(m2_xs, 1)
                take("xv0", layer, (vX[:, :, 0:512], 0, 512, ACT.Copy, 1.0, None))
                for r in range(2):
                    act.wait_ge(m2_seg, 2 * layer + r + 1)
                    nc.scalar.activation(Mm[:, 4 * r:4 * r + 4, :], pb[:, 4:8, 0:3 * P], ACT.Exp).then_inc(m2_e, 1)
                take("xv1", layer, (vX[:, :, 512:1024], 0, 512, ACT.Copy, 1.0, None))
                turn_out(norm_no(layer, "mixed"), xT, par_("out_w", layer))
                turn_out(norm_no(layer, "xa"), xT, par_("xa_w", layer))
                for i in range(2):
                    take(f"xq{i}", layer, (qX[:, 4 * i:4 * i + 4, :].rearrange("p (b a) s -> p b (a s)", b=2), 0, 512,
                                           ACT.Copy, 256 ** -0.5, None))
                act.wait_ge(xa_max, layer + 1)
                for hd in range(4):
                    for t in range(NT):
                        i = 2 * hd + t
                        ins = nc.scalar.activation(Px[:, i, :], pb[:, 4 + hd, t * S:(t + 1) * S], ACT.Exp,
                                                   bias=nmax[:, i:i + 1], accum_out=rsum[:, i:i + 1])
                ins.then_inc(xa_p, 1)
                act.wait_ge(xa_pt, 2 * layer + 1)
                nc.scalar.activation(PTx[:, 0:2, :, :].rearrange("p h m s -> p h (m s)"), pb[:, 4:6, :],
                                     ACT.Copy).then_inc(xa_pta, 1)
                act.wait_ge(xa_o, layer + 1)
                nc.scalar.activation(xT.rearrange("p (b a) s -> p b (a s)", a=2)[:, 0:4, :], pb[:, 4:8, :],
                                     ACT.Copy).then_inc(xa_oc, 1)
                turn_out(norm_no(layer, "ffn"), xT, par_("ffn_w", layer))

                def w1_silu(j, n0):
                    act.wait_ge(w_used, n0 + 2 * j + 2)
                    b = 2 * (j % 2)
                    nc.scalar.activation(silu[:, j % 2, :, :], pb[:, b:b + 2, 0:S], ACT.Silu).then_inc(silu_ready, 1)

                if layer == 0:
                    for j in range(NF // 2):
                        w1_silu(j, chunk0(0))
                else:
                    act.wait_ge(rt_d, 1)
                    nc.scalar.activation(ge, gd, ACT.Exp).then_inc(rt_e, 1)
                    with act.Fori(0, NE // 2) as pair:
                        for e in range(2):
                            for j in range(NF // 2):
                                w1_silu(j, pair * (2 * FFN_CHUNKS) + (MOE0 + e * FFN_CHUNKS))

        @block.tensor
        def _(pe):
            ident = const("ident")
            upto, after = const("upto"), const("after")
            ones = const("ones")
            a0 = CCOL["ones"][0]
            ones_after = consts[:, a0:a0 + 2 * P]
            upto_ones = consts[:, CCOL["upto"][0]:CCOL["upto"][0] + 2 * P]
            pe.wait_ge(tables_in, 48)

            def turn(no):
                pe.wait_ge(xn_ready, no + 1)
                for b in range(4):
                    for i in range(2):
                        k = 2 * b + i
                        for t in range(NT):
                            mm = nc.tensor.transpose(pb[:, 4 + b, i * S + t * P:i * S + (t + 1) * P],
                                                     xn[:, t, k * P:(k + 1) * P], ident)
                    mm.then_inc(turned, 1)

            def columns_ready(no):
                pe.wait_ge(xT_act, no + 1)
                pe.wait_ge(xT_dve, no + 1)

            def project(name, layer, act_in):
                g = GI[name, layer]
                if g >= 2:
                    prev = groups[g - 2]
                    pe.wait_ge(lin_dve if by_dve(prev) else lin_act, evac_count(prev))
                n = chunk0(layer, name)
                b = 2 * (g % 2)
                form = PROJ[PIDX[name]][1]
                for c in range(2):
                    loaded(pe, n + c)
                    w = slot(n + c)
                    if form == "T":
                        w = w.rearrange("p (k m) -> p k m", k=KT)
                        for i in range(2):
                            for k in range(KT):
                                mm = nc.tensor.matmul(pb[:, b + c, i * S:(i + 1) * S], w[:, k, i * P:(i + 1) * P],
                                                      act_in[:, k, :], start=(k == 0), stop=(k == KT - 1))
                    else:
                        w = w.rearrange("p (k m) -> p k m", k=KT // 2)
                        for t in range(NT):
                            for kk in range(KT // 2):
                                k = c * (KT // 2) + kk
                                mm = nc.tensor.matmul(pb[:, b + t, :], act_in[:, k, t * P:(t + 1) * P], w[:, kk, :],
                                                      start=(k == 0), stop=(k == KT - 1))
                    mm.then_inc(w_used, 1)

            def ffn(n0, later_w, dve_before, banks_free):
                for j in range(NF // 2):
                    pe.wait_ge(lin_dve, dve_before + (j - 1 if j >= 2 else 0))
                    b = 2 * (j % 2)
                    for i in range(2):
                        loaded(pe, n0 + 2 * j + i, later_w)
                        w = slot(n0 + 2 * j + i).rearrange("p (k m) -> p k m", k=KT)
                        for part in range(2):
                            for k in range(KT):
                                mm = nc.tensor.matmul(pb[:, b + i, part * S:(part + 1) * S],
                                                      w[:, k, part * P:(part + 1) * P], xT[:, k, :],
                                                      start=(k == 0), stop=(k == KT - 1))
                        mm.then_inc(w_used, 1)
                for c in range(W2_CHUNKS):
                    pe.wait_ge(lin_dve, dve_before + c + 1)
                    loaded(pe, n0 + W1_CHUNKS + c, later_w)
                    w = slot(n0 + W1_CHUNKS + c).rearrange("p (k m) -> p k m", k=2)
                    if c == 0:
                        banks_free()
                    for k in range(2):
                        f = 2 * c + k
                        for t in range(NT):
                            for half in range(2):
                                mm = nc.tensor.matmul(pb[:, 4 + 2 * t + half, :], hT[:, f, t * P:(t + 1) * P],
                                                      w[:, k, half * 512:(half + 1) * 512],
                                                      start=(f == 0), stop=(f == NF - 1))
                    mm.then_inc(w_used, 1)

            turn(0)
            for layer in range(DEPTH):
                turn(norm_no(layer, "mix"))
                columns_ready(norm_no(layer, "mix"))
                for name in ("hq_hf", "gate_small", "xbc0", "xbc1", "fq_fk", "fv_hi", "z"):
                    project(name, layer, xT)
                pe.wait_ge(lin_act, evac_count(("fv_hi", layer)))
                pe.wait_ge(fa_ready, layer + 1)
                for hd in range(FOX_H):
                    r = slice(DH * (hd % 2), DH * (hd % 2) + DH)
                    q, k = fqT[r, hd // 2, :], fkT[r, hd // 2, :]
                    b = pb[:, 4 + hd, :]
                    nc.tensor.matmul(b[:, 0:P], q[:, 0:P], k[:, 0:P], start=True, stop=False)
                    nc.tensor.matmul(b[:, 0:P], AUf[:, 0, hd, :], after, start=False, stop=False)
                    nc.tensor.matmul(b[:, 0:P], ident, const("neg"), start=False, stop=True)
                    nc.tensor.matmul(b[:, P:3 * P], q[:, P:S], k, start=True, stop=False)
                    nc.tensor.matmul(b[:, P:3 * P], AUf[:, 1, hd, :], ones_after, start=False, stop=False)
                    nc.tensor.matmul(b[:, P:2 * P], ABf[:, hd, :], after, start=False, stop=False)
                    mm = nc.tensor.matmul(b[:, 2 * P:3 * P], ident, const("neg"), start=False, stop=True)
                mm.then_inc(fox_lg, 1)
                pe.wait_ge(memw_ready, layer + 1)
                project("xk0", layer, memTw)
                pe.wait_ge(fox_p, layer + 1)
                for hd in range(FOX_H):
                    for i in range(3):
                        n = 3 * hd + i
                        mm = nc.tensor.transpose(pb[:, 4 + n // 4, (n % 4) * P:(n % 4 + 1) * P],
                                                 Pf[:, hd, i * P:(i + 1) * P], ident)
                mm.then_inc(fox_pt, 1)
                pe.wait_ge(fox_ptc, layer + 1)
                for hd in range(FOX_H):
                    v = vtok[:, :, hd * DH:(hd + 1) * DH]
                    o = pb[:, 7, :].rearrange("p (t h d) -> p t h d", t=NT, h=FOX_H)
                    nc.tensor.matmul(o[:, 0, hd, :], PTf[:, hd, 0, :], v[:, 0, :], start=True, stop=True)
                    nc.tensor.matmul(o[:, 1, hd, :], PTf[:, hd, 1, :], v[:, 0, :], start=True, stop=False)
                    mm = nc.tensor.matmul(o[:, 1, hd, :], PTf[:, hd, 2, :], v[:, 1, :], start=False, stop=True)
                mm.then_inc(fox_o, 1)
                project("xk1", layer, memTw)
                pe.wait_ge(fox_ok, layer + 1)
                NL = len(LEVELS) + 2
                for lv in range(NL):
                    n = layer * NL + lv
                    pe.wait_ge(hg_qk, n + 1)
                    if n >= 2:
                        pe.wait_ge(hg_sel, n - 1)
                    Q = (hqT.rearrange("p a s -> p (a s)") if lv == 0 else Ql[:, lv % 2, :])
                    K = (hk if lv == 0 else Kl[:, lv % 2, :])
                    b = 4 + 2 * (lv % 2)
                    for hd in range(HG_H):
                        r = slice(DH * (hd % 2), DH * (hd % 2) + DH)
                        o = S * (hd // 2)
                        if lv < NL - 1:
                            for t in range(NT):
                                i = 2 * (hd // 2) + t
                                mm = nc.tensor.matmul(pb[:, b + hd % 2, i * P:(i + 1) * P],
                                                      K[r, o + t * P:o + (t + 1) * P], Q[r, o + t * P:o + (t + 1) * P],
                                                      start=True, stop=True)
                        else:
                            i = hd // 2
                            mm = nc.tensor.matmul(pb[:, b + hd % 2, i * P:(i + 1) * P], K[r, o:o + P],
                                                  Q[r, o + P:o + 2 * P], start=True, stop=True)
                    mm.then_inc(hg_s, 1)
                pe.wait_ge(hg_sel, (layer + 1) * NL)
                for hd in range(HG_H):
                    v = vtok[:, :, 256 + hd * DH:256 + (hd + 1) * DH]
                    at = 4 * (hd % 2) + 2 * (hd // 2)
                    o = pb[:, 7, :].rearrange("p (t h d) -> p t h d", t=NT, h=HG_H)
                    nc.tensor.matmul(o[:, 0, hd, :], ScT[:, at, :], v[:, 0, :], start=True, stop=True)
                    nc.tensor.matmul(o[:, 1, hd, :], ScO[:, at // 2, :], v[:, 0, :], start=True, stop=False)
                    mm = nc.tensor.matmul(o[:, 1, hd, :], ScT[:, at + 1, :], v[:, 1, :], start=False, stop=True)
                mm.then_inc(hg_o, 1)
                project("xv0", layer, memTw)
                pe.wait_ge(xcv_ready, layer + 1)
                pe.wait_ge(hg_ok, layer + 1)
                for g in range(2):
                    B, C = xcv[:, 4 + g, :], xcv[:, 6 + g, :]
                    nc.tensor.matmul(pb[:, 4 + g, 0:S], B[:, 0:P], C, start=True, stop=True)
                    nc.tensor.matmul(pb[:, 4 + g, S:S + P], B[:, P:S], C[:, P:S], start=True, stop=True)
                for t in range(NT):
                    for c in range(4):
                        mm = nc.tensor.transpose(pb[:, 6 + t, c * P:(c + 1) * P], xcv[:, c, t * P:(t + 1) * P], ident)
                mm.then_inc(m2_t, 1)
                pe.wait_ge(m2_a, layer + 1)
                pe.wait_ge(m2_cb, layer + 1)
                pe.wait_ge(m2_xs, layer + 1)
                for rnd in range(2):
                    if rnd:
                        pe.wait_ge(m2_e, 2 * layer + 1)
                    for i in range(4):
                        hd = 4 * rnd + i
                        b = pb[:, 4 + i, :]
                        nc.tensor.matmul(b[:, 0:2 * P], ALm[:, 0, hd, :], upto_ones, start=True, stop=False)
                        nc.tensor.matmul(b[:, P:2 * P], ABm[:, hd, :], upto, start=False, stop=True)
                        mm = nc.tensor.matmul(b[:, 2 * P:3 * P], ALm[:, 1, hd, :], upto, start=True, stop=True)
                    mm.then_inc(m2_seg, 1)
                project("xv1", layer, memTw)
                pe.wait_ge(m2_m, 2 * layer + 2)
                for hd in range(M2_H):
                    xh = xcd[:, :, hd * DH:(hd + 1) * DH]
                    o = slice(hd * DH, (hd + 1) * DH)
                    nc.tensor.matmul(pb[:, 4, o], Mm[:, hd, 0:P], xh[:, 0, :], start=True, stop=True)
                    nc.tensor.matmul(pb[:, 5, o], Mm[:, hd, P:2 * P], xh[:, 0, :], start=True, stop=False)
                    mm = nc.tensor.matmul(pb[:, 5, o], Mm[:, hd, 2 * P:3 * P], xh[:, 1, :], start=False, stop=True)
                mm.then_inc(m2_y, 1)
                turn(norm_no(layer, "mixed"))
                columns_ready(norm_no(layer, "mixed"))
                for name in ("out0", "out1"):
                    project(name, layer, xT)
                turn(norm_no(layer, "xa"))
                columns_ready(norm_no(layer, "xa"))
                for name in ("xq0", "xq1"):
                    project(name, layer, xT)
                pe.wait_ge(lin_act, evac_count(("xq1", layer)))
                for hd in range(4):
                    for t in range(NT):
                        for k in range(2):
                            mm = nc.tensor.matmul(pb[:, 4 + hd, t * S:(t + 1) * S],
                                                  qX[:, 2 * hd + k, t * P:(t + 1) * P], kX[:, 2 * hd + k, :],
                                                  start=(k == 0), stop=(k == 1))
                mm.then_inc(xa_lg, 1)
                pe.wait_ge(xa_pn, layer + 1)
                for hd in range(4):
                    for m in range(2):
                        for t in range(NT):
                            mm = nc.tensor.transpose(pb[:, 4 + hd, m * S + t * P:m * S + (t + 1) * P],
                                                     Px[:, 2 * hd + t, m * P:(m + 1) * P], ident)
                    if hd % 2:
                        mm.then_inc(xa_pt, 1)
                pe.wait_ge(xa_pta, layer + 1)
                pe.wait_ge(xa_ptd, layer + 1)
                for hd in range(4):
                    for k in range(2):
                        for m in range(2):
                            c = hd * 256 + k * P
                            mm = nc.tensor.matmul(pb[:, 4 + hd, k * S:(k + 1) * S], vX[:, m, c:c + P],
                                                  PTx[:, hd, m, :], start=(m == 0), stop=(m == 1))
                mm.then_inc(xa_o, 1)
                pe.wait_ge(xa_oc, layer + 1)
                for name in ("xo0", "xo1"):
                    project(name, layer, xT)
                turn(norm_no(layer, "ffn"))
                columns_ready(norm_no(layer, "ffn"))
                if layer == 0:
                    ffn(chunk0(0), 0, evac_count(("xo1", 0)), lambda: None)
                    pe.wait_ge(ffn_added, 1)
                else:
                    router = par_("router").rearrange("p (k e) -> p k e", e=NE)
                    for t in range(NT):
                        for k in range(KT):
                            mm = nc.tensor.matmul(pb[:, 4, t * NE:(t + 1) * NE], xT[:, k, t * P:(t + 1) * P],
                                                  router[:, k, :], start=(k == 0), stop=(k == KT - 1))
                    mm.then_inc(rt_lg, 1)
                    pe.wait_ge(rt_d, 1)
                    with pe.Fori(0, NE // 2) as pair:
                        for e in range(2):
                            ffn(MOE0 + e * FFN_CHUNKS, pair * (2 * FFN_CHUNKS // RING * 16), DVE0 + e * (NF // 2) + pair * NF,
                                lambda: pe.wait_ge(ffn_added, 1 + e + pair * 2))

        @block.vector
        def _(dve):
            chain = [0]
            V = nc.vector

            def link(ins):
                chain[0] += 1
                ins.then_inc(dve_c, 1)
                dve.wait_ge(dve_c, chain[0])

            norms = [0]

            def root(n):
                norms[0] += 1
                dve.wait_ge(rs_ready, norms[0])

            def rstd_of(src):
                for t in range(NT):
                    ins = V.scalar_tensor_tensor(out=sq[:, t, :], in0=src[:, t, :], scalar=1.0 / D, in1=src[:, t, :],
                                                 op0=ALU.mult, op1=ALU.mult, accum_out=ssq[:, t:t + 1])
                link(ins)
                V.tensor_scalar(ssq[:, 0:NT], ssq[:, 0:NT], EPS, None, ALU.add).then_inc(ss_ready, 1)
                root(NT)

            def normalise(src):
                rstd_of(src)
                for t in range(NT):
                    ins = V.tensor_scalar(xn[:, t, :], src[:, t, :], rstd[:, t:t + 1], None, ALU.mult)
                ins.then_inc(xn_ready, 1)

            def turn_out(no, dst, w):
                for b in (1, 3):
                    dve.wait_ge(turned, 4 * no + b + 1)
                    for i in range(2):
                        k = 2 * b + i
                        src = pb[:, 4 + b, i * S:(i + 1) * S]
                        if w is None:
                            ins = V.tensor_copy(dst[:, k, :], src)
                        else:
                            ins = V.tensor_scalar(dst[:, k, :], src, w[:, k:k + 1], None, ALU.mult)
                ins.then_inc(xT_dve, 1)

            def bc(ap, n):
                return ap.unsqueeze(2).to_broadcast([P, ap.shape[1], n])

            def add_rows(name, layer, half):
                g = GI[name, layer]
                projected(dve, name, layer)
                b = 2 * (g % 2)
                hh = h[:, :, half * 512:(half + 1) * 512]
                V.tensor_tensor(hh, hh, pb[:, b:b + 2, :], ALU.add).then_inc(lin_dve, 1)

            dve.wait_ge(inputs_in, 32)
            normalise(xn)
            turn_out(0, memT, None)
            dve.wait_ge(tables_in, 48)
            raw = par_("lb_raw")
            link(V.tensor_tensor(lb_s, raw[:, 0:2], raw[:, 2:4], ALU.max))
            for l in range(DEPTH):
                ins = V.tensor_tensor(lbe[:, 2 * l:2 * l + 2], raw[:, 2 * l:2 * l + 2], lb_s, ALU.subtract)
            ins.then_inc(lbx_ready, 1)
            dve.wait_ge(lbx_ready, 2)
            link(V.tensor_tensor(lb_s, lbe[:, 0:2], lbe[:, 2:4], ALU.add))
            link(V.reciprocal(lb_s, lb_s))
            for l in range(DEPTH):
                ins = V.tensor_tensor(lbe[:, 2 * l:2 * l + 2], lbe[:, 2 * l:2 * l + 2], lb_s, ALU.mult)
            link(ins)
            V.tensor_tensor(lb[:, 0:2], lbe[:, 0:2], lbe[:, 0:2], ALU.subtract)
            link(V.tensor_tensor(lb[:, 2:4], lbe[:, 0:2], lbe[:, 2:4], ALU.add))
            link(V.tensor_tensor(lb[:, 2:4], lb[:, 2:4], lbe[:, 0:2], ALU.subtract))
            V.tensor_scalar(lb1m, lb, -1.0, 1.0, ALU.mult, ALU.add)
            link(V.tensor_scalar(lbfl, lb, FLOOR, None, ALU.max))

            for layer in range(DEPTH):
                normalise(h)
                turn_out(norm_no(layer, "mix"), xT, par_("mix_w", layer))
                if layer:
                    projected(dve, "xv1", layer - 1)
                dve.wait_ge(xT_act, 1)
                for k in range(KT):
                    w = par_("mem_w", layer)
                    ins = V.tensor_scalar(memTw[:, k, :], memT[:, k, :], w[:, k:k + 1], None, ALU.mult)
                ins.then_inc(memw_ready, 1)
                V.memset(xraw[:, :, 0:3], 0.0)
                dve.wait_ge(lin_act, evac_count(("gate_small", layer)))
                for t in range(NT):
                    V.scalar_tensor_tensor(out=X12[:, t, 0:4], in0=raw12[:, t, 0:4], scalar=-1.0,
                                           in1=par_("fox_b", layer), op0=ALU.mult, op1=ALU.subtract)
                    ins = V.tensor_tensor(X12[:, t, 4:12], raw12[:, t, 4:12], par_("dt_b", layer), ALU.add)
                link(ins)
                V.scalar_tensor_tensor(out=AX12, in0=X12, scalar=-1.0, in1=X12, op0=ALU.mult,
                                       op1=ALU.max).then_inc(x12_ready, 1)
                cw, cb = par_("conv_w", layer), par_("conv_b", layer)
                for c in range(8):
                    if c % 4 == 0:
                        dve.wait_ge(lin_act, evac_count((f"xbc{c // 4}", layer)))
                        link(V.memset(lb_s, 0.0))
                    V.tensor_scalar(xcv[:, c, :], xraw[:, c, 3:3 + S], cw[:, 4 * c + 3:4 * c + 4], cb[:, c:c + 1],
                                    ALU.mult, ALU.add).then_inc(dve_c, 1)
                    chain[0] += 1
                for tap in range(3):
                    for c in range(8):
                        dve.wait_ge(dve_c, chain[0] - 7)
                        chain[0] += 1
                        ins = V.scalar_tensor_tensor(out=xcv[:, c, :], in0=xraw[:, c, tap:tap + S],
                                                     scalar=cw[:, 4 * c + tap:4 * c + tap + 1], in1=xcv[:, c, :],
                                                     op0=ALU.mult, op1=ALU.add)
                        ins.then_inc(dve_c, 1)
                dve.wait_ge(dve_c, chain[0])
                V.tensor_scalar(lb_s, lb_s, 0.0, None, ALU.mult).then_inc(conv_ready, 1)
                dve.wait_ge(e12_ready, layer + 1)
                link(V.tensor_scalar(Z12, EX12, 2.0, None, ALU.add))
                link(V.reciprocal(Z12, Z12))
                link(V.tensor_tensor(Z12, Z12, EX12, ALU.mult))
                link(V.tensor_tensor(ZZ12, Z12, Z12, ALU.mult))
                link(V.tensor_scalar(PO12, ZZ12, 1.0 / 15, None, ALU.mult))
                for d in (13, 11, 9, 7, 5, 3):
                    link(V.scalar_tensor_tensor(out=PO12, in0=PO12, scalar=1.0 / d, in1=ZZ12, op0=ALU.add, op1=ALU.mult))
                link(V.scalar_tensor_tensor(out=PO12, in0=PO12, scalar=1.0, in1=Z12, op0=ALU.add, op1=ALU.mult))
                link(V.tensor_scalar(X12, X12, 0.0, None, ALU.max))
                link(V.scalar_tensor_tensor(out=SP12, in0=PO12, scalar=2.0, in1=X12, op0=ALU.mult, op1=ALU.add))
                for t in range(NT):
                    V.tensor_scalar(A12[:, t, 0:4], SP12[:, t, 0:4], -1.0, None, ALU.mult)
                    ins = V.scalar_tensor_tensor(out=A12[:, t, 4:12], in0=SP12[:, t, 4:12], scalar=-1.0, in1=aexp,
                                                 op0=ALU.mult, op1=ALU.mult)
                link(ins)
                for t in range(NT):
                    V.tensor_tensor(AUf[:, t, :, :], const("upto").unsqueeze(1).to_broadcast([P, FOX_H, P]),
                                    bc(A12[:, t, 0:4], P), ALU.mult)
                V.tensor_copy(ABf, bc(A12[:, 0, 0:4], P)).then_inc(fa_ready, 1)
                dve.wait_ge(fox_lg, layer + 1)
                V.tensor_reduce(nmax[:, 0:4], pb[:, 4:8, 0:P], AX.X, ALU.max, negate=True)
                V.tensor_reduce(nmax[:, 4:8], pb[:, 4:8, P:3 * P], AX.X, ALU.max, negate=True).then_inc(fox_max, 1)
                dve.wait_ge(hg_e, layer + 1)
                link(V.tensor_scalar(he, he, 1e37, None, ALU.min))
                link(V.tensor_scalar(hr, he, 1.0, None, ALU.add))
                link(V.reciprocal(hr, hr))
                for a in range(2):
                    i = 2 * layer + a
                    c = slice(a * S, (a + 1) * S)
                    V.scalar_tensor_tensor(out=hk[:, c], in0=he[:, c], scalar=lb1m[:, i:i + 1], in1=hr[:, c],
                                           op0=ALU.mult, op1=ALU.mult)
                    ins = V.tensor_scalar(hl[:, c], hr[:, c], lb1m[:, i:i + 1], lbfl[:, i:i + 1], ALU.mult, ALU.add)
                link(ins)
                link(V.tensor_scalar(hc, hl, 2.0 ** -40, 2.0 ** 60, ALU.is_lt, ALU.mult))
                V.scalar_tensor_tensor(out=hl, in0=hc, scalar=1.0, in1=hl, op0=ALU.max,
                                       op1=ALU.mult).then_inc(hg_f, 1)
                hq = hqT.rearrange("p a s -> p (a s)")
                V.tensor_scalar(hq, hq, DH ** -0.5, None, ALU.mult)
                link(V.memset(ScT, 0.0))
                V.tensor_scalar(lb_s, lb_s, 0.0, None, ALU.mult).then_inc(hg_qk, 1)
                dve.wait_ge(fox_pt, layer + 1)
                V.tensor_copy(PTf.rearrange("p h i q -> p (h i q)"),
                              pb[:, 4:7, :].rearrange("p b q -> p (b q)")).then_inc(fox_ptc, 1)
                link(V.reciprocal(rinv, rsum))
                dve.wait_ge(fox_o, layer + 1)
                V.tensor_tensor(xn[:, :, 0:256].rearrange("p t (h d) -> p t h d", d=DH),
                                pb[:, 7, :].rearrange("p (t h d) -> p t h d", t=NT, h=FOX_H),
                                rinv.rearrange("p (t h) -> p t h", t=NT).unsqueeze(3).to_broadcast([P, NT, FOX_H, DH]),
                                ALU.mult).then_inc(fox_ok, 1)
                dve.wait_ge(hg_l, layer + 1)
                link(V.scalar_tensor_tensor(out=hl, in0=hc, scalar=-60.0 * float(np.log(2.0)) / 2.0 ** 60, in1=hl,
                                            op0=ALU.mult, op1=ALU.add))
                link(V.tensor_tensor_scan(hc, const("restart"), hl, 0.0, ALU.mult, ALU.add))
                NL = len(LEVELS) + 2

                def exponents(lv):
                    n = layer * (NL - 1) + lv - 1
                    if n >= 2:
                        dve.wait_ge(hg_x, n - 1)
                    if lv == NL - 1:
                        c = hc.rearrange("p (a t b i) -> p a t b i", a=2, t=NT, b=2)
                        d = Dl[:, (lv - 1) % 2, :].rearrange("p (a t b i) -> p a t b i", a=2, t=NT, b=2)
                        e = Dl[:, (lv - 1) % 2, :]
                        for a in range(2):
                            for b in range(2):
                                s_last = hc[:, a * S + 64 * b + 63:a * S + 64 * b + 64]
                                s_end = hc[:, a * S + 127:a * S + 128]
                                o = a * S + 64 * b
                                link(V.tensor_scalar(e[:, o:o + 64], hc[:, o:o + 64], -1.0, s_last, ALU.mult, ALU.add))
                                if b == 0:
                                    link(V.tensor_scalar(e[:, o:o + 64], e[:, o:o + 64], s_end, None, ALU.add))
                                o += P
                                t_half = hc[:, a * S + P + 63:a * S + P + 64]
                                if b == 0:
                                    link(V.tensor_copy(e[:, o:o + 64], hc[:, o:o + 64]))
                                else:
                                    link(V.tensor_scalar(e[:, o:o + 64], hc[:, o:o + 64], t_half, None, ALU.add))
                        V.tensor_scalar(lb_s, lb_s, 0.0, None, ALU.mult).then_inc(hg_d, 1)
                        return
                    half = LEVELS[lv - 1]
                    c = hc.rearrange("p (b x i) -> p b x i", x=2, i=half)
                    d = Dl[:, (lv - 1) % 2, :].rearrange("p (b x i) -> p b x i", x=2, i=half)
                    nb = 2 * S // (2 * half)
                    mid = c[:, :, 0, half - 1:half].to_broadcast([P, nb, half])
                    V.tensor_tensor(d[:, :, 0, :], mid, c[:, :, 0, :], ALU.subtract)
                    if half == 64:
                        ins = V.tensor_copy(d[:, :, 1, :], c[:, :, 1, :])
                    else:
                        ins = V.tensor_tensor(d[:, :, 1, :], c[:, :, 1, :], mid, ALU.subtract)
                    ins.then_inc(hg_d, 1)

                def operands(lv):
                    n = layer * NL + lv
                    dve.wait_ge(hg_x, layer * (NL - 1) + lv)
                    if lv >= 3:
                        dve.wait_ge(hg_s, n - 1)
                    V.tensor_tensor(Ql[:, lv % 2, :], hq, El[:, (lv - 1) % 2, :], ALU.mult)
                    V.tensor_tensor(Kl[:, lv % 2, :], hk, El[:, (lv - 1) % 2, :], ALU.mult).then_inc(hg_qk, 1)

                def select(lv):
                    n = layer * NL + lv
                    dve.wait_ge(hg_s, n + 1)
                    b = 4 + 2 * (lv % 2)
                    if lv == NL - 1:
                        V.tensor_copy(ScO.rearrange("p (b h) q -> p b (h q)", b=2),
                                      pb[:, b:b + 2, 0:2 * P]).then_inc(hg_sel, 1)
                    else:
                        if n:
                            dve.wait_ge(hg_sel, n)
                        V.copy_predicated(ScT, lmask[:, lv, :].unsqueeze(1).to_broadcast([P, 8, P]),
                                          pb[:, b:b + 2, :].rearrange("p b (i q) -> p (b i) q", q=P)
                                          ).then_inc(hg_sel, 1)

                exponents(1)
                for lv in range(1, NL):
                    if lv + 1 < NL:
                        exponents(lv + 1)
                    operands(lv)
                    select(lv - 1)
                select(NL - 1)
                dve.wait_ge(hg_o, layer + 1)
                V.tensor_copy(xn[:, :, 256:512], pb[:, 7, :].rearrange("p (t c) -> p t c", t=NT)).then_inc(hg_ok, 1)
                for t in range(NT):
                    V.tensor_tensor(ALm[:, t, :, :], const("after").unsqueeze(1).to_broadcast([P, M2_H, P]),
                                    bc(A12[:, t, 4:12], P), ALU.mult)
                V.tensor_copy(ABm, bc(A12[:, 1, 4:12], P)).then_inc(m2_a, 1)
                dve.wait_ge(m2_t, layer + 1)
                V.tensor_tensor(CBs, pb[:, 4:6, 0:3 * P], const("m2mask").unsqueeze(1).to_broadcast([P, 2, 3 * P]),
                                ALU.mult).then_inc(m2_cb, 1)
                dve.wait_ge(m2_xs, layer + 1)
                for t in range(NT):
                    heads = xs[:, t, :].rearrange("p (h d) -> p h d", d=DH)
                    V.tensor_tensor(xcd[:, t, :].rearrange("p (h d) -> p h d", d=DH), heads, bc(SP12[:, t, 4:12], DH),
                                    ALU.mult)
                    V.tensor_tensor(ytmp[:, t, :].rearrange("p (h d) -> p h d", d=DH), heads,
                                    bc(par_("m2_d", layer), DH), ALU.mult)
                dve.wait_ge(m2_cb, layer + 1)
                for rnd in range(2):
                    dve.wait_ge(m2_e, 2 * layer + rnd + 1)
                    m = Mm[:, 4 * rnd:4 * rnd + 4, :]
                    V.tensor_tensor(m, m, CBs[:, rnd, :].unsqueeze(1).to_broadcast([P, 4, 3 * P]),
                                    ALU.mult).then_inc(m2_m, 1)
                dve.wait_ge(m2_y, layer + 1)
                om = xn[:, :, 512:1024]
                link(V.tensor_tensor(om, ytmp, pb[:, 4:6, :], ALU.add))
                link(V.tensor_tensor(om, om, zs, ALU.mult))
                link(V.tensor_tensor(sq, xn, xn, ALU.mult))
                ss = ssq.rearrange("p (t c) -> p t c", c=10)
                V.tensor_reduce(ss[:, :, 0:8], sq[:, :, 0:512].rearrange("p t (h d) -> p t h d", d=DH), AX.X, ALU.add)
                link(V.tensor_reduce(ss[:, :, 8:10], sq[:, :, 512:1024].rearrange("p t (h d) -> p t h d", d=256),
                                     AX.X, ALU.add))
                V.tensor_scalar(ss[:, :, 0:8], ss[:, :, 0:8], 1.0 / DH, EPS, ALU.mult, ALU.add)
                V.tensor_scalar(ss[:, :, 8:10], ss[:, :, 8:10], 1.0 / 256, EPS, ALU.mult, ALU.add).then_inc(ss_ready, 1)
                root(20)
                rs = rstd.rearrange("p (t c) -> p t c", c=10)
                for t in range(NT):
                    a = xn[:, t, 0:512].rearrange("p (h d) -> p h d", d=DH)
                    V.tensor_tensor(a, a, bc(rs[:, t, 0:8], DH), ALU.mult)
                    a = xn[:, t, 512:1024].rearrange("p (h d) -> p h d", d=256)
                    ins = V.tensor_tensor(a, a, bc(rs[:, t, 8:10], 256), ALU.mult)
                link(ins)
                V.tensor_tensor(xn[:, :, 256:512], xn[:, :, 256:512], gate, ALU.mult).then_inc(xn_ready, 1)
                turn_out(norm_no(layer, "mixed"), xT, par_("out_w", layer))
                add_rows("out0", layer, 0)
                add_rows("out1", layer, 1)
                dve.wait_ge(lin_dve, evac_count(("out1", layer)))
                normalise(h)
                turn_out(norm_no(layer, "xa"), xT, par_("xa_w", layer))
                dve.wait_ge(xa_lg, layer + 1)
                V.tensor_reduce(nmax, pb[:, 4:8, :].rearrange("p b (t m) -> p (b t) m", t=NT), AX.X, ALU.max,
                                negate=True).then_inc(xa_max, 1)
                dve.wait_ge(xa_p, layer + 1)
                link(V.reciprocal(rinv, rsum))
                V.tensor_tensor(Px, Px, bc(rinv, S), ALU.mult).then_inc(xa_pn, 1)
                dve.wait_ge(xa_pt, 2 * layer + 2)
                V.tensor_copy(PTx[:, 2:4, :, :].rearrange("p h m s -> p h (m s)"), pb[:, 6:8, :]).then_inc(xa_ptd, 1)
                add_rows("xo0", layer, 0)
                add_rows("xo1", layer, 1)
                dve.wait_ge(lin_dve, evac_count(("xo1", layer)))
                normalise(h)
                turn_out(norm_no(layer, "ffn"), xT, par_("ffn_w", layer))

                def w1_up(j, silus):
                    dve.wait_ge(silu_ready, silus + j + 1)
                    b = 2 * (j % 2)
                    V.tensor_tensor(hT[:, 2 * j:2 * j + 2, :], silu[:, j % 2, :, :], pb[:, b:b + 2, S:2 * S],
                                    ALU.mult).then_inc(lin_dve, 1)

                if layer == 0:
                    for j in range(NF // 2):
                        w1_up(j, 0)
                    dve.wait_ge(w_used, chunk0(0) + FFN_CHUNKS)
                    hh = h.rearrange("p t (n c) -> p (t n) c", c=512)
                    V.tensor_tensor(hh, hh, pb[:, 4:8, :], ALU.add).then_inc(ffn_added, 1)
                    dve.wait_ge(ffn_added, 1)
                else:
                    dve.wait_ge(rt_lg, 1)
                    link(V.tensor_copy(lg, pb[:, 4, 0:NT * NE].rearrange("p (t e) -> p t e", e=NE)))
                    for t in range(NT):
                        link(V.max(top8[:, t, :], lg[:, t, :]))
                        link(V.max_index(idx8[:, t, :].bitcast(U32), top8[:, t, :], lg[:, t, :]))
                        V.tensor_copy(idxf[:, t, :], idx8[:, t, :].bitcast(U32))
                        V.tensor_tensor(gd[:, t:t + 1], top8[:, t, 1:2], top8[:, t, 0:1], ALU.subtract)
                    V.tensor_copy(g12[:, 0, :], top8[:, :, 0]).then_inc(rt_d, 1)
                    dve.wait_ge(rt_e, 1)
                    link(V.tensor_scalar(gs, ge, 1.0, None, ALU.add))
                    link(V.reciprocal(g12[:, 0, :], gs))
                    link(V.tensor_tensor(g12[:, 1, :], g12[:, 0, :], ge, ALU.mult))
                    for t in range(NT):
                        V.tensor_scalar(oh[:, t, :], const("iota"), idxf[:, t, 0:1], g12[:, 0, t:t + 1],
                                        ALU.is_equal, ALU.mult)
                        ins = V.tensor_scalar(gates[:, t, :], const("iota"), idxf[:, t, 1:2], g12[:, 1, t:t + 1],
                                              ALU.is_equal, ALU.mult)
                    link(ins)
                    link(V.tensor_tensor(gates, gates, oh, ALU.add))
                    with dve.Fori(0, NE // 2) as pair:
                        for e in range(2):
                            for j in range(NF // 2):
                                w1_up(j, NF // 2 + e * (NF // 2) + pair * NF)
                            dve.wait_ge(w_used, pair * (2 * FFN_CHUNKS) + (MOE0 + (e + 1) * FFN_CHUNKS))
                            for t in range(NT):
                                for half in range(2):
                                    hh = h[:, t, half * 512:(half + 1) * 512]
                                    ins = V.scalar_tensor_tensor(
                                        out=hh, in0=pb[:, 4 + 2 * t + half, :],
                                        scalar=gates[:, t, bass.ds(pair * 2 + e, 1)], in1=hh,
                                        op0=ALU.mult, op1=ALU.add)
                            ins.then_inc(ffn_added, 1)
                    dve.wait_ge(ffn_added, 1 + NE)
            rstd_of(h)
            for t in range(NT):
                ins = V.scalar_tensor_tensor(out=xn[:, t, :], in0=h[:, t, :], scalar=rstd[:, t:t + 1],
                                             in1=par_("final_w"), op0=ALU.mult, op1=ALU.mult)
            ins.then_inc(fin_ready, 1)


def kernel(**inputs):
    import concourse.bacc as bacc
    from concourse.bass_utils import run_bass_kernel_spmd

    a = {k: np.asarray(v) for k, v in inputs.items()}

    def columns(w):
        return w.reshape(-1, P).T

    def rows(v):
        return np.broadcast_to(v[None, :], (P, v.shape[0]))

    par = []
    for l in range(DEPTH):
        heads = np.concatenate([a["fox_norm_w"][l], a["hg_norm_w"][l], a["m2_norm_w"][l]])
        par += [columns(a["mix_norm_w"][l]), columns(a["xa_norm_w"][l]), columns(a["xa_mem_norm_w"][l]),
                columns(a["ffn_norm_w"][l]), columns(heads),
                a["m2_conv_w"][l].reshape(4, 8, P).transpose(2, 1, 0).reshape(P, 32), columns(a["m2_conv_b"][l]),
                rows(a["fox_f_bias"][l]), rows(a["m2_dt_bias"][l]), rows(a["m2_a_log"][l]), rows(a["m2_d"][l])]
    par += [columns(a["hg_lb_raw"].reshape(-1)),
            a["moe_router"][0].reshape(KT, P, NE).transpose(1, 0, 2).reshape(P, KT * NE), rows(a["final_norm_w"])]
    par = np.ascontiguousarray(np.concatenate(par, axis=1))

    def projection(w, form):
        w = w.reshape(KT, P, 512)
        if form == "T":
            return [w[:, :, c * 256:(c + 1) * 256].transpose(1, 0, 2).reshape(P, CW) for c in range(2)]
        return [w[c * 4:(c + 1) * 4].transpose(1, 0, 2).reshape(P, CW) for c in range(2)]

    lin = []
    for l in range(DEPTH):
        w_in = a["w_in"][l]
        cut = np.cumsum([0, 256, 256, 256, FOX_H, 256, 256, 256, 256, 512, 1024, M2_H])
        fq, fk, fv, ff, hq, hf, hi, hg, z, xbc, dt = (w_in[:, i:j] for i, j in zip(cut[:-1], cut[1:]))
        pad = np.zeros((D, 512 - 256 - FOX_H - M2_H), w_in.dtype)
        w = {"hq_hf": np.concatenate([hq, hf], 1), "gate_small": np.concatenate([hg, ff, dt, pad], 1),
             "xbc0": xbc[:, :512], "xbc1": xbc[:, 512:], "fq_fk": np.concatenate([fq, fk], 1),
             "fv_hi": np.concatenate([fv, hi], 1), "z": z}
        for i in range(2):
            s = slice(512 * i, 512 * i + 512)
            w[f"xk{i}"], w[f"xv{i}"] = a["xa_w_kv"][l][:, :D][:, s], a["xa_w_kv"][l][:, D:][:, s]
            w[f"out{i}"], w[f"xq{i}"], w[f"xo{i}"] = a["w_out"][l][:, s], a["xa_w_q"][l][:, s], a["xa_w_o"][l][:, s]
        for name, form in PROJ:
            lin += projection(w[name], form)
    lin = np.stack(lin)

    def swiglu(w1, w2):
        w1 = w1.reshape(KT, P, 2, NF, P).transpose(3, 1, 0, 2, 4).reshape(NF, P, CW)
        w2 = w2.reshape(NF // 2, 2, P, D).transpose(0, 2, 1, 3).reshape(NF // 2, P, CW)
        return np.concatenate([w1, w2])

    ffn = np.stack([swiglu(a["ffn_w1"][0], a["ffn_w2"][0])] +
                   [swiglu(a["moe_w1"][0, e], a["moe_w2"][0, e]) for e in range(NE)])
    arrays = {"x": a["x"], "mem": a["mem"], "par": par, "con": constants(), "lvl": level_masks(), "lin_w": lin,
              "ffn_w": ffn}
    nc = bacc.Bacc("TRN2", target_bir_lowering=False, num_devices=1)
    args = {}
    for name in list(arrays):
        arr = np.ascontiguousarray(arrays[name])
        arrays[f"in_{name}"] = arr
        del arrays[name]
        args[name] = nc.dram_tensor(f"in_{name}", arr.shape, mybir.dt.from_np(arr.dtype), kind="ExternalInput").ap()
    out = nc.dram_tensor("out_0", (1, S, D), F32, kind="ExternalOutput").ap()
    build(nc, out=out, **args)
    r = run_bass_kernel_spmd(nc, [arrays], core_ids=[0])
    return r.results[0]["out_0"]
```

```python
from contextlib import ExitStack

import numpy as np

import concourse.bass as bass
from concourse import mybir

ALU = mybir.AluOpType
ACT = mybir.ActivationFunctionType
F32 = mybir.dt.float32
F32R = mybir.dt.float32r
U32 = mybir.dt.uint32
AX = mybir.AxisListType

P = 128
D = 1024
S = 256
NT = S // P
KT = D // P
DEPTH = 2
DFF = 2816
NF = DFF // P
NE = 8
DH = 64
FOX_H, HG_H, M2_H = 4, 4, 8
EPS = 1e-6
FLOOR = 1e-30
NEG = -1e30
LEVELS = (1, 2, 4, 8, 16, 32, 64)

CW = 2048
RING = 3
XRING = 6
PASSES = 2
LIN = 17
LIN_CHUNKS = 2 * LIN
W1_CHUNKS = NF
W2_CHUNKS = NF // 2
FFN_CHUNKS = W1_CHUNKS + W2_CHUNKS
PROJ = (("hq_hf", "T"), ("gate_small", "R"), ("xbc0", "T"), ("xbc1", "T"), ("fq_fk", "T"), ("fv_hi", "R"),
        ("z", "R"), ("xk0", "T"), ("xk1", "T"), ("xv0", "R"), ("xv1", "R"), ("out0", "R"), ("out1", "R"),
        ("xq0", "T"), ("xq1", "T"), ("xo0", "R"), ("xo1", "R"))
PIDX = {name: i for i, (name, _) in enumerate(PROJ)}
DVE_EVAC = ("out0", "out1", "xo0", "xo1")
assert len(PROJ) == LIN

_PER_LAYER = (("mix_w", 8), ("xa_w", 8), ("mem_w", 8), ("ffn_w", 8), ("out_w", 8), ("conv_w", 32), ("conv_b", 8),
              ("fox_b", 4), ("dt_b", 8), ("a_log", 8), ("m2_d", 8))
PCOL = {}
_n = 0
for _l in range(DEPTH):
    for _name, _w in _PER_LAYER:
        PCOL[_name, _l] = (_n, _n + _w)
        _n += _w
for _name, _w in (("lb_raw", 4), ("router", KT * NE), ("final_w", D)):
    PCOL[_name] = (_n, _n + _w)
    _n += _w
NPAR = _n

CCOL = {}
_n = 0
for _name, _w in (("ident", P), ("neg", P), ("upto", P), ("ones", P), ("after", P), ("m2mask", 3 * P),
                  ("before", P), ("restart", 2 * S), ("iota", P), ("minus_half", 20)):
    CCOL[_name] = (_n, _n + _w)
    _n += _w
NCONST = _n


def constants():
    r = np.arange(P)
    upto = (r[:, None] <= r[None, :]).astype(np.float32)
    one = np.ones((P, P), np.float32)
    restart = np.broadcast_to((np.arange(2 * S) % 64 != 0).astype(np.float32), (P, 2 * S))
    parts = [np.eye(P, dtype=np.float32), (upto - np.eye(P)) * NEG, upto, one, (r[:, None] > r[None, :]) * 1.0,
             upto, one, upto, upto - np.eye(P), restart, np.broadcast_to(np.arange(P), (P, P)), np.full((P, 20), -0.5)]
    return np.concatenate([p.astype(np.float32) for p in parts], axis=1)


def level_masks():
    r = np.arange(P)
    masks = [r[:, None] == r[None, :]]
    for half in LEVELS:
        same = (r[:, None] // (2 * half)) == (r[None, :] // (2 * half))
        masks.append(same & ((r[:, None] // half) % 2 == 0) & ((r[None, :] // half) % 2 == 1))
    return np.stack(masks, axis=1).astype(np.uint32).reshape(P, -1)


def build(nc, x, mem, par, con, lvl, lin_w, ffn_w, out):
    groups = []
    for layer in range(DEPTH):
        groups += [(name, layer) for name, _ in PROJ]
        if layer == 0:
            groups += [("w1", j) for j in range(NF // 2)]
    GI = {g: i for i, g in enumerate(groups)}

    def by_dve(g):
        return g[0] in DVE_EVAC

    def evac_count(g):
        return sum(by_dve(q) == by_dve(g) for q in groups[:GI[g] + 1] if q[0] != "w1")

    def chunk0(layer, name=None):
        base = layer * (LIN_CHUNKS + FFN_CHUNKS)
        return base + (LIN_CHUNKS if name is None else 2 * PIDX[name])

    MOE0 = chunk0(1)

    with ExitStack() as ctx:
        def sb(name, shape, dt=F32):
            return ctx.enter_context(nc.sbuf_tensor(name, shape, dt))[:]

        def sem(name):
            return ctx.enter_context(nc.semaphore(name))

        ARENA = 17600
        arena_at = -(-nc.sbuf_base // 32) * 32
        arena = sb("arena", [P, ARENA])

        def over(name, at, n):
            return nc.alloc_sbuf_tensor_at(name, [P, n], F32R, offset=arena_at + 4 * at)[:]

        raw = sb("raw", [P, RING, CW])
        whi = sb("whi", [P, 2, CW], F32R)
        wlo = sb("wlo", [P, 2, CW], F32R)
        h = sb("h", [P, NT, D])
        xn = sb("xn", [P, NT, D])
        xTh, xTl = sb("xTh", [P, KT, S], F32R), sb("xTl", [P, KT, S], F32R)
        mTh, mTl = sb("mTh", [P, KT * S], F32R), sb("mTl", [P, KT * S], F32R)
        memTh, memTl = (m.rearrange("p (k s) -> p k s", k=KT) for m in (mTh, mTl))
        xgh, xgl = (m.rearrange("p (e k s) -> p e k s", e=2, k=KT) for m in (mTh, mTl))
        kvX = sb("kvX", [P, 4 * D])
        kX = kvX[:, 0:2 * D].rearrange("p (k s) -> p k s", k=KT)
        vX = kvX[:, 2 * D:4 * D].rearrange("p (t d) -> p t d", t=NT)
        params = sb("params", [P, NPAR])
        consts = sb("consts", [P, NCONST])
        lmask = sb("lmask", [P, len(LEVELS) + 1, P], U32)
        small = sb("small", [P, 600])

        top = [0]

        def small_(n):
            top[0] += n
            assert top[0] <= 600
            return small[:, top[0] - n:top[0]]

        def carve(at, *shape):
            n = int(np.prod(shape))
            assert at + n <= ARENA, at + n
            v = arena[:, at:at + n]
            if len(shape) == 1:
                return v
            names = "abcd"[:len(shape)]
            return v.rearrange(f"p ({' '.join(names)}) -> p {' '.join(names)}",
                               **{c: s for c, s in zip(names[1:], shape[1:])})

        def const(name):
            return consts[:, CCOL[name][0]:CCOL[name][1]]

        def par_(name, layer=None):
            a, b = PCOL[name if layer is None else (name, layer)]
            return params[:, a:b]

        hqT = carve(0, 2, S)
        hfT = carve(512, 2, S)
        gate = carve(1024, NT, 256)
        zs = carve(1536, NT, 512)
        fqT = carve(2560, 2, S)
        fkT = carve(3072, 2, S)
        vtok = carve(3584, NT, 512)
        xraw = carve(4608, 8, S + 3)
        xcv = carve(6688, 8, S)
        AUf = carve(8736, NT, FOX_H, P)
        ABf = carve(9760, FOX_H, P)
        Pf = carve(10272, FOX_H, 3 * P)
        PTf = carve(10272, FOX_H, 3, P)
        El = carve(8736, 2, 2 * S)
        ScO = carve(9760, HG_H, P)
        hk = carve(11808, 2 * S)
        hl = carve(12320, 2 * S)
        hc = carve(12832, 2 * S)
        he = carve(13344, 2 * S)
        hr = carve(13856, 2 * S)
        Dl = carve(13344, 2, 2 * S)
        Ql = carve(14368, 2, 2 * S)
        Kl = carve(15392, 2, 2 * S)
        ScT = carve(16416, FOX_H * NT, P)
        Mm = carve(8736, M2_H, 3 * P)
        CBs = carve(11808, 2, 3 * P)
        xs = carve(12576, NT, 512)
        xcd = carve(4608, NT, 512)
        ALm = carve(14368, NT, M2_H, P)
        ABm = carve(2560, M2_H, P)
        ytmp = carve(3584, NT, 512)
        sq = carve(4608, NT, D)
        memrows = carve(8736, NT, D)
        qX = carve(0, KT, S)
        Px = carve(2048, 4 * NT, S)
        PTx = carve(11264, 4, 2, S)
        hTh, hTl = (over(name, at, NF * S).rearrange("p (f s) -> p f s", f=NF)
                    for name, at in (("hTh", 0), ("hTl", NF * S)))
        silu = carve(11264, 2, 2, S)
        gated = carve(12288, 2, 2, S)
        xfull = carve(0, KT, S)
        xsilu = carve(11264, 2, S)
        xgated = carve(11776, 2, S)
        sel = carve(12288, 2, NT, P)
        yh, yl = over("yh", 12800, D), over("yl", 13824, D)
        selT = over("selT", 14848, S)
        xraw_slots = [kvX[:, 0:CW], kvX[:, CW:2 * CW], carve(15104, CW), raw[:, (MOE0 - 3) % RING, :],
                      raw[:, (MOE0 - 2) % RING, :], raw[:, (MOE0 - 1) % RING, :]]

        raw12 = small_(NT * 12).rearrange("p (t c) -> p t c", c=12)
        X12, AX12, EX12, Z12, ZZ12, PO12, SP12, A12 = (
            small_(NT * 12).rearrange("p (t c) -> p t c", c=12) for _ in range(8))
        aexp = small_(8)
        lbe = small_(4)
        lb_s = small_(2)
        lb = small_(4)
        lb1m = small_(4)
        lbfl = small_(4)
        nmax = small_(8)
        rsum = small_(8)
        rinv = small_(8)
        ssq = small_(20)
        rstd = small_(20)
        lg = small_(NT * NE).rearrange("p (t e) -> p t e", e=NE)
        top8 = small_(NT * 8).rearrange("p (t e) -> p t e", e=8)
        idx8 = small_(NT * 8).rearrange("p (t e) -> p t e", e=8)
        idxf = small_(NT * 8).rearrange("p (t e) -> p t e", e=8)
        gd = small_(NT)
        ge = small_(NT)
        gs = small_(NT)
        g12 = small_(2 * NT).rearrange("p (k t) -> p k t", k=2)
        oh = small_(NT * NE).rearrange("p (t e) -> p t e", e=NE)
        routed = small_(NT * NE).rearrange("p (t e) -> p t e", e=NE)
        gates = small_(NT * (NE + 1)).rearrange("p (t e) -> p t e", e=NE + 1)
        pos = small_(PASSES * NT * (NE + 1)).rearrange("p (r t e) -> p r t e", r=PASSES, t=NT)
        most = small_(1)
        over_flag = small_(1)

        pb = ctx.enter_context(nc.psum_tensor("pb", [P, 8, 512], F32))[:]

        slot_loaded = [sem(f"slot_loaded{i}") for i in range(RING)]
        hi_ready = sem("hi_ready")
        lo_ready = sem("lo_ready")
        w_used = sem("w_used")
        x_in = sem("x_in")
        mem_in = sem("mem_in")
        tables_in = sem("tables_in")
        out_sent = sem("out_sent")
        xn_ready = sem("xn_ready")
        turned = sem("turned")
        xT_hi = sem("xT_hi")
        xT_lo = sem("xT_lo")
        ss_ready = sem("ss_ready")
        rs_ready = sem("rs_ready")
        lin_act = sem("lin_act")
        lin_dve = sem("lin_dve")
        dve_c = sem("dve_c")
        act_c = sem("act_c")
        pool_c = sem("pool_c")
        conv_ready = sem("conv_ready")
        xcv_ready = sem("xcv_ready")
        x12_ready = sem("x12_ready")
        e12_ready = sem("e12_ready")
        lbx_ready = sem("lbx_ready")
        fa_ready = sem("fa_ready")
        fox_lg = sem("fox_lg")
        fox_max = sem("fox_max")
        fox_p = sem("fox_p")
        fox_pt = sem("fox_pt")
        fox_ptc = sem("fox_ptc")
        fox_o = sem("fox_o")
        fox_ok = sem("fox_ok")
        hg_e = sem("hg_e")
        hg_f = sem("hg_f")
        hg_l = sem("hg_l")
        hg_d = sem("hg_d")
        hg_x = sem("hg_x")
        hg_qk = sem("hg_qk")
        hg_s = sem("hg_s")
        hg_sel = sem("hg_sel")
        hg_o = sem("hg_o")
        hg_ok = sem("hg_ok")
        m2_t = sem("m2_t")
        m2_xs = sem("m2_xs")
        m2_cb = sem("m2_cb")
        m2_a = sem("m2_a")
        m2_seg = sem("m2_seg")
        m2_e = sem("m2_e")
        m2_m = sem("m2_m")
        m2_y = sem("m2_y")
        xa_lg = sem("xa_lg")
        xa_max = sem("xa_max")
        xa_p = sem("xa_p")
        xa_pn = sem("xa_pn")
        xa_pt = sem("xa_pt")
        xa_pta = sem("xa_pta")
        xa_ptd = sem("xa_ptd")
        xa_o = sem("xa_o")
        xa_oh = sem("xa_oh")
        xa_ol = sem("xa_ol")
        silu_ready = sem("silu_ready")
        g_ready = sem("g_ready")
        hT_hi = sem("hT_hi")
        hT_lo = sem("hT_lo")
        rt_sum = sem("rt_sum")
        rt_rank = sem("rt_rank")
        routed_ok = sem("routed_ok")
        x_loaded = [sem(f"x_loaded{i}") for i in range(XRING)]
        sel_ready = sem("sel_ready")
        gathered = sem("gathered")
        xg_hi = sem("xg_hi")
        xg_lo = sem("xg_lo")
        hid_turned = sem("hid_turned")
        y_hi = sem("y_hi")
        y_lo = sem("y_lo")
        selT_psum = sem("selT_psum")
        selT_ready = sem("selT_ready")
        spread = sem("spread")
        ffn_added = sem("ffn_added")
        rt_lg = sem("rt_lg")
        rt_d = sem("rt_d")
        rt_e = sem("rt_e")
        fin_ready = sem("fin_ready")

        def moe_chunk(p):
            return MOE0 + p * NE * FFN_CHUNKS

        def projected(eng, name, layer):
            eng.wait_ge(w_used, chunk0(layer, name) + 2)

        def norm_no(layer, what):
            return 5 * layer + ("mix", "mem", "mixed", "xa", "ffn").index(what)

        def bank(name, layer):
            return 2 * (GI[name, layer] % 2)

        block = ctx.enter_context(nc.Block())

        @block.sync
        def _(sp):
            sp.dma_start(params[:, :], par).then_inc(tables_in, 16)
            sp.dma_start(consts[:, :], con).then_inc(tables_in, 16)
            sp.dma_start(lmask[:, :, :].rearrange("p a b -> p (a b)"), lvl).then_inc(tables_in, 16)

            def load(n, src):
                if n >= RING:
                    sp.wait_ge(lo_ready, n - RING + 1)
                sp.dma_start(raw[:, n % RING, :], src).then_inc(slot_loaded[n % RING], 16)

            for layer in range(DEPTH):
                for c in range(LIN_CHUNKS):
                    load(chunk0(layer, PROJ[0][0]) + c, lin_w[layer * LIN_CHUNKS + c])
                if layer == 0:
                    for c in range(FFN_CHUNKS):
                        load(chunk0(0) + c, ffn_w[0, c])
            sp.wait_ge(w_used, chunk0(1, "xo0") + 1)

            def load_experts(p):
                with sp.Fori(0, NE // 2) as pair:
                    for e in range(2):
                        for c in range(FFN_CHUNKS):
                            m = e * FFN_CHUNKS + c
                            sp.wait_ge(lo_ready, pair * (2 * FFN_CHUNKS) + (moe_chunk(p) + m - XRING + 1))
                            sp.dma_start(xraw_slots[m % XRING], ffn_w[1 + pair * 2 + e, c]
                                         ).then_inc(x_loaded[m % XRING], 16)

            load_experts(0)
            sp.wait_ge(routed_ok, 1)
            more = sp.value_load(over_flag[0:1, :].bitcast(U32), min_val=0, max_val=1)
            with sp.If(more):
                load_experts(1)
            sp.wait_ge(fin_ready, 1)
            sp.dma_start(out.rearrange("b (t p) d -> p (b t) d", p=P), xn[:, :, :]).then_inc(out_sent, 16)
            sp.wait_ge(out_sent, 16)

        @block.gpsimd
        def _(pool):
            order = []
            for layer in range(DEPTH):
                order += [NT, NT, 20, NT, NT]
            order.append(NT)
            for i, n in enumerate(order):
                pool.wait_ge(ss_ready, i + 1)
                if i == 0:
                    pool.wait_ge(tables_in, 48)
                nc.gpsimd.tensor_tensor(rstd[:, 0:n], ssq[:, 0:n], const("minus_half")[:, 0:n],
                                        ALU.pow).then_inc(rs_ready, 1)

        @block.scalar
        def _(act):
            chain, split = [0], [0]

            def link(ins):
                chain[0] += 1
                ins.then_inc(act_c, 1)
                act.wait_ge(act_c, chain[0])

            def split_to(n):
                while split[0] <= min(n, MOE0 - 1):
                    m = split[0]
                    act.wait_ge(slot_loaded[m % RING], 16 * (m // RING + 1))
                    if m >= 2:
                        act.wait_ge(w_used, m - 1)
                    nc.scalar.activation(whi[:, m % 2, :], raw[:, m % RING, :], ACT.Copy).then_inc(hi_ready, 1)
                    split[0] += 1

            def after(name, layer):
                split_to(chunk0(layer, name) + 3)

            split_to(1)
            act.dma_start(h[:, :, :], x.rearrange("b (t p) d -> p (b t) d", p=P)).then_inc(x_in, 16)
            act.wait_ge(tables_in, 48)

            def turn_out(no, dst, w):
                for b in range(4):
                    act.wait_ge(turned, 4 * no + b + 1)
                    for i in range(2):
                        k = 2 * b + i
                        ins = nc.scalar.activation(dst[:, k, :], pb[:, 4 + b, i * S:(i + 1) * S], ACT.Copy,
                                                   scale=w[:, k:k + 1])
                    ins.then_inc(xT_hi, 1)

            def take(name, layer, *ops):
                after(name, layer)
                projected(act, name, layer)
                b = bank(name, layer)
                for dst, a, z, func, scale, one in ops:
                    src = pb[:, b:b + 2, a:z] if one is None else pb[:, b + one, a:z]
                    ins = nc.scalar.activation(dst, src, func, scale=scale)
                ins.then_inc(lin_act, 1)

            def cols(ap):
                return ap.rearrange("p a s -> p (a s)")

            def tiles(ap):
                return ap.rearrange("p (b a) s -> p b (a s)", b=2)

            act.wait_ge(lbx_ready, 1)
            nc.scalar.activation(lbe, lbe, ACT.Exp).then_inc(lbx_ready, 1)

            for layer in range(DEPTH):
                if layer:
                    act.wait_ge(ffn_added, 1)
                act.dma_start(memrows, mem.rearrange("b (t p) d -> p (b t) d", p=P)).then_inc(mem_in, 16)
                turn_out(norm_no(layer, "mix"), xTh, par_("mix_w", layer))
                take("hq_hf", layer, (cols(hqT), 0, 512, ACT.Silu, 1.0, 0), (cols(hfT), 0, 512, ACT.Copy, 1.0, 1))
                take("gate_small", layer, (gate, 0, 256, ACT.Silu, 1.0, None),
                     (raw12, 256, 268, ACT.Copy, 1.0, None))
                turn_out(norm_no(layer, "mem"), memTh, par_("mem_w", layer))
                for i in range(2):
                    after(f"xbc{i}", layer)
                    projected(act, f"xbc{i}", layer)
                    for b in range(2):
                        ins = nc.scalar.activation(
                            xraw[:, 4 * i + 2 * b:4 * i + 2 * b + 2, 3:],
                            pb[:, bank(f"xbc{i}", layer) + b, :].rearrange("p (a s) -> p a s", a=2), ACT.Copy)
                    ins.then_inc(lin_act, 1)
                take("fq_fk", layer, (cols(fqT), 0, 512, ACT.Copy, DH ** -0.5, 0),
                     (cols(fkT), 0, 512, ACT.Copy, 1.0, 1))
                take("fv_hi", layer, (vtok, 0, 512, ACT.Copy, 1.0, None))
                take("z", layer, (zs, 0, 512, ACT.Silu, 1.0, None))
                act.wait_ge(conv_ready, layer + 1)
                nc.scalar.activation(xcv, xcv, ACT.Silu).then_inc(xcv_ready, 1)
                nc.scalar.preload_act_table_set("natural_log_exp_and_others")
                act.wait_ge(x12_ready, layer + 1)
                nc.scalar.activation(aexp, par_("a_log", layer), ACT.Exp)
                nc.scalar.activation(EX12, AX12, ACT.Exp, scale=-1.0).then_inc(e12_ready, 1)
                nc.scalar.activation(hr, cols(hfT), ACT.Exp, scale=-1.0).then_inc(hg_e, 1)
                act.wait_ge(fox_max, layer + 1)
                for hd in range(FOX_H):
                    for t in range(NT):
                        a, z = (0, P) if t == 0 else (P, 3 * P)
                        i = t * FOX_H + hd
                        ins = nc.scalar.activation(Pf[:, hd, a:z], pb[:, 4 + hd, a:z], ACT.Exp,
                                                   bias=nmax[:, i:i + 1], accum_out=rsum[:, i:i + 1])
                ins.then_inc(fox_p, 1)
                take("xk0", layer, (tiles(kX[:, 0:4, :]), 0, 512, ACT.Copy, 1.0, None))
                act.wait_ge(hg_f, layer + 1)
                nc.scalar.activation(hl, hl, ACT.Ln).then_inc(hg_l, 1)
                take("xk1", layer, (tiles(kX[:, 4:8, :]), 0, 512, ACT.Copy, 1.0, None))
                NL = len(LEVELS) + 2
                for lv in range(1, NL):
                    act.wait_ge(hg_d, layer * (NL - 1) + lv)
                    act.wait_ge(hg_qk, layer * NL + max(1, lv - 1))
                    nc.scalar.activation(El[:, (lv - 1) % 2, :], Dl[:, (lv - 1) % 2, :], ACT.Exp).then_inc(hg_x, 1)
                take("xv0", layer, (vX[:, :, 0:512], 0, 512, ACT.Copy, 1.0, None))
                act.wait_ge(m2_t, layer + 1)
                nc.scalar.activation(xs, pb[:, 6:8, :], ACT.Copy).then_inc(m2_xs, 1)
                for r in range(2):
                    act.wait_ge(m2_seg, 2 * layer + r + 1)
                    nc.scalar.activation(Mm[:, 4 * r:4 * r + 4, :], pb[:, 4:8, 0:3 * P], ACT.Exp).then_inc(m2_e, 1)
                take("xv1", layer, (vX[:, :, 512:1024], 0, 512, ACT.Copy, 1.0, None))
                turn_out(norm_no(layer, "mixed"), xTh, par_("out_w", layer))
                after("out1", layer)
                turn_out(norm_no(layer, "xa"), xTh, par_("xa_w", layer))
                for i in range(2):
                    take(f"xq{i}", layer, (tiles(qX[:, 4 * i:4 * i + 4, :]), 0, 512, ACT.Copy, 256 ** -0.5, None))
                act.wait_ge(xa_max, layer + 1)
                for hd in range(4):
                    for t in range(NT):
                        i = 2 * hd + t
                        ins = nc.scalar.activation(Px[:, i, :], pb[:, 4 + hd, t * S:(t + 1) * S], ACT.Exp,
                                                   bias=nmax[:, i:i + 1], accum_out=rsum[:, i:i + 1])
                ins.then_inc(xa_p, 1)
                act.wait_ge(xa_pt, 2 * layer + 1)
                nc.scalar.activation(PTx[:, 0:2, :, :].rearrange("p h m s -> p h (m s)"), pb[:, 4:6, :],
                                     ACT.Copy).then_inc(xa_pta, 1)
                act.wait_ge(xa_o, layer + 1)
                nc.scalar.activation(xTh.rearrange("p (b a) s -> p b (a s)", a=2), pb[:, 4:8, :],
                                     ACT.Copy).then_inc(xa_oh, 1)
                after("xo1", layer)
                turn_out(norm_no(layer, "ffn"), xTh, par_("ffn_w", layer))
                if layer == 0:
                    for j in range(NF // 2):
                        split_to(chunk0(0) + 2 * j + 3)
                        act.wait_ge(w_used, chunk0(0) + 2 * j + 2)
                        b = 2 * (j % 2)
                        nc.scalar.activation(silu[:, j % 2, :, :], pb[:, b:b + 2, 0:S], ACT.Silu).then_inc(silu_ready, 1)
                        act.wait_ge(g_ready, j + 1)
                        nc.scalar.activation(hTh[:, 2 * j:2 * j + 2, :], gated[:, j % 2, :, :],
                                             ACT.Copy).then_inc(hT_hi, 1)
                    split_to(chunk0(0) + FFN_CHUNKS + 1)

            act.wait_ge(rt_d, 1)
            nc.scalar.activation(ge, gd, ACT.Exp).then_inc(rt_e, 1)

            def experts(p):
                def gathered_hi(expert, e):
                    act.wait_ge(gathered, expert + 1)
                    for k in range(KT):
                        w = par_("ffn_w", 1)
                        ins = nc.scalar.activation(xgh[:, e, k, :], pb[:, 6 + k // 4, (k % 4) * P:(k % 4 + 1) * P],
                                                   ACT.Copy, scale=w[:, k:k + 1])
                    ins.then_inc(xg_hi, 1)

                def outputs_hi(expert):
                    act.wait_ge(w_used, expert * FFN_CHUNKS + MOE0)
                    nc.scalar.activation(yh.rearrange("p (a c) -> p a c", a=2), pb[:, 2:4, :],
                                         ACT.Copy).then_inc(y_hi, 1)

                def selection_turned(expert):
                    act.wait_ge(selT_psum, expert + 1)
                    nc.scalar.activation(selT, pb[:, 6, 0:S], ACT.Copy).then_inc(selT_ready, 1)

                gathered_hi(p * (NE + 1), 0)
                with act.Fori(0, NE // 2) as pair:
                    for e in range(2):
                        expert = pair * 2 + (e + p * NE)
                        lag = pair * 2 + (e + p * (NE + 1))
                        done = [0]

                        def split_experts(m):
                            while done[0] <= m:
                                c = e * FFN_CHUNKS + done[0]
                                at = pair * (2 * FFN_CHUNKS) + (moe_chunk(p) + c)
                                act.wait_ge(x_loaded[c % XRING], pair * (2 * FFN_CHUNKS // XRING * 16) + 16 * (
                                    c // XRING + 1 + p * NE * FFN_CHUNKS // XRING))
                                act.wait_ge(w_used, at - 1)
                                nc.scalar.activation(whi[:, (MOE0 + c) % 2, :], xraw_slots[c % XRING],
                                                     ACT.Copy).then_inc(hi_ready, 1)
                                done[0] += 1

                        split_experts(1)
                        outputs_hi(expert)
                        for j in range(NF // 2):
                            split_experts(2 * j + 3)
                            act.wait_ge(w_used, expert * FFN_CHUNKS + (MOE0 + 2 * j + 2))
                            nc.scalar.activation(xsilu[:, j % 2, :], pb[:, j % 2, 0:S], ACT.Silu).then_inc(silu_ready, 1)
                            if j >= 1:
                                hidden_hi(act, j - 1, expert)
                            if j == 1:
                                selection_turned(lag)
                            if j == 8:
                                gathered_hi(lag + 1, 1 - e)
                        split_experts(2 * (NF // 2) + 2)
                        hidden_hi(act, NF // 2 - 1, expert)
                        split_experts(FFN_CHUNKS - 1)
                outputs_hi((p + 1) * NE)
                selection_turned(p * (NE + 1) + NE)

            def hidden_hi(eng, j, expert):
                eng.wait_ge(hid_turned, expert * (NF // 2) + (j + 1))
                nc.scalar.activation(hTh[:, 2 * j:2 * j + 2, 0:P],
                                     pb[:, 4 + j % 2, 0:2 * P].rearrange("p (f s) -> p f s", f=2),
                                     ACT.Copy).then_inc(hT_hi, 1)

            experts(0)
            act.wait_ge(routed_ok, 1)
            more = act.value_load(over_flag[0:1, :].bitcast(U32), min_val=0, max_val=1)
            with act.If(more):
                experts(1)

        @block.tensor
        def _(pe):
            ident = const("ident")
            upto, after, before, ones = const("upto"), const("after"), const("before"), const("ones")
            ones_after = consts[:, CCOL["ones"][0]:CCOL["ones"][0] + 2 * P]
            upto_ones = consts[:, CCOL["upto"][0]:CCOL["upto"][0] + 2 * P]
            pe.wait_ge(tables_in, 48)

            def turn(no):
                pe.wait_ge(xn_ready, no + 1)
                for b in range(4):
                    for i in range(2):
                        k = 2 * b + i
                        for t in range(NT):
                            mm = nc.tensor.transpose(pb[:, 4 + b, i * S + t * P:i * S + (t + 1) * P],
                                                     xn[:, t, k * P:(k + 1) * P], ident)
                    mm.then_inc(turned, 1)

            def split_product(o, lhs, rhs, first, last):
                (lh, ll), (rh, rl) = lhs, rhs
                nc.tensor.matmul(o, lh, rh, start=first, stop=False)
                nc.tensor.matmul(o, lh, rl, start=False, stop=False)
                return nc.tensor.matmul(o, ll, rh, start=False, stop=last)

            def project(name, layer, act_in):
                g = GI[name, layer]
                prev = groups[g - 2]
                if g >= 2 and prev[0] != "w1":
                    pe.wait_ge(lin_dve if by_dve(prev) else lin_act, evac_count(prev))
                b = bank(name, layer)
                for c in range(2):
                    n = chunk0(layer, name) + c
                    pe.wait_ge(lo_ready, n + 1)
                    if PROJ[PIDX[name]][1] == "T":
                        w = [part[:, n % 2, :].rearrange("p (k m) -> p k m", k=KT) for part in (whi, wlo)]
                        for i in range(2):
                            for k in range(KT):
                                mm = split_product(pb[:, b + c, i * S:(i + 1) * S],
                                                   [part[:, k, i * P:(i + 1) * P] for part in w],
                                                   [part[:, k, :] for part in act_in], k == 0, k == KT - 1)
                    else:
                        w = [part[:, n % 2, :].rearrange("p (k m) -> p k m", k=KT // 2) for part in (whi, wlo)]
                        for t in range(NT):
                            for kk in range(KT // 2):
                                k = c * (KT // 2) + kk
                                mm = split_product(pb[:, b + t, :], [part[:, k, t * P:(t + 1) * P] for part in act_in],
                                                   [part[:, kk, :] for part in w], k == 0, k == KT - 1)
                    mm.then_inc(w_used, 1)

            X, M = (xTh, xTl), (memTh, memTl)
            for layer in range(DEPTH):
                turn(norm_no(layer, "mix"))
                pe.wait_ge(xT_lo, norm_no(layer, "mix") + 1)
                project("hq_hf", layer, X)
                project("gate_small", layer, X)
                turn(norm_no(layer, "mem"))
                for name in ("xbc0", "xbc1", "fq_fk", "fv_hi", "z"):
                    project(name, layer, X)
                pe.wait_ge(lin_act, evac_count(("fv_hi", layer)))
                pe.wait_ge(fa_ready, layer + 1)
                for hd in range(FOX_H):
                    r = slice(DH * (hd % 2), DH * (hd % 2) + DH)
                    q, k = fqT[r, hd // 2, :], fkT[r, hd // 2, :]
                    b = pb[:, 4 + hd, :]
                    nc.tensor.matmul(b[:, 0:P], q[:, 0:P], k[:, 0:P], start=True, stop=False)
                    nc.tensor.matmul(b[:, 0:P], AUf[:, 0, hd, :], after, start=False, stop=False)
                    nc.tensor.matmul(b[:, 0:P], ident, const("neg"), start=False, stop=True)
                    nc.tensor.matmul(b[:, P:3 * P], q[:, P:S], k, start=True, stop=False)
                    nc.tensor.matmul(b[:, P:3 * P], AUf[:, 1, hd, :], ones_after, start=False, stop=False)
                    nc.tensor.matmul(b[:, P:2 * P], ABf[:, hd, :], after, start=False, stop=False)
                    mm = nc.tensor.matmul(b[:, 2 * P:3 * P], ident, const("neg"), start=False, stop=True)
                mm.then_inc(fox_lg, 1)
                pe.wait_ge(xT_lo, norm_no(layer, "mem") + 1)
                project("xk0", layer, M)
                pe.wait_ge(fox_p, layer + 1)
                for hd in range(FOX_H):
                    for i in range(3):
                        n = 3 * hd + i
                        mm = nc.tensor.transpose(pb[:, 4 + n // 4, (n % 4) * P:(n % 4 + 1) * P],
                                                 Pf[:, hd, i * P:(i + 1) * P], ident)
                mm.then_inc(fox_pt, 1)
                pe.wait_ge(fox_ptc, layer + 1)
                for hd in range(FOX_H):
                    v = vtok[:, :, hd * DH:(hd + 1) * DH]
                    o = pb[:, 7, :].rearrange("p (t h d) -> p t h d", t=NT, h=FOX_H)
                    nc.tensor.matmul(o[:, 0, hd, :], PTf[:, hd, 0, :], v[:, 0, :], start=True, stop=True)
                    nc.tensor.matmul(o[:, 1, hd, :], PTf[:, hd, 1, :], v[:, 0, :], start=True, stop=False)
                    mm = nc.tensor.matmul(o[:, 1, hd, :], PTf[:, hd, 2, :], v[:, 1, :], start=False, stop=True)
                mm.then_inc(fox_o, 1)
                project("xk1", layer, M)
                pe.wait_ge(fox_ok, layer + 1)
                NL = len(LEVELS) + 2
                for lv in range(NL):
                    n = layer * NL + lv
                    pe.wait_ge(hg_qk, n + 1)
                    if n >= 2:
                        pe.wait_ge(hg_sel, n - 1)
                    Q = (hqT.rearrange("p a s -> p (a s)") if lv == 0 else Ql[:, lv % 2, :])
                    K = (hk if lv == 0 else Kl[:, lv % 2, :])
                    b = 4 + 2 * (lv % 2)
                    for hd in range(HG_H):
                        r = slice(DH * (hd % 2), DH * (hd % 2) + DH)
                        o = S * (hd // 2)
                        if lv < NL - 1:
                            for t in range(NT):
                                i = 2 * (hd // 2) + t
                                mm = nc.tensor.matmul(pb[:, b + hd % 2, i * P:(i + 1) * P],
                                                      K[r, o + t * P:o + (t + 1) * P], Q[r, o + t * P:o + (t + 1) * P],
                                                      start=True, stop=True)
                        else:
                            i = hd // 2
                            mm = nc.tensor.matmul(pb[:, b + hd % 2, i * P:(i + 1) * P], K[r, o:o + P],
                                                  Q[r, o + P:o + 2 * P], start=True, stop=True)
                    mm.then_inc(hg_s, 1)
                project("xv0", layer, M)
                pe.wait_ge(hg_sel, (layer + 1) * NL)
                for hd in range(HG_H):
                    v = vtok[:, :, 256 + hd * DH:256 + (hd + 1) * DH]
                    at = 4 * (hd % 2) + 2 * (hd // 2)
                    o = pb[:, 7, :].rearrange("p (t h d) -> p t h d", t=NT, h=HG_H)
                    nc.tensor.matmul(o[:, 0, hd, :], ScT[:, at, :], v[:, 0, :], start=True, stop=True)
                    nc.tensor.matmul(o[:, 1, hd, :], ScO[:, at // 2, :], v[:, 0, :], start=True, stop=False)
                    mm = nc.tensor.matmul(o[:, 1, hd, :], ScT[:, at + 1, :], v[:, 1, :], start=False, stop=True)
                mm.then_inc(hg_o, 1)
                pe.wait_ge(xcv_ready, layer + 1)
                pe.wait_ge(hg_ok, layer + 1)
                for g in range(2):
                    B, C = xcv[:, 4 + g, :], xcv[:, 6 + g, :]
                    nc.tensor.matmul(pb[:, 4 + g, 0:S], B[:, 0:P], C, start=True, stop=True)
                    nc.tensor.matmul(pb[:, 4 + g, S:S + P], B[:, P:S], C[:, P:S], start=True, stop=True)
                for t in range(NT):
                    for c in range(4):
                        mm = nc.tensor.transpose(pb[:, 6 + t, c * P:(c + 1) * P], xcv[:, c, t * P:(t + 1) * P], ident)
                mm.then_inc(m2_t, 1)
                pe.wait_ge(m2_a, layer + 1)
                pe.wait_ge(m2_cb, layer + 1)
                pe.wait_ge(m2_xs, layer + 1)
                for rnd in range(2):
                    if rnd:
                        pe.wait_ge(m2_e, 2 * layer + 1)
                    for i in range(4):
                        hd = 4 * rnd + i
                        b = pb[:, 4 + i, :]
                        nc.tensor.matmul(b[:, 0:2 * P], ALm[:, 0, hd, :], upto_ones, start=True, stop=False)
                        nc.tensor.matmul(b[:, P:2 * P], ABm[:, hd, :], upto, start=False, stop=True)
                        mm = nc.tensor.matmul(b[:, 2 * P:3 * P], ALm[:, 1, hd, :], upto, start=True, stop=True)
                    mm.then_inc(m2_seg, 1)
                project("xv1", layer, M)
                pe.wait_ge(m2_m, 2 * layer + 2)
                for hd in range(M2_H):
                    xh = xcd[:, :, hd * DH:(hd + 1) * DH]
                    o = slice(hd * DH, (hd + 1) * DH)
                    nc.tensor.matmul(pb[:, 4, o], Mm[:, hd, 0:P], xh[:, 0, :], start=True, stop=True)
                    nc.tensor.matmul(pb[:, 5, o], Mm[:, hd, P:2 * P], xh[:, 0, :], start=True, stop=False)
                    mm = nc.tensor.matmul(pb[:, 5, o], Mm[:, hd, 2 * P:3 * P], xh[:, 1, :], start=False, stop=True)
                mm.then_inc(m2_y, 1)
                turn(norm_no(layer, "mixed"))
                pe.wait_ge(xT_lo, norm_no(layer, "mixed") + 1)
                project("out0", layer, X)
                project("out1", layer, X)
                turn(norm_no(layer, "xa"))
                pe.wait_ge(xT_lo, norm_no(layer, "xa") + 1)
                project("xq0", layer, X)
                project("xq1", layer, X)
                pe.wait_ge(lin_act, evac_count(("xq1", layer)))
                for hd in range(4):
                    for t in range(NT):
                        for k in range(2):
                            mm = nc.tensor.matmul(pb[:, 4 + hd, t * S:(t + 1) * S],
                                                  qX[:, 2 * hd + k, t * P:(t + 1) * P], kX[:, 2 * hd + k, :],
                                                  start=(k == 0), stop=(k == 1))
                mm.then_inc(xa_lg, 1)
                pe.wait_ge(xa_pn, layer + 1)
                for hd in range(4):
                    for m in range(2):
                        for t in range(NT):
                            mm = nc.tensor.transpose(pb[:, 4 + hd, m * S + t * P:m * S + (t + 1) * P],
                                                     Px[:, 2 * hd + t, m * P:(m + 1) * P], ident)
                    if hd % 2:
                        mm.then_inc(xa_pt, 1)
                pe.wait_ge(xa_pta, layer + 1)
                pe.wait_ge(xa_ptd, layer + 1)
                for hd in range(4):
                    for k in range(2):
                        for m in range(2):
                            c = hd * 256 + k * P
                            mm = nc.tensor.matmul(pb[:, 4 + hd, k * S:(k + 1) * S], vX[:, m, c:c + P],
                                                  PTx[:, hd, m, :], start=(m == 0), stop=(m == 1))
                mm.then_inc(xa_o, 1)
                pe.wait_ge(xa_ol, layer + 1)
                project("xo0", layer, X)
                project("xo1", layer, X)
                turn(norm_no(layer, "ffn"))
                pe.wait_ge(xT_lo, norm_no(layer, "ffn") + 1)
                if layer == 0:
                    pe.wait_ge(lin_dve, evac_count(("xo1", 0)))
                    for j in range(NF // 2):
                        if j >= 2:
                            pe.wait_ge(g_ready, j - 1)
                        b = 2 * (j % 2)
                        for i in range(2):
                            n = chunk0(0) + 2 * j + i
                            pe.wait_ge(lo_ready, n + 1)
                            w = [part[:, n % 2, :].rearrange("p (k m) -> p k m", k=KT) for part in (whi, wlo)]
                            for half in range(2):
                                for k in range(KT):
                                    mm = split_product(pb[:, b + i, half * S:(half + 1) * S],
                                                       [part[:, k, half * P:(half + 1) * P] for part in w],
                                                       [part[:, k, :] for part in X], k == 0, k == KT - 1)
                            mm.then_inc(w_used, 1)
                    for c in range(W2_CHUNKS):
                        n = chunk0(0) + W1_CHUNKS + c
                        pe.wait_ge(hT_lo, c + 1)
                        pe.wait_ge(lo_ready, n + 1)
                        w = [part[:, n % 2, :].rearrange("p (k m) -> p k m", k=2) for part in (whi, wlo)]
                        for k in range(2):
                            f = 2 * c + k
                            for t in range(NT):
                                for half in range(2):
                                    mm = split_product(pb[:, 4 + 2 * t + half, :],
                                                       [part[:, f, t * P:(t + 1) * P] for part in (hTh, hTl)],
                                                       [part[:, k, half * 512:(half + 1) * 512] for part in w],
                                                       f == 0, f == NF - 1)
                        mm.then_inc(w_used, 1)
                    pe.wait_ge(ffn_added, 1)

            router = par_("router").rearrange("p (k e) -> p k e", e=NE)
            pe.wait_ge(rt_sum, 1)
            for t in range(NT):
                for k in range(KT):
                    mm = nc.tensor.matmul(pb[:, 4, t * NE:(t + 1) * NE], xfull[:, k, t * P:(t + 1) * P],
                                          router[:, k, :], start=(k == 0), stop=(k == KT - 1))
            mm.then_inc(rt_lg, 1)
            pe.wait_ge(rt_sum, 2)
            rank = pb[:, 5, :]
            nc.tensor.matmul(rank[:, 0:NE], before, routed[:, 0, :], start=True, stop=True)
            nc.tensor.matmul(rank[:, NE:2 * NE], ones, routed[:, 0, :], start=True, stop=False)
            nc.tensor.matmul(rank[:, NE:2 * NE], before, routed[:, 1, :], start=False, stop=True)
            nc.tensor.matmul(rank[:, 2 * NE:3 * NE], ones, routed[:, 0, :], start=True, stop=False)
            nc.tensor.matmul(rank[:, 2 * NE:3 * NE], ones, routed[:, 1, :], start=False,
                             stop=True).then_inc(rt_rank, 1)

            def experts(p):
                def gather(count, e):
                    pe.wait_ge(sel_ready, count + 1)
                    for k in range(KT):
                        for t in range(NT):
                            mm = nc.tensor.matmul(pb[:, 6 + k // 4, (k % 4) * P:(k % 4 + 1) * P],
                                                  xn[:, t, k * P:(k + 1) * P], sel[:, e, t, :],
                                                  start=(t == 0), stop=(t == NT - 1))
                    mm.then_inc(gathered, 1)

                def turn_selection(count, e):
                    for t in range(NT):
                        mm = nc.tensor.transpose(pb[:, 6, t * P:(t + 1) * P], sel[:, e, t, :], ident)
                    mm.then_inc(selT_psum, 1)

                def spread_outputs(count, t):
                    if t == 0:
                        pe.wait_ge(selT_ready, count + 1)
                        pe.wait_ge(y_lo, count + 1)
                    else:
                        pe.wait_ge(ffn_added, count * 2 + 2)
                    for half in range(2):
                        c = slice(half * 512, (half + 1) * 512)
                        nc.tensor.matmul(pb[:, 6 + half, :], selT[:, t * P:(t + 1) * P], yh[:, c], start=True, stop=False)
                        mm = nc.tensor.matmul(pb[:, 6 + half, :], selT[:, t * P:(t + 1) * P], yl[:, c],
                                              start=False, stop=True)
                    mm.then_inc(spread, 1)

                gather(p * (NE + 1), 0)
                with pe.Fori(0, NE // 2) as pair:
                    for e in range(2):
                        expert = pair * 2 + (e + p * NE)
                        lag = pair * 2 + (e + p * (NE + 1))

                        def turn_hidden(j):
                            pe.wait_ge(g_ready, expert * (NF // 2) + (NF // 2 + j + 1))
                            for i in range(2):
                                mm = nc.tensor.transpose(pb[:, 4 + j % 2, i * P:(i + 1) * P],
                                                         xgated[:, j % 2, i * P:(i + 1) * P], ident)
                            mm.then_inc(hid_turned, 1)

                        def ready(c):
                            pe.wait_ge(lo_ready, expert * FFN_CHUNKS + (MOE0 + c + 1))
                            n = MOE0 + e * FFN_CHUNKS + c
                            return [part[:, n % 2, :] for part in (whi, wlo)]

                        pe.wait_ge(xg_lo, lag + 1)
                        for j in range(NF // 2):
                            pe.wait_ge(g_ready, expert * (NF // 2) + (NF // 2 + max(0, j - 1)))
                            for c in range(2):
                                w = [part.rearrange("p (k m) -> p k m", k=KT // 2) for part in ready(2 * j + c)]
                                for kk in range(KT // 2):
                                    k = c * (KT // 2) + kk
                                    mm = split_product(pb[:, j % 2, :], [part[:, e, k, :] for part in (xgh, xgl)],
                                                       [part[:, kk, :] for part in w], k == 0, k == KT - 1)
                                mm.then_inc(w_used, 1)
                            if j >= 1:
                                if j >= 3:
                                    pe.wait_ge(hT_lo, expert * (NF // 2) + (NF // 2 + j - 2))
                                turn_hidden(j - 1)
                            if j == 1:
                                turn_selection(lag, 1 - e)
                            if j == 3:
                                spread_outputs(lag, 0)
                            if j == 6:
                                spread_outputs(lag, 1)
                            if j == 8:
                                pe.wait_ge(ffn_added, lag * 2 + 3)
                                gather(lag + 1, 1 - e)
                        for c in range(W2_CHUNKS):
                            w = [part.rearrange("p (k m) -> p k m", k=2) for part in ready(W1_CHUNKS + c)]
                            if c == 0:
                                pe.wait_ge(y_lo, lag + 1)
                            pe.wait_ge(hT_lo, expert * (NF // 2) + (NF // 2 + c + 1))
                            for k in range(2):
                                f = 2 * c + k
                                for half in range(2):
                                    mm = split_product(pb[:, 2 + half, :], [part[:, f, 0:P] for part in (hTh, hTl)],
                                                       [part[:, k, half * 512:(half + 1) * 512] for part in w],
                                                       f == 0, f == NF - 1)
                            mm.then_inc(w_used, 1)
                            if c == 0:
                                pe.wait_ge(hT_lo, expert * (NF // 2) + (2 * (NF // 2) - 2))
                                turn_hidden(NF // 2 - 1)
                count = p * (NE + 1) + NE
                pe.wait_ge(xg_lo, count + 1)
                turn_selection(count, 1)
                spread_outputs(count, 0)
                spread_outputs(count, 1)

            experts(0)
            pe.wait_ge(routed_ok, 1)
            more = pe.value_load(over_flag[0:1, :].bitcast(U32), min_val=0, max_val=1)
            with pe.If(more):
                pe.wait_ge(ffn_added, 1 + 2 * (NE + 1))
                experts(1)

        @block.vector
        def _(dve):
            chain, split = [0], [0]
            V = nc.vector

            def link(ins):
                chain[0] += 1
                ins.then_inc(dve_c, 1)
                dve.wait_ge(dve_c, chain[0])

            def split_to(n):
                while split[0] <= min(n, MOE0 - 1):
                    m = split[0]
                    dve.wait_ge(hi_ready, m + 1)
                    V.tensor_tensor(wlo[:, m % 2, :], raw[:, m % RING, :], whi[:, m % 2, :].bitcast(F32),
                                    ALU.subtract).then_inc(lo_ready, 1)
                    split[0] += 1

            def after(name, layer):
                split_to(chunk0(layer, name) + 3)

            norms = [0]

            def root(n):
                norms[0] += 1
                dve.wait_ge(rs_ready, norms[0])

            def rstd_of(src, scratch):
                for t in range(NT):
                    ins = V.scalar_tensor_tensor(out=scratch[:, t, :], in0=src[:, t, :], scalar=1.0 / D,
                                                 in1=src[:, t, :], op0=ALU.mult, op1=ALU.mult,
                                                 accum_out=ssq[:, t:t + 1])
                link(ins)
                V.tensor_scalar(ssq[:, 0:NT], ssq[:, 0:NT], EPS, None, ALU.add).then_inc(ss_ready, 1)
                root(NT)

            def normalise(src, scratch):
                rstd_of(src, scratch)
                for t in range(NT):
                    ins = V.tensor_scalar(xn[:, t, :], src[:, t, :], rstd[:, t:t + 1], None, ALU.mult)
                ins.then_inc(xn_ready, 1)

            def turn_out(no, hi, lo, w):
                for b in range(4):
                    dve.wait_ge(xT_hi, 4 * no + b + 1)
                    for i in range(2):
                        k = 2 * b + i
                        ins = V.scalar_tensor_tensor(out=lo[:, k, :], in0=pb[:, 4 + b, i * S:(i + 1) * S],
                                                     scalar=w[:, k:k + 1], in1=hi[:, k, :].bitcast(F32),
                                                     op0=ALU.mult, op1=ALU.subtract)
                ins.then_inc(xT_lo, 1)

            def bc(ap, n):
                return ap.unsqueeze(2).to_broadcast([P, ap.shape[1], n])

            def add_rows(name, layer, half):
                after(name, layer)
                projected(dve, name, layer)
                b = bank(name, layer)
                hh = h[:, :, half * 512:(half + 1) * 512]
                V.tensor_tensor(hh, hh, pb[:, b:b + 2, :], ALU.add).then_inc(lin_dve, 1)

            split_to(1)
            dve.wait_ge(tables_in, 48)
            rawlb = par_("lb_raw")
            link(V.tensor_tensor(lb_s, rawlb[:, 0:2], rawlb[:, 2:4], ALU.max))
            for l in range(DEPTH):
                ins = V.tensor_tensor(lbe[:, 2 * l:2 * l + 2], rawlb[:, 2 * l:2 * l + 2], lb_s, ALU.subtract)
            ins.then_inc(lbx_ready, 1)
            dve.wait_ge(lbx_ready, 2)
            link(V.tensor_tensor(lb_s, lbe[:, 0:2], lbe[:, 2:4], ALU.add))
            link(V.reciprocal(lb_s, lb_s))
            for l in range(DEPTH):
                ins = V.tensor_tensor(lbe[:, 2 * l:2 * l + 2], lbe[:, 2 * l:2 * l + 2], lb_s, ALU.mult)
            link(ins)
            V.tensor_tensor(lb[:, 0:2], lbe[:, 0:2], lbe[:, 0:2], ALU.subtract)
            link(V.tensor_tensor(lb[:, 2:4], lbe[:, 0:2], lbe[:, 2:4], ALU.add))
            link(V.tensor_tensor(lb[:, 2:4], lb[:, 2:4], lbe[:, 0:2], ALU.subtract))
            V.tensor_scalar(lb1m, lb, -1.0, 1.0, ALU.mult, ALU.add)
            link(V.tensor_scalar(lbfl, lb, FLOOR, None, ALU.max))

            for layer in range(DEPTH):
                if layer == 0:
                    dve.wait_ge(x_in, 16)
                normalise(h, sq)
                turn_out(norm_no(layer, "mix"), xTh, xTl, par_("mix_w", layer))
                dve.wait_ge(mem_in, 16 * (layer + 1))
                normalise(memrows, sq)
                V.memset(xraw[:, :, 0:3], 0.0)
                after("gate_small", layer)
                dve.wait_ge(lin_act, evac_count(("gate_small", layer)))
                for t in range(NT):
                    V.scalar_tensor_tensor(out=X12[:, t, 0:4], in0=raw12[:, t, 0:4], scalar=-1.0,
                                           in1=par_("fox_b", layer), op0=ALU.mult, op1=ALU.subtract)
                    ins = V.tensor_tensor(X12[:, t, 4:12], raw12[:, t, 4:12], par_("dt_b", layer), ALU.add)
                link(ins)
                V.scalar_tensor_tensor(out=AX12, in0=X12, scalar=-1.0, in1=X12, op0=ALU.mult,
                                       op1=ALU.max).then_inc(x12_ready, 1)
                turn_out(norm_no(layer, "mem"), memTh, memTl, par_("mem_w", layer))
                cw, cb = par_("conv_w", layer), par_("conv_b", layer)
                for half in range(2):
                    after(f"xbc{half}", layer)
                    dve.wait_ge(lin_act, evac_count((f"xbc{half}", layer)))
                    for tap in (3, 2, 1, 0):
                        for c in range(4 * half, 4 * half + 4):
                            if tap == 3:
                                ins = V.tensor_scalar(xcv[:, c, :], xraw[:, c, 3:3 + S], cw[:, 4 * c + 3:4 * c + 4],
                                                      cb[:, c:c + 1], ALU.mult, ALU.add)
                            else:
                                dve.wait_ge(dve_c, chain[0] - 3)
                                ins = V.scalar_tensor_tensor(out=xcv[:, c, :], in0=xraw[:, c, tap:tap + S],
                                                             scalar=cw[:, 4 * c + tap:4 * c + tap + 1],
                                                             in1=xcv[:, c, :], op0=ALU.mult, op1=ALU.add)
                            chain[0] += 1
                            if half == 1 and tap == 0 and c == 7:
                                chain[0] -= 1
                                ins.then_inc(conv_ready, 1)
                            else:
                                ins.then_inc(dve_c, 1)
                after("z", layer)
                dve.wait_ge(e12_ready, layer + 1)
                link(V.tensor_scalar(Z12, EX12, 2.0, None, ALU.add))
                link(V.reciprocal(Z12, Z12))
                link(V.tensor_tensor(Z12, Z12, EX12, ALU.mult))
                link(V.tensor_tensor(ZZ12, Z12, Z12, ALU.mult))
                link(V.tensor_scalar(PO12, ZZ12, 1.0 / 15, None, ALU.mult))
                for d in (13, 11, 9, 7, 5, 3):
                    link(V.scalar_tensor_tensor(out=PO12, in0=PO12, scalar=1.0 / d, in1=ZZ12, op0=ALU.add, op1=ALU.mult))
                link(V.scalar_tensor_tensor(out=PO12, in0=PO12, scalar=1.0, in1=Z12, op0=ALU.add, op1=ALU.mult))
                link(V.tensor_scalar(X12, X12, 0.0, None, ALU.max))
                link(V.scalar_tensor_tensor(out=SP12, in0=PO12, scalar=2.0, in1=X12, op0=ALU.mult, op1=ALU.add))
                for t in range(NT):
                    V.tensor_scalar(A12[:, t, 0:4], SP12[:, t, 0:4], -1.0, None, ALU.mult)
                    ins = V.scalar_tensor_tensor(out=A12[:, t, 4:12], in0=SP12[:, t, 4:12], scalar=-1.0, in1=aexp,
                                                 op0=ALU.mult, op1=ALU.mult)
                link(ins)
                for t in range(NT):
                    V.tensor_tensor(AUf[:, t, :, :], const("upto").unsqueeze(1).to_broadcast([P, FOX_H, P]),
                                    bc(A12[:, t, 0:4], P), ALU.mult)
                V.tensor_copy(ABf, bc(A12[:, 0, 0:4], P)).then_inc(fa_ready, 1)
                dve.wait_ge(fox_lg, layer + 1)
                V.tensor_reduce(nmax[:, 0:4], pb[:, 4:8, 0:P], AX.X, ALU.max, negate=True)
                V.tensor_reduce(nmax[:, 4:8], pb[:, 4:8, P:3 * P], AX.X, ALU.max, negate=True).then_inc(fox_max, 1)
                dve.wait_ge(hg_e, layer + 1)
                link(V.tensor_scalar(he, hr, 1e37, None, ALU.min))
                link(V.tensor_scalar(hr, he, 1.0, None, ALU.add))
                link(V.reciprocal(hr, hr))
                for a in range(2):
                    i = 2 * layer + a
                    c = slice(a * S, (a + 1) * S)
                    V.scalar_tensor_tensor(out=hk[:, c], in0=he[:, c], scalar=lb1m[:, i:i + 1], in1=hr[:, c],
                                           op0=ALU.mult, op1=ALU.mult)
                    ins = V.tensor_scalar(hl[:, c], hr[:, c], lb1m[:, i:i + 1], lbfl[:, i:i + 1], ALU.mult, ALU.add)
                link(ins)
                link(V.tensor_scalar(hc, hl, 2.0 ** -40, 2.0 ** 60, ALU.is_lt, ALU.mult))
                V.scalar_tensor_tensor(out=hl, in0=hc, scalar=1.0, in1=hl, op0=ALU.max,
                                       op1=ALU.mult).then_inc(hg_f, 1)
                hq = hqT.rearrange("p a s -> p (a s)")
                V.tensor_scalar(hq, hq, DH ** -0.5, None, ALU.mult)
                V.memset(ScT, 0.0).then_inc(hg_qk, 1)
                after("xk0", layer)
                dve.wait_ge(fox_pt, layer + 1)
                V.tensor_copy(PTf.rearrange("p h i q -> p (h i q)"),
                              pb[:, 4:7, :].rearrange("p b q -> p (b q)")).then_inc(fox_ptc, 1)
                link(V.reciprocal(rinv, rsum))
                dve.wait_ge(fox_o, layer + 1)
                V.tensor_tensor(xn[:, :, 0:256].rearrange("p t (h d) -> p t h d", d=DH),
                                pb[:, 7, :].rearrange("p (t h d) -> p t h d", t=NT, h=FOX_H),
                                rinv.rearrange("p (t h) -> p t h", t=NT).unsqueeze(3).to_broadcast([P, NT, FOX_H, DH]),
                                ALU.mult).then_inc(fox_ok, 1)
                dve.wait_ge(hg_l, layer + 1)
                link(V.scalar_tensor_tensor(out=hl, in0=hc, scalar=-60.0 * float(np.log(2.0)) / 2.0 ** 60, in1=hl,
                                            op0=ALU.mult, op1=ALU.add))
                link(V.tensor_tensor_scan(hc, const("restart"), hl, 0.0, ALU.mult, ALU.add))
                NL = len(LEVELS) + 2

                def exponents(lv):
                    n = layer * (NL - 1) + lv - 1
                    if lv >= 3:
                        dve.wait_ge(hg_x, n - 1)
                    if lv < NL - 1:
                        half = LEVELS[lv - 1]
                        c = hc.rearrange("p (b x i) -> p b x i", x=2, i=half)
                        d = Dl[:, (lv - 1) % 2, :].rearrange("p (b x i) -> p b x i", x=2, i=half)
                        nb = 2 * S // (2 * half)
                        mid = c[:, :, 0, half - 1:half].to_broadcast([P, nb, half])
                        V.tensor_tensor(d[:, :, 0, :], mid, c[:, :, 0, :], ALU.subtract)
                        if half == 64:
                            ins = V.tensor_copy(d[:, :, 1, :], c[:, :, 1, :])
                        else:
                            ins = V.tensor_tensor(d[:, :, 1, :], c[:, :, 1, :], mid, ALU.subtract)
                        ins.then_inc(hg_d, 1)
                        return
                    e = Dl[:, (lv - 1) % 2, :].rearrange("p (a t i) -> p a t i", a=2, t=NT)
                    c = hc.rearrange("p (a t i) -> p a t i", a=2, t=NT)
                    mid, end = ([c[:, :, 0, i:i + 1].to_broadcast([P, 2, 64]) for i in (63, 127)])
                    V.tensor_tensor(e[:, :, 0, 0:64], mid, c[:, :, 0, 0:64], ALU.subtract)
                    V.tensor_tensor(e[:, :, 0, 64:P], end, c[:, :, 0, 64:P], ALU.subtract)
                    V.tensor_copy(e[:, :, 1, 0:64], c[:, :, 1, 0:64])
                    link(V.tensor_tensor(e[:, :, 1, 64:P], c[:, :, 1, 64:P],
                                         c[:, :, 1, 63:64].to_broadcast([P, 2, 64]), ALU.add))
                    V.tensor_tensor(e[:, :, 0, 0:64], e[:, :, 0, 0:64], end, ALU.add).then_inc(hg_d, 1)

                def operands(lv):
                    dve.wait_ge(hg_x, layer * (NL - 1) + lv)
                    if lv >= 3:
                        dve.wait_ge(hg_s, layer * NL + lv - 1)
                    V.tensor_tensor(Ql[:, lv % 2, :], hq, El[:, (lv - 1) % 2, :], ALU.mult)
                    V.tensor_tensor(Kl[:, lv % 2, :], hk, El[:, (lv - 1) % 2, :], ALU.mult).then_inc(hg_qk, 1)

                def select(lv):
                    n = layer * NL + lv
                    dve.wait_ge(hg_s, n + 1)
                    b = 4 + 2 * (lv % 2)
                    if lv == NL - 1:
                        V.tensor_copy(ScO.rearrange("p (b h) q -> p b (h q)", b=2),
                                      pb[:, b:b + 2, 0:2 * P]).then_inc(hg_sel, 1)
                    else:
                        if n:
                            dve.wait_ge(hg_sel, n)
                        V.copy_predicated(ScT, lmask[:, lv, :].unsqueeze(1).to_broadcast([P, 8, P]),
                                          pb[:, b:b + 2, :].rearrange("p b (i q) -> p (b i) q", q=P)
                                          ).then_inc(hg_sel, 1)

                after("xk1", layer)
                exponents(1)
                for lv in range(1, NL):
                    if lv + 1 < NL:
                        exponents(lv + 1)
                    operands(lv)
                    select(lv - 1)
                select(NL - 1)
                V.tensor_copy(ABm, bc(A12[:, 1, 4:12], P))
                for t in range(NT):
                    ins = V.tensor_tensor(ALm[:, t, :, :], const("after").unsqueeze(1).to_broadcast([P, M2_H, P]),
                                          bc(A12[:, t, 4:12], P), ALU.mult)
                ins.then_inc(m2_a, 1)
                after("xv0", layer)
                dve.wait_ge(hg_o, layer + 1)
                V.tensor_copy(xn[:, :, 256:512], pb[:, 7, :].rearrange("p (t c) -> p t c", t=NT)).then_inc(hg_ok, 1)
                dve.wait_ge(m2_t, layer + 1)
                V.tensor_tensor(CBs, pb[:, 4:6, 0:3 * P], const("m2mask").unsqueeze(1).to_broadcast([P, 2, 3 * P]),
                                ALU.mult).then_inc(m2_cb, 1)
                dve.wait_ge(m2_xs, layer + 1)
                for t in range(NT):
                    heads = xs[:, t, :].rearrange("p (h d) -> p h d", d=DH)
                    V.tensor_tensor(xcd[:, t, :].rearrange("p (h d) -> p h d", d=DH), heads, bc(SP12[:, t, 4:12], DH),
                                    ALU.mult)
                    V.tensor_tensor(ytmp[:, t, :].rearrange("p (h d) -> p h d", d=DH), heads,
                                    bc(par_("m2_d", layer), DH), ALU.mult)
                dve.wait_ge(m2_cb, layer + 1)
                for rnd in range(2):
                    dve.wait_ge(m2_e, 2 * layer + rnd + 1)
                    m = Mm[:, 4 * rnd:4 * rnd + 4, :]
                    V.tensor_tensor(m, m, CBs[:, rnd, :].unsqueeze(1).to_broadcast([P, 4, 3 * P]),
                                    ALU.mult).then_inc(m2_m, 1)
                after("xv1", layer)
                dve.wait_ge(m2_y, layer + 1)
                om = xn[:, :, 512:1024]
                link(V.tensor_tensor(om, ytmp, pb[:, 4:6, :], ALU.add))
                link(V.tensor_tensor(om, om, zs, ALU.mult))
                link(V.tensor_tensor(sq, xn, xn, ALU.mult))
                ss = ssq.rearrange("p (t c) -> p t c", c=10)
                V.tensor_reduce(ss[:, :, 0:8], sq[:, :, 0:512].rearrange("p t (h d) -> p t h d", d=DH), AX.X, ALU.add)
                link(V.tensor_reduce(ss[:, :, 8:10], sq[:, :, 512:1024].rearrange("p t (h d) -> p t h d", d=256),
                                     AX.X, ALU.add))
                V.tensor_scalar(ss[:, :, 0:8], ss[:, :, 0:8], 1.0 / DH, EPS, ALU.mult, ALU.add)
                V.tensor_scalar(ss[:, :, 8:10], ss[:, :, 8:10], 1.0 / 256, EPS, ALU.mult, ALU.add).then_inc(ss_ready, 1)
                root(20)
                rs = rstd.rearrange("p (t c) -> p t c", c=10)
                for t in range(NT):
                    a = xn[:, t, 0:512].rearrange("p (h d) -> p h d", d=DH)
                    V.tensor_tensor(a, a, bc(rs[:, t, 0:8], DH), ALU.mult)
                    a = xn[:, t, 512:1024].rearrange("p (h d) -> p h d", d=256)
                    ins = V.tensor_tensor(a, a, bc(rs[:, t, 8:10], 256), ALU.mult)
                link(ins)
                V.tensor_tensor(xn[:, :, 256:512], xn[:, :, 256:512], gate, ALU.mult).then_inc(xn_ready, 1)
                turn_out(norm_no(layer, "mixed"), xTh, xTl, par_("out_w", layer))
                add_rows("out0", layer, 0)
                add_rows("out1", layer, 1)
                dve.wait_ge(lin_dve, evac_count(("out1", layer)))
                normalise(h, sq)
                turn_out(norm_no(layer, "xa"), xTh, xTl, par_("xa_w", layer))
                after("xq1", layer)
                dve.wait_ge(xa_lg, layer + 1)
                V.tensor_reduce(nmax, pb[:, 4:8, :].rearrange("p b (t m) -> p (b t) m", t=NT), AX.X, ALU.max,
                                negate=True).then_inc(xa_max, 1)
                dve.wait_ge(xa_p, layer + 1)
                link(V.reciprocal(rinv, rsum))
                V.tensor_tensor(Px, Px, bc(rinv, S), ALU.mult).then_inc(xa_pn, 1)
                dve.wait_ge(xa_pt, 2 * layer + 2)
                V.tensor_copy(PTx[:, 2:4, :, :].rearrange("p h m s -> p h (m s)"), pb[:, 6:8, :]).then_inc(xa_ptd, 1)
                dve.wait_ge(xa_oh, layer + 1)
                V.tensor_tensor(xTl.rearrange("p (b a) s -> p b (a s)", a=2), pb[:, 4:8, :],
                                xTh.rearrange("p (b a) s -> p b (a s)", a=2).bitcast(F32),
                                ALU.subtract).then_inc(xa_ol, 1)
                add_rows("xo0", layer, 0)
                add_rows("xo1", layer, 1)
                dve.wait_ge(lin_dve, evac_count(("xo1", layer)))
                normalise(h, sq)
                turn_out(norm_no(layer, "ffn"), xTh, xTl, par_("ffn_w", layer))
                if layer == 0:
                    for j in range(NF // 2):
                        split_to(chunk0(0) + 2 * j + 3)
                        dve.wait_ge(silu_ready, j + 1)
                        b = 2 * (j % 2)
                        V.tensor_tensor(gated[:, j % 2, :, :], silu[:, j % 2, :, :], pb[:, b:b + 2, S:2 * S],
                                        ALU.mult).then_inc(g_ready, 1)
                        dve.wait_ge(g_ready, j + 1)
                        dve.wait_ge(hT_hi, j + 1)
                        V.tensor_tensor(hTl[:, 2 * j:2 * j + 2, :], gated[:, j % 2, :, :],
                                        hTh[:, 2 * j:2 * j + 2, :].bitcast(F32), ALU.subtract).then_inc(hT_lo, 1)
                    split_to(chunk0(0) + FFN_CHUNKS + 1)
                    dve.wait_ge(w_used, chunk0(0) + FFN_CHUNKS)
                    hh = h.rearrange("p t (n c) -> p (t n) c", c=512)
                    V.tensor_tensor(hh, hh, pb[:, 4:8, :], ALU.add).then_inc(ffn_added, 1)
                    dve.wait_ge(ffn_added, 1)

            dve.wait_ge(xT_lo, norm_no(1, "ffn") + 1)
            V.tensor_tensor(xfull, xTh.bitcast(F32), xTl.bitcast(F32), ALU.add).then_inc(rt_sum, 1)
            dve.wait_ge(rt_lg, 1)
            link(V.tensor_copy(lg, pb[:, 4, 0:NT * NE].rearrange("p (t e) -> p t e", e=NE)))
            for t in range(NT):
                link(V.max(top8[:, t, :], lg[:, t, :]))
                link(V.max_index(idx8[:, t, :].bitcast(U32), top8[:, t, :], lg[:, t, :]))
                V.tensor_copy(idxf[:, t, :], idx8[:, t, :].bitcast(U32))
                ins = V.tensor_tensor(gd[:, t:t + 1], top8[:, t, 1:2], top8[:, t, 0:1], ALU.subtract)
            ins.then_inc(rt_d, 1)
            link(V.memset(gates, 0.0))
            iota8 = const("iota")[:, 0:NE]
            for t in range(NT):
                V.tensor_scalar(oh[:, t, :], iota8, idxf[:, t, 0:1], None, ALU.is_equal)
                ins = V.tensor_scalar(lg[:, t, :], iota8, idxf[:, t, 1:2], None, ALU.is_equal)
            link(ins)
            V.tensor_tensor(routed, oh, lg, ALU.add).then_inc(rt_sum, 1)
            dve.wait_ge(rt_e, 1)
            link(V.tensor_scalar(gs, ge, 1.0, None, ALU.add))
            link(V.reciprocal(g12[:, 0, :], gs))
            link(V.tensor_tensor(g12[:, 1, :], g12[:, 0, :], ge, ALU.mult))
            for t in range(NT):
                V.tensor_scalar(oh[:, t, :], oh[:, t, :], g12[:, 0, t:t + 1], None, ALU.mult)
            link(V.tensor_scalar(lg[:, 0, :], lg[:, 0, :], g12[:, 1, 0:1], None, ALU.mult))
            link(V.tensor_scalar(lg[:, 1, :], lg[:, 1, :], g12[:, 1, 1:2], None, ALU.mult))
            link(V.tensor_tensor(gates[:, :, 1:NE + 1], oh, lg, ALU.add))
            dve.wait_ge(rt_rank, 1)
            link(V.memset(pos, 4.0 * S))
            link(V.tensor_scalar(oh, routed, -4.0 * S, 4.0 * S, ALU.mult, ALU.add))
            link(V.tensor_tensor(pos[:, 0, :, 0:NE], oh, pb[:, 5, 0:NT * NE].rearrange("p (t e) -> p t e", e=NE), ALU.add))
            link(V.tensor_scalar(pos[:, 1, :, 0:NE], pos[:, 0, :, 0:NE], -float(P), None, ALU.add))
            link(V.tensor_reduce(most, pb[:, 5, 2 * NE:3 * NE], AX.X, ALU.max))
            V.tensor_scalar(over_flag.bitcast(U32), most, float(P), None, ALU.is_gt).then_inc(routed_ok, 1)
            dve.wait_ge(routed_ok, 1)

            def experts(p):
                def select_tokens(col, e):
                    for t in range(NT):
                        ins = V.tensor_scalar(sel[:, e, t, :], const("iota"), pos[:, p, t, bass.ds(col, 1)], None,
                                              ALU.is_equal)
                    ins.then_inc(sel_ready, 1)

                def gathered_lo(count, e):
                    dve.wait_ge(xg_hi, count + 1)
                    w = par_("ffn_w", 1)
                    for k in range(KT):
                        ins = V.scalar_tensor_tensor(
                            out=xgl[:, e, k, :], in0=pb[:, 6 + k // 4, (k % 4) * P:(k % 4 + 1) * P],
                            scalar=w[:, k:k + 1], in1=xgh[:, e, k, :].bitcast(F32), op0=ALU.mult, op1=ALU.subtract)
                    ins.then_inc(xg_lo, 1)

                def outputs_lo(count):
                    dve.wait_ge(y_hi, count + 1)
                    V.tensor_tensor(yl.rearrange("p (a c) -> p a c", a=2), pb[:, 2:4, :],
                                    yh.rearrange("p (a c) -> p a c", a=2).bitcast(F32),
                                    ALU.subtract).then_inc(y_lo, 1)

                def add_outputs(count, col, t):
                    dve.wait_ge(spread, count * 2 + (t + 1))
                    for half in range(2):
                        hh = h[:, t, half * 512:(half + 1) * 512]
                        ins = V.scalar_tensor_tensor(out=hh, in0=pb[:, 6 + half, :],
                                                     scalar=gates[:, t, bass.ds(col, 1)], in1=hh,
                                                     op0=ALU.mult, op1=ALU.add)
                    ins.then_inc(ffn_added, 1)

                V.memset(sel[:, 1, :, :], 0.0)
                select_tokens(0, 0)
                gathered_lo(p * (NE + 1), 0)
                with dve.Fori(0, NE // 2) as pair:
                    for e in range(2):
                        expert = pair * 2 + (e + p * NE)
                        lag = pair * 2 + (e + p * (NE + 1))
                        done = [0]

                        def split_experts(m):
                            while done[0] <= m:
                                c = e * FFN_CHUNKS + done[0]
                                dve.wait_ge(hi_ready, pair * (2 * FFN_CHUNKS) + (moe_chunk(p) + c + 1))
                                V.tensor_tensor(wlo[:, (MOE0 + c) % 2, :], xraw_slots[c % XRING],
                                                whi[:, (MOE0 + c) % 2, :].bitcast(F32),
                                                ALU.subtract).then_inc(lo_ready, 1)
                                done[0] += 1

                        def hidden_lo(j):
                            dve.wait_ge(hT_hi, expert * (NF // 2) + (NF // 2 + j + 1))
                            V.tensor_tensor(hTl[:, 2 * j:2 * j + 2, 0:P],
                                            pb[:, 4 + j % 2, 0:2 * P].rearrange("p (f s) -> p f s", f=2),
                                            hTh[:, 2 * j:2 * j + 2, 0:P].bitcast(F32),
                                            ALU.subtract).then_inc(hT_lo, 1)

                        split_experts(1)
                        outputs_lo(lag)
                        for j in range(NF // 2):
                            split_experts(2 * j + 3)
                            dve.wait_ge(silu_ready, expert * (NF // 2) + (NF // 2 + j + 1))
                            V.tensor_tensor(xgated[:, j % 2, :], xsilu[:, j % 2, :], pb[:, j % 2, S:2 * S],
                                            ALU.mult).then_inc(g_ready, 1)
                            if j >= 1:
                                hidden_lo(j - 1)
                            if j == 3:
                                add_outputs(lag, pair * 2 + e, 0)
                            if j == 4:
                                dve.wait_ge(selT_psum, lag + 1)
                                select_tokens(pair * 2 + (e + 1), 1 - e)
                            if j == 6:
                                add_outputs(lag, pair * 2 + e, 1)
                            if j == 8:
                                gathered_lo(lag + 1, 1 - e)
                        split_experts(2 * (NF // 2) + 2)
                        hidden_lo(NF // 2 - 1)
                        split_experts(FFN_CHUNKS - 1)
                count = p * (NE + 1) + NE
                outputs_lo(count)
                add_outputs(count, NE, 0)
                add_outputs(count, NE, 1)
                dve.wait_ge(ffn_added, 1 + 2 * (NE + 1) * (p + 1))

            experts(0)
            more = dve.value_load(over_flag[0:1, :].bitcast(U32), min_val=0, max_val=1)
            with dve.If(more):
                experts(1)
            rstd_of(h, sq)
            for t in range(NT):
                ins = V.scalar_tensor_tensor(out=xn[:, t, :], in0=h[:, t, :], scalar=rstd[:, t:t + 1],
                                             in1=par_("final_w"), op0=ALU.mult, op1=ALU.mult)
            ins.then_inc(fin_ready, 1)


def kernel(**inputs):
    import concourse.bacc as bacc
    from concourse.bass_utils import run_bass_kernel_spmd

    a = {k: np.asarray(v) for k, v in inputs.items()}

    def columns(w):
        return w.reshape(-1, P).T

    def rows(v):
        return np.broadcast_to(v[None, :], (P, v.shape[0]))

    par = []
    for l in range(DEPTH):
        heads = np.concatenate([a["fox_norm_w"][l], a["hg_norm_w"][l], a["m2_norm_w"][l]])
        par += [columns(a["mix_norm_w"][l]), columns(a["xa_norm_w"][l]), columns(a["xa_mem_norm_w"][l]),
                columns(a["ffn_norm_w"][l]), columns(heads),
                a["m2_conv_w"][l].reshape(4, 8, P).transpose(2, 1, 0).reshape(P, 32), columns(a["m2_conv_b"][l]),
                rows(a["fox_f_bias"][l]), rows(a["m2_dt_bias"][l]), rows(a["m2_a_log"][l]), rows(a["m2_d"][l])]
    par += [columns(a["hg_lb_raw"].reshape(-1)),
            a["moe_router"][0].reshape(KT, P, NE).transpose(1, 0, 2).reshape(P, KT * NE), rows(a["final_norm_w"])]
    par = np.ascontiguousarray(np.concatenate(par, axis=1))

    def projection(w, form):
        w = w.reshape(KT, P, 512)
        if form == "T":
            return [w[:, :, c * 256:(c + 1) * 256].transpose(1, 0, 2).reshape(P, CW) for c in range(2)]
        return [w[c * 4:(c + 1) * 4].transpose(1, 0, 2).reshape(P, CW) for c in range(2)]

    lin = []
    for l in range(DEPTH):
        w_in = a["w_in"][l]
        cut = np.cumsum([0, 256, 256, 256, FOX_H, 256, 256, 256, 256, 512, 1024, M2_H])
        fq, fk, fv, ff, hq, hf, hi, hg, z, xbc, dt = (w_in[:, i:j] for i, j in zip(cut[:-1], cut[1:]))
        pad = np.zeros((D, 512 - 256 - FOX_H - M2_H), w_in.dtype)
        w = {"hq_hf": np.concatenate([hq, hf], 1), "gate_small": np.concatenate([hg, ff, dt, pad], 1),
             "xbc0": xbc[:, :512], "xbc1": xbc[:, 512:], "fq_fk": np.concatenate([fq, fk], 1),
             "fv_hi": np.concatenate([fv, hi], 1), "z": z}
        for i in range(2):
            s = slice(512 * i, 512 * i + 512)
            w[f"xk{i}"], w[f"xv{i}"] = a["xa_w_kv"][l][:, :D][:, s], a["xa_w_kv"][l][:, D:][:, s]
            w[f"out{i}"], w[f"xq{i}"], w[f"xo{i}"] = a["w_out"][l][:, s], a["xa_w_q"][l][:, s], a["xa_w_o"][l][:, s]
        for name, form in PROJ:
            lin += projection(w[name], form)
    lin = np.stack(lin)

    def swiglu(w1, w2, expert):
        if expert:
            w1 = w1.reshape(2, KT // 2, P, 2, NF // 2, S).transpose(4, 0, 2, 1, 3, 5).reshape(NF, P, CW)
        else:
            w1 = w1.reshape(KT, P, 2, NF, P).transpose(3, 1, 0, 2, 4).reshape(NF, P, CW)
        w2 = w2.reshape(NF // 2, 2, P, D).transpose(0, 2, 1, 3).reshape(NF // 2, P, CW)
        return np.concatenate([w1, w2])

    ffn = np.stack([swiglu(a["ffn_w1"][0], a["ffn_w2"][0], False)] +
                   [swiglu(a["moe_w1"][0, e], a["moe_w2"][0, e], True) for e in range(NE)])
    arrays = {"x": a["x"], "mem": a["mem"], "par": par, "con": constants(), "lvl": level_masks(), "lin_w": lin,
              "ffn_w": ffn}
    nc = bacc.Bacc("TRN2", target_bir_lowering=False, num_devices=1)
    args = {}
    for name in list(arrays):
        arr = np.ascontiguousarray(arrays[name])
        arrays[f"in_{name}"] = arr
        del arrays[name]
        args[name] = nc.dram_tensor(f"in_{name}", arr.shape, mybir.dt.from_np(arr.dtype), kind="ExternalInput").ap()
    out = nc.dram_tensor("out_0", (1, S, D), F32, kind="ExternalOutput").ap()
    build(nc, out=out, **args)
    r = run_bass_kernel_spmd(nc, [arrays], core_ids=[0])
    return r.results[0]["out_0"]
```

```python
from contextlib import ExitStack

import numpy as np

import concourse.bass as bass
from concourse import mybir

ALU = mybir.AluOpType
ACT = mybir.ActivationFunctionType
F32 = mybir.dt.float32
F32R = mybir.dt.float32r
U32 = mybir.dt.uint32
AX = mybir.AxisListType

P = 128
D = 1024
S = 256
NT = S // P
KT = D // P
DEPTH = 2
DFF = 2816
NF = DFF // P
NE = 8
DH = 64
FOX_H, HG_H, M2_H = 4, 4, 8
EPS = 1e-6
FLOOR = 1e-30
NEG = -1e30
LEVELS = (1, 2, 4, 8, 16, 32, 64)

CW = 2048
RING = 4
XRING = 6
HRING = 3
PASSES = 2
LIN = 17
LIN_CHUNKS = 2 * LIN
W1_CHUNKS = NF
W2_CHUNKS = NF // 2
FFN_CHUNKS = W1_CHUNKS + W2_CHUNKS
PROJ = (("hq_hf", "T"), ("gate_small", "R"), ("fq_fk", "T"), ("fv_hi", "R"), ("xbc0", "T"), ("xbc1", "T"),
        ("z", "R"), ("xk0", "T"), ("xk1", "T"), ("xv0", "R"), ("out0", "R"), ("out1", "R"), ("xv1", "R"),
        ("xq0", "T"), ("xq1", "T"), ("xo0", "R"), ("xo1", "R"))
PIDX = {name: i for i, (name, _) in enumerate(PROJ)}
DVE_EVAC = ("out0", "out1", "xo0", "xo1")
assert len(PROJ) == LIN

_PER_LAYER = (("mix_w", 8), ("xa_w", 8), ("mem_w", 8), ("ffn_w", 8), ("out_w", 8), ("conv_w", 32), ("conv_b", 8),
              ("fox_b", 4), ("dt_b", 8), ("a_log", 8), ("m2_d", 8))
PCOL = {}
_n = 0
for _l in range(DEPTH):
    for _name, _w in _PER_LAYER:
        PCOL[_name, _l] = (_n, _n + _w)
        _n += _w
for _name, _w in (("lb_raw", 4), ("router", KT * NE), ("final_w", D)):
    PCOL[_name] = (_n, _n + _w)
    _n += _w
NPAR = _n

CCOL = {}
_n = 0
for _name, _w in (("ident", P), ("neg", P), ("upto", P), ("ones", P), ("after", P), ("m2mask", 3 * P),
                  ("before", P), ("restart", 2 * S), ("iota", P), ("minus_half", 20)):
    CCOL[_name] = (_n, _n + _w)
    _n += _w
NCONST = _n


def constants():
    r = np.arange(P)
    upto = (r[:, None] <= r[None, :]).astype(np.float32)
    one = np.ones((P, P), np.float32)
    restart = np.broadcast_to((np.arange(2 * S) % 64 != 0).astype(np.float32), (P, 2 * S))
    parts = [np.eye(P, dtype=np.float32), (upto - np.eye(P)) * NEG, upto, one, (r[:, None] > r[None, :]) * 1.0,
             upto, one, upto, upto - np.eye(P), restart, np.broadcast_to(np.arange(P), (P, P)), np.full((P, 20), -0.5)]
    return np.concatenate([p.astype(np.float32) for p in parts], axis=1)


def level_masks():
    r = np.arange(P)
    masks = [r[:, None] == r[None, :]]
    for half in LEVELS:
        same = (r[:, None] // (2 * half)) == (r[None, :] // (2 * half))
        masks.append(same & ((r[:, None] // half) % 2 == 0) & ((r[None, :] // half) % 2 == 1))
    return np.stack(masks, axis=1).astype(np.uint32).reshape(P, -1)


def build(nc, x, mem, par, con, lvl, lin_w, ffn_w, out):
    groups = []
    for layer in range(DEPTH):
        groups += [(name, layer) for name, _ in PROJ]
        if layer == 0:
            groups += [("w1", j) for j in range(NF // 2)]
    GI = {g: i for i, g in enumerate(groups)}

    def by_dve(g):
        return g[0] in DVE_EVAC

    def evac_count(g):
        return sum(by_dve(q) == by_dve(g) for q in groups[:GI[g] + 1] if q[0] != "w1")

    def chunk0(layer, name=None):
        base = layer * (LIN_CHUNKS + FFN_CHUNKS)
        return base + (LIN_CHUNKS if name is None else 2 * PIDX[name])

    MOE0 = chunk0(1)

    with ExitStack() as ctx:
        def sb(name, shape, dt=F32):
            return ctx.enter_context(nc.sbuf_tensor(name, shape, dt))[:]

        def sem(name):
            return ctx.enter_context(nc.semaphore(name))

        ARENA = 17600
        arena_at = -(-nc.sbuf_base // 32) * 32
        arena = sb("arena", [P, ARENA])

        def over(name, at, n):
            return nc.alloc_sbuf_tensor_at(name, [P, n], F32R, offset=arena_at + 4 * at)[:]

        raw_at = -(-nc.sbuf_base // 32) * 32
        raw = sb("raw", [P, RING, CW])
        wlo = nc.alloc_sbuf_tensor_at("wlo", [P, RING, CW], F32R, offset=raw_at)[:]
        whi = sb("whi", [P, HRING, CW], F32R)
        h = sb("h", [P, NT, D])
        xn = sb("xn", [P, NT, D])
        xTh, xTl = sb("xTh", [P, KT, S], F32R), sb("xTl", [P, KT, S], F32R)
        mTh, mTl = sb("mTh", [P, KT * S], F32R), sb("mTl", [P, KT * S], F32R)
        memTh, memTl = (m.rearrange("p (k s) -> p k s", k=KT) for m in (mTh, mTl))
        xgh, xgl = (m.rearrange("p (e k s) -> p e k s", e=2, k=KT) for m in (mTh, mTl))
        kvX_at = -(-nc.sbuf_base // 32) * 32
        kvX = sb("kvX", [P, 4 * D])
        kX = kvX[:, 0:2 * D].rearrange("p (k s) -> p k s", k=KT)
        vX = kvX[:, 2 * D:4 * D].rearrange("p (t d) -> p t d", t=NT)
        params = sb("params", [P, NPAR])
        consts = sb("consts", [P, NCONST])
        lmask = sb("lmask", [P, len(LEVELS) + 1, P], U32)
        small = sb("small", [P, 600])

        top = [0]

        def small_(n):
            top[0] += n
            assert top[0] <= 600
            return small[:, top[0] - n:top[0]]

        def carve(at, *shape):
            n = int(np.prod(shape))
            assert at + n <= ARENA, at + n
            v = arena[:, at:at + n]
            if len(shape) == 1:
                return v
            names = "abcd"[:len(shape)]
            return v.rearrange(f"p ({' '.join(names)}) -> p {' '.join(names)}",
                               **{c: s for c, s in zip(names[1:], shape[1:])})

        def const(name):
            return consts[:, CCOL[name][0]:CCOL[name][1]]

        def par_(name, layer=None):
            a, b = PCOL[name if layer is None else (name, layer)]
            return params[:, a:b]

        hqT = carve(0, 2, S)
        hfT = carve(512, 2, S)
        gate = carve(1024, NT, 256)
        zs = carve(1536, NT, 512)
        fqT = carve(2560, 2, S)
        fkT = carve(3072, 2, S)
        vtok = carve(3584, NT, 512)
        xraw = carve(4608, 8, S + 3)
        xcv = carve(6688, 8, S)
        AUf = carve(8736, NT, FOX_H, P)
        ABf = carve(9760, FOX_H, P)
        Pf = carve(10272, FOX_H, 3 * P)
        PTf = carve(10272, FOX_H, 3, P)
        El = carve(8736, 2, 2 * S)
        ScO = carve(9760, HG_H, P)
        hk = carve(11808, 2 * S)
        hl = carve(12320, 2 * S)
        hc = carve(12832, 2 * S)
        he = carve(13344, 2 * S)
        hr = carve(13856, 2 * S)
        Dl = carve(13344, 2, 2 * S)
        Ql = carve(14368, 2, 2 * S)
        Kl = carve(15392, 2, 2 * S)
        ScT = carve(16416, FOX_H * NT, P)
        Mm = carve(8736, M2_H, 3 * P)
        CBs = carve(11808, 2, 3 * P)
        xs = carve(12576, NT, 512)
        xcd = carve(4608, NT, 512)
        ALm = carve(14368, NT, M2_H, P)
        ABm = carve(2560, M2_H, P)
        ytmp = carve(3584, NT, 512)
        sq = carve(4608, NT, D)
        memrows = carve(8736, NT, D)
        qX = carve(0, KT, S)
        Px = carve(2048, 4 * NT, S)
        PTx = carve(11264, 4, 2, S)
        hTh, hTl = (over(name, at, NF * S).rearrange("p (f s) -> p f s", f=NF)
                    for name, at in (("hTh", 0), ("hTl", NF * S)))
        silu = carve(11264, 2, 2, S)
        gated = carve(12288, 2, 2, S)
        xfull = carve(0, KT, S)
        xsilu = carve(11264, 2, S)
        xgated = carve(11776, 2, S)
        sel = over("sel", 12288, 2 * NT * P).rearrange("p (e t s) -> p e t s", e=2, t=NT)
        xnh, xnl = (m.rearrange("p k s -> p (k s)").rearrange("p (t d) -> p t d", t=NT) for m in (xTh, xTl))
        yh, yl = over("yh", 12800, D), over("yl", 13824, D)
        selT = over("selT", 14848, S)
        kvXr = nc.alloc_sbuf_tensor_at("kvXr", [P, 2, CW], F32R, offset=kvX_at)
        xraw_slots = [kvX[:, 0:CW], kvX[:, CW:2 * CW]] + [raw[:, (MOE0 + i) % RING, :] for i in range(RING)]
        xlo_slots = [kvXr[:, 0, :], kvXr[:, 1, :]] + [wlo[:, (MOE0 + i) % RING, :] for i in range(RING)]

        raw12 = small_(NT * 12).rearrange("p (t c) -> p t c", c=12)
        X12, AX12, EX12, Z12, ZZ12, PO12, SP12, A12 = (
            small_(NT * 12).rearrange("p (t c) -> p t c", c=12) for _ in range(8))
        aexp = small_(8)
        lbe = small_(4)
        lb_s = small_(2)
        lb = small_(4)
        lb1m = small_(4)
        lbfl = small_(4)
        nmax = small_(8)
        rsum = small_(8)
        rinv = small_(8)
        ssq = small_(20)
        rstd = small_(20)
        lg = small_(NT * NE).rearrange("p (t e) -> p t e", e=NE)
        top8 = small_(NT * 8).rearrange("p (t e) -> p t e", e=8)
        idx8 = small_(NT * 8).rearrange("p (t e) -> p t e", e=8)
        idxf = small_(NT * 8).rearrange("p (t e) -> p t e", e=8)
        gd = small_(NT)
        ge = small_(NT)
        gs = small_(NT)
        g12 = small_(2 * NT).rearrange("p (k t) -> p k t", k=2)
        oh = small_(NT * NE).rearrange("p (t e) -> p t e", e=NE)
        routed = small_(NT * NE).rearrange("p (t e) -> p t e", e=NE)
        gates = small_(NT * (NE + 1)).rearrange("p (t e) -> p t e", e=NE + 1)
        pos = small_(PASSES * NT * (NE + 1)).rearrange("p (r t e) -> p r t e", r=PASSES, t=NT)
        most = small_(1)
        over_flag = small_(1)

        pb = ctx.enter_context(nc.psum_tensor("pb", [P, 8, 512], F32))[:]

        slot_loaded = [sem(f"slot_loaded{i}") for i in range(RING)]
        hi_ready = sem("hi_ready")
        lo_ready = sem("lo_ready")
        w_used = sem("w_used")
        x_in = sem("x_in")
        mem_in = sem("mem_in")
        tables_in = sem("tables_in")
        masks_in = sem("masks_in")
        out_sent = sem("out_sent")
        xn_ready = sem("xn_ready")
        turned = sem("turned")
        xT_hi = sem("xT_hi")
        xT_lo = sem("xT_lo")
        rows_ready = sem("rows_ready")
        sq_act = sem("sq_act")
        half0_added = sem("half0_added")
        ss_ready = sem("ss_ready")
        rs_ready = sem("rs_ready")
        lin_act = sem("lin_act")
        lin_dve = sem("lin_dve")
        dve_c = sem("dve_c")
        pool_c = sem("pool_c")
        conv_ready = sem("conv_ready")
        xcv_ready = sem("xcv_ready")
        x12_ready = sem("x12_ready")
        e12_ready = sem("e12_ready")
        lbx_ready = sem("lbx_ready")
        fa_ready = sem("fa_ready")
        fox_lg = sem("fox_lg")
        fox_max = sem("fox_max")
        fox_p = sem("fox_p")
        fox_pt = sem("fox_pt")
        fox_ptc = sem("fox_ptc")
        fox_o = sem("fox_o")
        fox_ok = sem("fox_ok")
        hg_e = sem("hg_e")
        hg_f = sem("hg_f")
        hg_l = sem("hg_l")
        hg_d = sem("hg_d")
        hg_x = sem("hg_x")
        hg_qk = sem("hg_qk")
        hg_s = sem("hg_s")
        hg_sel = sem("hg_sel")
        hg_o = sem("hg_o")
        hg_ok = sem("hg_ok")
        m2_t = sem("m2_t")
        m2_xs = sem("m2_xs")
        m2_cb = sem("m2_cb")
        m2_a = sem("m2_a")
        m2_seg = sem("m2_seg")
        m2_e = sem("m2_e")
        m2_m = sem("m2_m")
        m2_y = sem("m2_y")
        xa_lg = sem("xa_lg")
        xa_max = sem("xa_max")
        xa_p = sem("xa_p")
        xa_pn = sem("xa_pn")
        xa_pt = sem("xa_pt")
        xa_pta = sem("xa_pta")
        xa_ptd = sem("xa_ptd")
        xa_o = sem("xa_o")
        xa_oh = sem("xa_oh")
        xa_ol = sem("xa_ol")
        silu_ready = sem("silu_ready")
        g_ready = sem("g_ready")
        hT_hi = sem("hT_hi")
        hT_lo = sem("hT_lo")
        xn_hi = sem("xn_hi")
        xn_lo = sem("xn_lo")
        rt_sum = sem("rt_sum")
        rt_rank = sem("rt_rank")
        routed_ok = sem("routed_ok")
        x_loaded = [sem(f"x_loaded{i}") for i in range(XRING)]
        sel_ready = sem("sel_ready")
        gathered = sem("gathered")
        xg_hi = sem("xg_hi")
        xg_lo = sem("xg_lo")
        hid_turned = sem("hid_turned")
        y_hi = sem("y_hi")
        y_lo = sem("y_lo")
        selT_psum = sem("selT_psum")
        selT_ready = sem("selT_ready")
        spread = sem("spread")
        ffn_added = sem("ffn_added")
        rt_lg = sem("rt_lg")
        rt_d = sem("rt_d")
        rt_e = sem("rt_e")
        fin_ready = sem("fin_ready")

        def moe_chunk(p):
            return MOE0 + p * NE * FFN_CHUNKS

        def projected(eng, name, layer):
            eng.wait_ge(w_used, chunk0(layer, name) + 2)

        def norm_no(layer, what):
            return 5 * layer + ("mix", "mem", "mixed", "xa", "ffn").index(what)

        def bank(name, layer):
            return 2 * (GI[name, layer] % 2)

        block = ctx.enter_context(nc.Block())

        @block.sync
        def _(sp):
            sp.dma_start(h[:, :, :], x.rearrange("b (t p) d -> p (b t) d", p=P)).then_inc(x_in, 16)
            sp.dma_start(consts[:, :], con).then_inc(tables_in, 16)
            sp.dma_start(params[:, :], par).then_inc(tables_in, 16)

            def load(n, src):
                if n >= RING:
                    sp.wait_ge(w_used, n - RING + 1)
                sp.dma_start(raw[:, n % RING, :], src).then_inc(slot_loaded[n % RING], 16)

            for layer in range(DEPTH):
                for c in range(LIN_CHUNKS):
                    load(chunk0(layer, PROJ[0][0]) + c, lin_w[layer * LIN_CHUNKS + c])
                    if layer == 0 and c == RING - 1:
                        sp.dma_start(lmask[:, :, :].rearrange("p a b -> p (a b)"), lvl).then_inc(masks_in, 16)
                if layer == 0:
                    for c in range(FFN_CHUNKS):
                        load(chunk0(0) + c, ffn_w[0, c])
            sp.wait_ge(w_used, chunk0(1, "xo0") + 1)

            def load_experts(p):
                with sp.Fori(0, NE // 2) as pair:
                    for e in range(2):
                        for c in range(FFN_CHUNKS):
                            m = e * FFN_CHUNKS + c
                            sp.wait_ge(w_used, pair * (2 * FFN_CHUNKS) + (moe_chunk(p) + m - XRING + 1))
                            sp.dma_start(xraw_slots[m % XRING], ffn_w[1 + pair * 2 + e, c]
                                         ).then_inc(x_loaded[m % XRING], 16)

            load_experts(0)
            sp.wait_ge(routed_ok, 1)
            more = sp.value_load(over_flag[0:1, :].bitcast(U32), min_val=0, max_val=1)
            with sp.If(more):
                load_experts(1)
            sp.wait_ge(fin_ready, 1)
            sp.dma_start(out.rearrange("b (t p) d -> p (b t) d", p=P), xn[:, :, :]).then_inc(out_sent, 16)
            sp.wait_ge(out_sent, 16)

        @block.gpsimd
        def _(pool):
            order = []
            for layer in range(DEPTH):
                order += [NT, NT, 20, NT, NT]
            order.append(NT)
            for i, n in enumerate(order):
                pool.wait_ge(ss_ready, i + 1)
                if i == 0:
                    pool.wait_ge(tables_in, 32)
                nc.gpsimd.tensor_tensor(rstd[:, 0:n], ssq[:, 0:n], const("minus_half")[:, 0:n],
                                        ALU.pow).then_inc(rs_ready, 1)

        @block.scalar
        def _(act):
            split, squares = [0], [0]

            def split_to(n):
                while split[0] <= min(n, MOE0 - 1):
                    m = split[0]
                    act.wait_ge(slot_loaded[m % RING], 16 * (m // RING + 1))
                    if m >= HRING:
                        act.wait_ge(w_used, m - HRING + 1)
                    nc.scalar.activation(whi[:, m % HRING, :], raw[:, m % RING, :], ACT.Copy).then_inc(hi_ready, 1)
                    split[0] += 1

            def after(name, layer):
                split_to(chunk0(layer, name) + 1 + HRING)

            def mean_square(src, by_dve=True):
                if by_dve:
                    squares[0] += 1
                    act.wait_ge(rows_ready, squares[0])
                nc.scalar.activation(sq[:, 1, :], src[:, 1, :], ACT.Square, scale=D ** -0.5,
                                     accum_out=ssq[:, 1:2]).then_inc(sq_act, 1)

            act.wait_ge(x_in, 16)
            mean_square(h, False)
            act.wait_ge(lbx_ready, 1)
            nc.scalar.activation(lbe, lbe, ACT.Exp).then_inc(lbx_ready, 1)
            split_to(0)
            act.wait_ge(tables_in, 32)

            def turn_out(no, dst, w):
                for b in range(4):
                    act.wait_ge(turned, 4 * no + b + 1)
                    for i in range(2):
                        k = 2 * b + i
                        ins = nc.scalar.activation(dst[:, k, :], pb[:, 4 + b, i * S:(i + 1) * S], ACT.Copy,
                                                   scale=w[:, k:k + 1])
                    ins.then_inc(xT_hi, 1)

            def take(name, layer, *ops):
                after(name, layer)
                projected(act, name, layer)
                b = bank(name, layer)
                for dst, a, z, func, scale, one in ops:
                    src = pb[:, b:b + 2, a:z] if one is None else pb[:, b + one, a:z]
                    ins = nc.scalar.activation(dst, src, func, scale=scale)
                ins.then_inc(lin_act, 1)

            def cols(ap):
                return ap.rearrange("p a s -> p (a s)")

            def tiles(ap):
                return ap.rearrange("p (b a) s -> p b (a s)", b=2)

            for layer in range(DEPTH):
                if layer:
                    mean_square(h)
                    act.wait_ge(ffn_added, 1)
                act.dma_start(memrows, mem.rearrange("b (t p) d -> p (b t) d", p=P)).then_inc(mem_in, 16)
                turn_out(norm_no(layer, "mix"), xTh, par_("mix_w", layer))
                split_to(chunk0(layer, PROJ[0][0]) - 1 + HRING)
                act.wait_ge(mem_in, 16 * (layer + 1))
                mean_square(memrows, False)
                take("hq_hf", layer, (cols(hqT), 0, 512, ACT.Silu, 1.0, 0), (cols(hfT), 0, 512, ACT.Copy, 1.0, 1))
                take("gate_small", layer, (gate, 0, 256, ACT.Silu, 1.0, None),
                     (raw12, 256, 268, ACT.Copy, 1.0, None))
                nc.scalar.preload_act_table_set("natural_log_exp_and_others")
                act.wait_ge(x12_ready, layer + 1)
                nc.scalar.activation(aexp, par_("a_log", layer), ACT.Exp)
                nc.scalar.activation(EX12, AX12, ACT.Exp, scale=-1.0).then_inc(e12_ready, 1)
                nc.scalar.activation(hr, cols(hfT), ACT.Exp, scale=-1.0).then_inc(hg_e, 1)
                take("fq_fk", layer, (cols(fqT), 0, 512, ACT.Copy, DH ** -0.5, 0),
                     (cols(fkT), 0, 512, ACT.Copy, 1.0, 1))
                turn_out(norm_no(layer, "mem"), memTh, par_("mem_w", layer))
                take("fv_hi", layer, (vtok, 0, 512, ACT.Copy, 1.0, None))
                act.wait_ge(hg_f, layer + 1)
                nc.scalar.activation(hl, hl, ACT.Ln).then_inc(hg_l, 1)
                act.wait_ge(fox_max, layer + 1)
                for hd in range(FOX_H):
                    for t in range(NT):
                        a, z = (0, P) if t == 0 else (P, 3 * P)
                        i = t * FOX_H + hd
                        ins = nc.scalar.activation(Pf[:, hd, a:z], pb[:, 4 + hd, a:z], ACT.Exp,
                                                   bias=nmax[:, i:i + 1], accum_out=rsum[:, i:i + 1])
                ins.then_inc(fox_p, 1)
                def take_xbc(i):
                    after(f"xbc{i}", layer)
                    projected(act, f"xbc{i}", layer)
                    for b in range(2):
                        ins = nc.scalar.activation(
                            xraw[:, 4 * i + 2 * b:4 * i + 2 * b + 2, 3:],
                            pb[:, bank(f"xbc{i}", layer) + b, :].rearrange("p (a s) -> p a s", a=2), ACT.Copy)
                    ins.then_inc(lin_act, 1)

                take_xbc(0)
                split_to(chunk0(layer, "xbc1") + HRING)
                NL = len(LEVELS) + 2
                for lv in range(1, NL):
                    act.wait_ge(hg_d, layer * (NL - 1) + lv)
                    act.wait_ge(hg_qk, layer * NL + max(1, lv - 1))
                    nc.scalar.activation(El[:, (lv - 1) % 2, :], Dl[:, (lv - 1) % 2, :], ACT.Exp).then_inc(hg_x, 1)
                    if lv == 2:
                        take_xbc(1)
                split_to(chunk0(layer, "z") + HRING)
                act.wait_ge(conv_ready, layer + 1)
                nc.scalar.activation(xcv, xcv, ACT.Silu).then_inc(xcv_ready, 1)
                take("z", layer, (zs, 0, 512, ACT.Silu, 1.0, None))
                take("xk0", layer, (tiles(kX[:, 0:4, :]), 0, 512, ACT.Copy, 1.0, None))
                act.wait_ge(m2_t, layer + 1)
                nc.scalar.activation(xs, pb[:, 6:8, :], ACT.Copy).then_inc(m2_xs, 1)
                for r in range(2):
                    act.wait_ge(m2_seg, 2 * layer + r + 1)
                    nc.scalar.activation(Mm[:, 4 * r:4 * r + 4, :], pb[:, 4:8, 0:3 * P], ACT.Exp).then_inc(m2_e, 1)
                    if r == 1:
                        split_to(chunk0(layer, "xk1") + HRING)
                take("xk1", layer, (tiles(kX[:, 4:8, :]), 0, 512, ACT.Copy, 1.0, None))
                split_to(chunk0(layer, "xv0") + HRING)
                turn_out(norm_no(layer, "mixed"), xTh, par_("out_w", layer))
                take("xv0", layer, (vX[:, :, 0:512], 0, 512, ACT.Copy, 1.0, None))
                after("out0", layer)
                after("out1", layer)
                mean_square(h)
                split_to(chunk0(layer, "xv1") + HRING)
                turn_out(norm_no(layer, "xa"), xTh, par_("xa_w", layer))
                take("xv1", layer, (vX[:, :, 512:1024], 0, 512, ACT.Copy, 1.0, None))
                for i in range(2):
                    take(f"xq{i}", layer, (tiles(qX[:, 4 * i:4 * i + 4, :]), 0, 512, ACT.Copy, 256 ** -0.5, None))
                for hd in range(4):
                    if hd % 2 == 0:
                        act.wait_ge(xa_max, 2 * layer + hd // 2 + 1)
                    for t in range(NT):
                        i = 2 * hd + t
                        ins = nc.scalar.activation(Px[:, i, :], pb[:, 4 + hd, t * S:(t + 1) * S], ACT.Exp,
                                                   bias=nmax[:, i:i + 1], accum_out=rsum[:, i:i + 1])
                    if hd % 2:
                        ins.then_inc(xa_p, 1)
                act.wait_ge(xa_pt, 2 * layer + 1)
                nc.scalar.activation(PTx[:, 0:2, :, :].rearrange("p h m s -> p h (m s)"), pb[:, 4:6, :],
                                     ACT.Copy).then_inc(xa_pta, 1)
                for i in range(2):
                    act.wait_ge(xa_o, 2 * layer + i + 1)
                    nc.scalar.activation(xTh[:, 4 * i:4 * i + 4, :].rearrange("p (b a) s -> p b (a s)", a=2),
                                         pb[:, 4 + 2 * i:6 + 2 * i, :], ACT.Copy).then_inc(xa_oh, 1)
                after("xo1", layer)
                mean_square(h)
                turn_out(norm_no(layer, "ffn"), xTh, par_("ffn_w", layer))
                if layer == 0:
                    for j in range(NF // 2):
                        split_to(chunk0(0) + 2 * j + 1 + HRING)
                        act.wait_ge(w_used, chunk0(0) + 2 * j + 2)
                        b = 2 * (j % 2)
                        nc.scalar.activation(silu[:, j % 2, :, :], pb[:, b:b + 2, 0:S], ACT.Silu).then_inc(silu_ready, 1)
                        act.wait_ge(g_ready, j + 1)
                        nc.scalar.activation(hTh[:, 2 * j:2 * j + 2, :], gated[:, j % 2, :, :],
                                             ACT.Copy).then_inc(hT_hi, 1)
                    split_to(chunk0(0) + FFN_CHUNKS - 2 + HRING)

            def first_chunks(p):
                for c in range(HRING):
                    act.wait_ge(x_loaded[c], 16 * (1 + p * NE * FFN_CHUNKS // XRING))
                    act.wait_ge(w_used, moe_chunk(p) + c - HRING + 1)
                    nc.scalar.activation(whi[:, (MOE0 + c) % HRING, :], xraw_slots[c], ACT.Copy).then_inc(hi_ready, 1)

            first_chunks(0)
            act.wait_ge(rt_sum, 1)
            nc.scalar.activation(xnh, xn, ACT.Copy).then_inc(xn_hi, 1)
            act.wait_ge(rt_d, 1)
            nc.scalar.activation(ge, gd, ACT.Exp).then_inc(rt_e, 1)

            def experts(p):
                def gathered_hi(expert, e):
                    act.wait_ge(gathered, expert + 1)
                    for k in range(KT):
                        w = par_("ffn_w", 1)
                        ins = nc.scalar.activation(xgh[:, e, k, :], pb[:, 6 + k // 4, (k % 4) * P:(k % 4 + 1) * P],
                                                   ACT.Copy, scale=w[:, k:k + 1])
                    ins.then_inc(xg_hi, 1)

                def outputs_hi(expert):
                    act.wait_ge(w_used, expert * FFN_CHUNKS + MOE0)
                    nc.scalar.activation(yh.rearrange("p (a c) -> p a c", a=2), pb[:, 2:4, :],
                                         ACT.Copy).then_inc(y_hi, 1)

                def selection_turned(expert):
                    act.wait_ge(selT_psum, expert + 1)
                    nc.scalar.activation(selT, pb[:, 6, 0:S], ACT.Copy).then_inc(selT_ready, 1)

                def two_experts(pair, last):
                    for e in range(2):
                        expert = pair * 2 + (e + p * NE)
                        lag = pair * 2 + (e + p * (NE + 1))
                        done = [HRING]

                        def split_experts(m):
                            while done[0] <= m and not (last and e * FFN_CHUNKS + done[0] >= 2 * FFN_CHUNKS):
                                c = e * FFN_CHUNKS + done[0]
                                at = pair * (2 * FFN_CHUNKS) + (moe_chunk(p) + c)
                                act.wait_ge(x_loaded[c % XRING], pair * (2 * FFN_CHUNKS // XRING * 16) + 16 * (
                                    c // XRING + 1 + p * NE * FFN_CHUNKS // XRING))
                                act.wait_ge(w_used, at - HRING + 1)
                                nc.scalar.activation(whi[:, (MOE0 + c) % HRING, :], xraw_slots[c % XRING],
                                                     ACT.Copy).then_inc(hi_ready, 1)
                                done[0] += 1

                        outputs_hi(expert)
                        for j in range(NF // 2):
                            split_experts(2 * j + 1 + HRING)
                            act.wait_ge(w_used, expert * FFN_CHUNKS + (MOE0 + 2 * j + 2))
                            nc.scalar.activation(xsilu[:, j % 2, :], pb[:, j % 2, 0:S], ACT.Silu).then_inc(silu_ready, 1)
                            if j >= 1:
                                hidden_hi(act, j - 1, expert)
                            if j == 1:
                                selection_turned(lag)
                            if j == 8:
                                gathered_hi(lag + 1, 1 - e)
                        split_experts(W1_CHUNKS + HRING)
                        hidden_hi(act, NF // 2 - 1, expert)
                        split_experts(FFN_CHUNKS - 1 + HRING)

                gathered_hi(p * (NE + 1), 0)
                with act.Fori(0, NE // 2 - 1) as pair:
                    two_experts(pair, False)
                two_experts(NE // 2 - 1, True)
                outputs_hi((p + 1) * NE)
                selection_turned(p * (NE + 1) + NE)

            def hidden_hi(eng, j, expert):
                eng.wait_ge(hid_turned, expert * (NF // 2) + (j + 1))
                nc.scalar.activation(hTh[:, 2 * j:2 * j + 2, 0:P],
                                     pb[:, 4 + j % 2, 0:2 * P].rearrange("p (f s) -> p f s", f=2),
                                     ACT.Copy).then_inc(hT_hi, 1)

            experts(0)
            act.wait_ge(routed_ok, 1)
            more = act.value_load(over_flag[0:1, :].bitcast(U32), min_val=0, max_val=1)
            with act.If(more):
                first_chunks(1)
                experts(1)
            mean_square(h)

        @block.tensor
        def _(pe):
            ident = const("ident")
            upto, after, before, ones = const("upto"), const("after"), const("before"), const("ones")
            ones_after = consts[:, CCOL["ones"][0]:CCOL["ones"][0] + 2 * P]
            upto_ones = consts[:, CCOL["upto"][0]:CCOL["upto"][0] + 2 * P]
            pe.wait_ge(tables_in, 32)

            def turn(no):
                pe.wait_ge(xn_ready, no + 1)
                for b in range(4):
                    for i in range(2):
                        k = 2 * b + i
                        for t in range(NT):
                            mm = nc.tensor.transpose(pb[:, 4 + b, i * S + t * P:i * S + (t + 1) * P],
                                                     xn[:, t, k * P:(k + 1) * P], ident)
                    mm.then_inc(turned, 1)

            def split_product(o, lhs, rhs, first, last):
                (lh, ll), (rh, rl) = lhs, rhs
                nc.tensor.matmul(o, lh, rh, start=first, stop=False)
                nc.tensor.matmul(o, lh, rl, start=False, stop=False)
                return nc.tensor.matmul(o, ll, rh, start=False, stop=last)

            def parts(n):
                return whi[:, n % HRING, :], wlo[:, n % RING, :]

            def columns_ready(layer, what, k):
                pe.wait_ge(xT_lo, 4 * norm_no(layer, what) + k // 2 + 1)

            def project(name, layer, act_in, chunks=(0, 1), norm=None):
                g = GI[name, layer]
                prev = groups[g - 2]
                if 0 in chunks and g >= 2 and prev[0] != "w1":
                    pe.wait_ge(lin_dve if by_dve(prev) else lin_act, evac_count(prev))
                b = bank(name, layer)
                for c in chunks:
                    n = chunk0(layer, name) + c
                    pe.wait_ge(lo_ready, n + 1)
                    if PROJ[PIDX[name]][1] == "T":
                        w = [part.rearrange("p (k m) -> p k m", k=KT) for part in parts(n)]
                        for i in range(2):
                            for k in range(KT):
                                if norm and c == 0 and i == 0:
                                    columns_ready(layer, norm, k)
                                mm = split_product(pb[:, b + c, i * S:(i + 1) * S],
                                                   [part[:, k, i * P:(i + 1) * P] for part in w],
                                                   [part[:, k, :] for part in act_in], k == 0, k == KT - 1)
                    else:
                        w = [part.rearrange("p (k m) -> p k m", k=KT // 2) for part in parts(n)]
                        for t in range(NT):
                            for kk in range(KT // 2):
                                k = c * (KT // 2) + kk
                                if norm and t == 0:
                                    columns_ready(layer, norm, k)
                                mm = split_product(pb[:, b + t, :], [part[:, k, t * P:(t + 1) * P] for part in act_in],
                                                   [part[:, kk, :] for part in w], k == 0, k == KT - 1)
                    mm.then_inc(w_used, 1)

            X, M = (xTh, xTl), (memTh, memTl)
            for layer in range(DEPTH):
                turn(norm_no(layer, "mix"))
                project("hq_hf", layer, X, norm="mix")
                project("gate_small", layer, X)
                project("fq_fk", layer, X)
                turn(norm_no(layer, "mem"))
                project("fv_hi", layer, X)
                pe.wait_ge(lin_act, evac_count(("fq_fk", layer)))
                pe.wait_ge(fa_ready, layer + 1)
                pe.wait_ge(xT_lo, 4 * norm_no(layer, "mem") + 4)
                for hd in range(FOX_H):
                    r = slice(DH * (hd % 2), DH * (hd % 2) + DH)
                    q, k = fqT[r, hd // 2, :], fkT[r, hd // 2, :]
                    b = pb[:, 4 + hd, :]
                    nc.tensor.matmul(b[:, 0:P], q[:, 0:P], k[:, 0:P], start=True, stop=False)
                    nc.tensor.matmul(b[:, 0:P], AUf[:, 0, hd, :], after, start=False, stop=False)
                    nc.tensor.matmul(b[:, 0:P], ident, const("neg"), start=False, stop=True)
                    nc.tensor.matmul(b[:, P:3 * P], q[:, P:S], k, start=True, stop=False)
                    nc.tensor.matmul(b[:, P:3 * P], AUf[:, 1, hd, :], ones_after, start=False, stop=False)
                    nc.tensor.matmul(b[:, P:2 * P], ABf[:, hd, :], after, start=False, stop=False)
                    mm = nc.tensor.matmul(b[:, 2 * P:3 * P], ident, const("neg"), start=False, stop=True)
                mm.then_inc(fox_lg, 1)
                project("xbc0", layer, X, (0,))
                pe.wait_ge(fox_p, layer + 1)
                for hd in range(FOX_H):
                    for i in range(3):
                        n = 3 * hd + i
                        mm = nc.tensor.transpose(pb[:, 4 + n // 4, (n % 4) * P:(n % 4 + 1) * P],
                                                 Pf[:, hd, i * P:(i + 1) * P], ident)
                mm.then_inc(fox_pt, 1)
                pe.wait_ge(lin_act, evac_count(("fv_hi", layer)))
                project("xbc0", layer, X, (1,))
                project("xbc1", layer, X, (0,))
                pe.wait_ge(fox_ptc, layer + 1)
                for hd in range(FOX_H):
                    v = vtok[:, :, hd * DH:(hd + 1) * DH]
                    o = pb[:, 7, :].rearrange("p (t h d) -> p t h d", t=NT, h=FOX_H)
                    nc.tensor.matmul(o[:, 0, hd, :], PTf[:, hd, 0, :], v[:, 0, :], start=True, stop=True)
                    nc.tensor.matmul(o[:, 1, hd, :], PTf[:, hd, 1, :], v[:, 0, :], start=True, stop=False)
                    mm = nc.tensor.matmul(o[:, 1, hd, :], PTf[:, hd, 2, :], v[:, 1, :], start=False, stop=True)
                mm.then_inc(fox_o, 1)
                project("xbc1", layer, X, (1,))
                pe.wait_ge(fox_ok, layer + 1)
                NL = len(LEVELS) + 2
                for lv in range(NL):
                    n = layer * NL + lv
                    pe.wait_ge(hg_qk, n + 1)
                    if n >= 2:
                        pe.wait_ge(hg_sel, n - 1)
                    Q = (hqT.rearrange("p a s -> p (a s)") if lv == 0 else Ql[:, lv % 2, :])
                    K = (hk if lv == 0 else Kl[:, lv % 2, :])
                    b = 4 + 2 * (lv % 2)
                    for hd in range(HG_H):
                        r = slice(DH * (hd % 2), DH * (hd % 2) + DH)
                        o = S * (hd // 2)
                        if lv < NL - 1:
                            for t in range(NT):
                                i = 2 * (hd // 2) + t
                                mm = nc.tensor.matmul(pb[:, b + hd % 2, i * P:(i + 1) * P],
                                                      K[r, o + t * P:o + (t + 1) * P], Q[r, o + t * P:o + (t + 1) * P],
                                                      start=True, stop=True)
                        else:
                            i = hd // 2
                            mm = nc.tensor.matmul(pb[:, b + hd % 2, i * P:(i + 1) * P], K[r, o:o + P],
                                                  Q[r, o + P:o + 2 * P], start=True, stop=True)
                    mm.then_inc(hg_s, 1)
                    if lv in (1, 3):
                        project("z", layer, X, ((lv - 1) // 2,))
                project("xk0", layer, M, (0,))
                pe.wait_ge(hg_sel, (layer + 1) * NL)
                for hd in range(HG_H):
                    v = vtok[:, :, 256 + hd * DH:256 + (hd + 1) * DH]
                    at = 4 * (hd % 2) + 2 * (hd // 2)
                    o = pb[:, 7, :].rearrange("p (t h d) -> p t h d", t=NT, h=HG_H)
                    nc.tensor.matmul(o[:, 0, hd, :], ScT[:, at, :], v[:, 0, :], start=True, stop=True)
                    nc.tensor.matmul(o[:, 1, hd, :], ScO[:, at // 2, :], v[:, 0, :], start=True, stop=False)
                    mm = nc.tensor.matmul(o[:, 1, hd, :], ScT[:, at + 1, :], v[:, 1, :], start=False, stop=True)
                mm.then_inc(hg_o, 1)
                project("xk0", layer, M, (1,))
                pe.wait_ge(xcv_ready, layer + 1)
                pe.wait_ge(hg_ok, layer + 1)
                for g in range(2):
                    B, C = xcv[:, 4 + g, :], xcv[:, 6 + g, :]
                    nc.tensor.matmul(pb[:, 4 + g, 0:S], B[:, 0:P], C, start=True, stop=True)
                    nc.tensor.matmul(pb[:, 4 + g, S:S + P], B[:, P:S], C[:, P:S], start=True, stop=True)
                for t in range(NT):
                    for c in range(4):
                        mm = nc.tensor.transpose(pb[:, 6 + t, c * P:(c + 1) * P], xcv[:, c, t * P:(t + 1) * P], ident)
                mm.then_inc(m2_t, 1)
                pe.wait_ge(m2_a, layer + 1)
                pe.wait_ge(m2_cb, layer + 1)
                pe.wait_ge(m2_xs, layer + 1)
                for rnd in range(2):
                    if rnd:
                        project("xk1", layer, M, (0,))
                        pe.wait_ge(m2_e, 2 * layer + 1)
                    for i in range(4):
                        hd = 4 * rnd + i
                        b = pb[:, 4 + i, :]
                        nc.tensor.matmul(b[:, 0:2 * P], ALm[:, 0, hd, :], upto_ones, start=True, stop=False)
                        nc.tensor.matmul(b[:, P:2 * P], ABm[:, hd, :], upto, start=False, stop=True)
                        mm = nc.tensor.matmul(b[:, 2 * P:3 * P], ALm[:, 1, hd, :], upto, start=True, stop=True)
                    mm.then_inc(m2_seg, 1)
                project("xk1", layer, M, (1,))
                pe.wait_ge(m2_m, 2 * layer + 2)
                for hd in range(M2_H):
                    xh = xcd[:, :, hd * DH:(hd + 1) * DH]
                    o = slice(hd * DH, (hd + 1) * DH)
                    nc.tensor.matmul(pb[:, 4, o], Mm[:, hd, 0:P], xh[:, 0, :], start=True, stop=True)
                    nc.tensor.matmul(pb[:, 5, o], Mm[:, hd, P:2 * P], xh[:, 0, :], start=True, stop=False)
                    mm = nc.tensor.matmul(pb[:, 5, o], Mm[:, hd, 2 * P:3 * P], xh[:, 1, :], start=False, stop=True)
                mm.then_inc(m2_y, 1)
                project("xv0", layer, M)
                turn(norm_no(layer, "mixed"))
                project("out0", layer, X, norm="mixed")
                project("out1", layer, X)
                project("xv1", layer, M)
                turn(norm_no(layer, "xa"))
                project("xq0", layer, X, norm="xa")
                project("xq1", layer, X)
                pe.wait_ge(lin_act, evac_count(("xq1", layer)))
                for hd in range(4):
                    for t in range(NT):
                        for k in range(2):
                            mm = nc.tensor.matmul(pb[:, 4 + hd, t * S:(t + 1) * S],
                                                  qX[:, 2 * hd + k, t * P:(t + 1) * P], kX[:, 2 * hd + k, :],
                                                  start=(k == 0), stop=(k == 1))
                    if hd % 2:
                        mm.then_inc(xa_lg, 1)
                for hd in range(4):
                    if hd % 2 == 0:
                        pe.wait_ge(xa_pn, 2 * layer + hd // 2 + 1)
                    for m in range(2):
                        for t in range(NT):
                            mm = nc.tensor.transpose(pb[:, 4 + hd, m * S + t * P:m * S + (t + 1) * P],
                                                     Px[:, 2 * hd + t, m * P:(m + 1) * P], ident)
                    if hd % 2:
                        mm.then_inc(xa_pt, 1)
                for hd in range(4):
                    if hd % 2 == 0:
                        pe.wait_ge((xa_pta, xa_ptd)[hd // 2], layer + 1)
                    for k in range(2):
                        for m in range(2):
                            c = hd * 256 + k * P
                            mm = nc.tensor.matmul(pb[:, 4 + hd, k * S:(k + 1) * S], vX[:, m, c:c + P],
                                                  PTx[:, hd, m, :], start=(m == 0), stop=(m == 1))
                    if hd % 2:
                        mm.then_inc(xa_o, 1)
                pe.wait_ge(xa_ol, 2 * layer + 2)
                project("xo0", layer, X)
                project("xo1", layer, X)
                turn(norm_no(layer, "ffn"))
                if layer == 0:
                    pe.wait_ge(lin_dve, evac_count(("xo1", 0)))
                    for j in range(NF // 2):
                        if j >= 2:
                            pe.wait_ge(g_ready, j - 1)
                        b = 2 * (j % 2)
                        for i in range(2):
                            n = chunk0(0) + 2 * j + i
                            pe.wait_ge(lo_ready, n + 1)
                            w = [part.rearrange("p (k m) -> p k m", k=KT) for part in parts(n)]
                            for half in range(2):
                                for k in range(KT):
                                    if j + i + half == 0:
                                        columns_ready(0, "ffn", k)
                                    mm = split_product(pb[:, b + i, half * S:(half + 1) * S],
                                                       [part[:, k, half * P:(half + 1) * P] for part in w],
                                                       [part[:, k, :] for part in X], k == 0, k == KT - 1)
                            mm.then_inc(w_used, 1)
                    for c in range(W2_CHUNKS):
                        n = chunk0(0) + W1_CHUNKS + c
                        pe.wait_ge(hT_lo, c + 1)
                        pe.wait_ge(lo_ready, n + 1)
                        w = [part.rearrange("p (k m) -> p k m", k=2) for part in parts(n)]
                        for k in range(2):
                            f = 2 * c + k
                            for t in range(NT):
                                for half in range(2):
                                    mm = split_product(pb[:, 4 + 2 * t + half, :],
                                                       [part[:, f, t * P:(t + 1) * P] for part in (hTh, hTl)],
                                                       [part[:, k, half * 512:(half + 1) * 512] for part in w],
                                                       f == 0, f == NF - 1)
                        mm.then_inc(w_used, 1)
                    pe.wait_ge(ffn_added, 1)

            router = par_("router").rearrange("p (k e) -> p k e", e=NE)
            pe.wait_ge(rt_sum, 1)
            for t in range(NT):
                for k in range(KT):
                    mm = nc.tensor.matmul(pb[:, 4, t * NE:(t + 1) * NE], xfull[:, k, t * P:(t + 1) * P],
                                          router[:, k, :], start=(k == 0), stop=(k == KT - 1))
            mm.then_inc(rt_lg, 1)
            pe.wait_ge(rt_sum, 2)
            rank = pb[:, 5, :]
            nc.tensor.matmul(rank[:, 0:NE], before, routed[:, 0, :], start=True, stop=True)
            nc.tensor.matmul(rank[:, NE:2 * NE], ones, routed[:, 0, :], start=True, stop=False)
            nc.tensor.matmul(rank[:, NE:2 * NE], before, routed[:, 1, :], start=False, stop=True)
            nc.tensor.matmul(rank[:, 2 * NE:3 * NE], ones, routed[:, 0, :], start=True, stop=False)
            nc.tensor.matmul(rank[:, 2 * NE:3 * NE], ones, routed[:, 1, :], start=False,
                             stop=True).then_inc(rt_rank, 1)

            def experts(p):
                def gather(count, e):
                    pe.wait_ge(sel_ready, count + 1)
                    for k in range(KT):
                        for t in range(NT):
                            for i, part in enumerate((xnh, xnl)):
                                mm = nc.tensor.matmul(pb[:, 6 + k // 4, (k % 4) * P:(k % 4 + 1) * P],
                                                      part[:, t, k * P:(k + 1) * P], sel[:, e, t, :],
                                                      start=(t + i == 0), stop=(t + i == NT))
                    mm.then_inc(gathered, 1)

                def turn_selection(count, e):
                    for t in range(NT):
                        mm = nc.tensor.transpose(pb[:, 6, t * P:(t + 1) * P], sel[:, e, t, :].bitcast(F32), ident)
                    mm.then_inc(selT_psum, 1)

                def spread_outputs(count, t):
                    if t == 0:
                        pe.wait_ge(selT_ready, count + 1)
                        pe.wait_ge(y_lo, count + 1)
                    else:
                        pe.wait_ge(ffn_added, count * 2 + 2)
                    for half in range(2):
                        c = slice(half * 512, (half + 1) * 512)
                        nc.tensor.matmul(pb[:, 6 + half, :], selT[:, t * P:(t + 1) * P], yh[:, c], start=True, stop=False)
                        mm = nc.tensor.matmul(pb[:, 6 + half, :], selT[:, t * P:(t + 1) * P], yl[:, c],
                                              start=False, stop=True)
                    mm.then_inc(spread, 1)

                pe.wait_ge(xn_lo, 1)
                gather(p * (NE + 1), 0)
                with pe.Fori(0, NE // 2) as pair:
                    for e in range(2):
                        expert = pair * 2 + (e + p * NE)
                        lag = pair * 2 + (e + p * (NE + 1))

                        def turn_hidden(j):
                            pe.wait_ge(g_ready, expert * (NF // 2) + (NF // 2 + j + 1))
                            for i in range(2):
                                mm = nc.tensor.transpose(pb[:, 4 + j % 2, i * P:(i + 1) * P],
                                                         xgated[:, j % 2, i * P:(i + 1) * P], ident)
                            mm.then_inc(hid_turned, 1)

                        def ready(c):
                            pe.wait_ge(lo_ready, expert * FFN_CHUNKS + (MOE0 + c + 1))
                            n = MOE0 + e * FFN_CHUNKS + c
                            return whi[:, n % HRING, :], xlo_slots[(n - MOE0) % XRING]

                        pe.wait_ge(xg_lo, lag + 1)
                        for j in range(NF // 2):
                            pe.wait_ge(g_ready, expert * (NF // 2) + (NF // 2 + max(0, j - 1)))
                            for c in range(2):
                                w = [part.rearrange("p (k m) -> p k m", k=KT // 2) for part in ready(2 * j + c)]
                                for kk in range(KT // 2):
                                    k = c * (KT // 2) + kk
                                    mm = split_product(pb[:, j % 2, :], [part[:, e, k, :] for part in (xgh, xgl)],
                                                       [part[:, kk, :] for part in w], k == 0, k == KT - 1)
                                mm.then_inc(w_used, 1)
                            if j >= 1:
                                if j >= 3:
                                    pe.wait_ge(hT_lo, expert * (NF // 2) + (NF // 2 + j - 2))
                                turn_hidden(j - 1)
                            if j == 1:
                                turn_selection(lag, 1 - e)
                            if j == 3:
                                spread_outputs(lag, 0)
                            if j == 6:
                                spread_outputs(lag, 1)
                            if j == 8:
                                pe.wait_ge(ffn_added, lag * 2 + 3)
                                gather(lag + 1, 1 - e)
                        for c in range(W2_CHUNKS):
                            w = [part.rearrange("p (k m) -> p k m", k=2) for part in ready(W1_CHUNKS + c)]
                            if c == 0:
                                pe.wait_ge(y_lo, lag + 1)
                            pe.wait_ge(hT_lo, expert * (NF // 2) + (NF // 2 + c + 1))
                            for k in range(2):
                                f = 2 * c + k
                                for half in range(2):
                                    mm = split_product(pb[:, 2 + half, :], [part[:, f, 0:P] for part in (hTh, hTl)],
                                                       [part[:, k, half * 512:(half + 1) * 512] for part in w],
                                                       f == 0, f == NF - 1)
                            mm.then_inc(w_used, 1)
                            if c == 0:
                                pe.wait_ge(hT_lo, expert * (NF // 2) + (2 * (NF // 2) - 2))
                                turn_hidden(NF // 2 - 1)
                count = p * (NE + 1) + NE
                pe.wait_ge(xg_lo, count + 1)
                turn_selection(count, 1)
                spread_outputs(count, 0)
                spread_outputs(count, 1)

            experts(0)
            pe.wait_ge(routed_ok, 1)
            more = pe.value_load(over_flag[0:1, :].bitcast(U32), min_val=0, max_val=1)
            with pe.If(more):
                pe.wait_ge(ffn_added, 1 + 2 * (NE + 1))
                experts(1)

        @block.vector
        def _(dve):
            chain, split = [0], [0]
            V = nc.vector

            def link(ins):
                chain[0] += 1
                ins.then_inc(dve_c, 1)
                dve.wait_ge(dve_c, chain[0])

            def split_to(n):
                while split[0] <= min(n, MOE0 - 1):
                    m = split[0]
                    dve.wait_ge(hi_ready, m + 1)
                    V.tensor_tensor(wlo[:, m % RING, :], raw[:, m % RING, :], whi[:, m % HRING, :].bitcast(F32),
                                    ALU.subtract).then_inc(lo_ready, 1)
                    split[0] += 1

            def after(name, layer):
                split_to(chunk0(layer, name) + 1 + HRING)

            norms, squares = [0], [0]

            def root():
                norms[0] += 1
                dve.wait_ge(rs_ready, norms[0])

            def rstd_of(src):
                link(V.scalar_tensor_tensor(out=sq[:, 0, :], in0=src[:, 0, :], scalar=1.0 / D, in1=src[:, 0, :],
                                            op0=ALU.mult, op1=ALU.mult, accum_out=ssq[:, 0:1]))
                squares[0] += 1
                dve.wait_ge(sq_act, squares[0])
                V.tensor_scalar(ssq[:, 0:NT], ssq[:, 0:NT], EPS, None, ALU.add).then_inc(ss_ready, 1)
                root()

            def normalise(src):
                rstd_of(src)
                for t in range(NT):
                    ins = V.tensor_scalar(xn[:, t, :], src[:, t, :], rstd[:, t:t + 1], None, ALU.mult)
                ins.then_inc(xn_ready, 1)

            def turn_out(no, hi, lo, w):
                for b in range(4):
                    dve.wait_ge(xT_hi, 4 * no + b + 1)
                    for i in range(2):
                        k = 2 * b + i
                        ins = V.scalar_tensor_tensor(out=lo[:, k, :], in0=pb[:, 4 + b, i * S:(i + 1) * S],
                                                     scalar=w[:, k:k + 1], in1=hi[:, k, :].bitcast(F32),
                                                     op0=ALU.mult, op1=ALU.subtract)
                    ins.then_inc(xT_lo, 1)

            def bc(ap, n):
                return ap.unsqueeze(2).to_broadcast([P, ap.shape[1], n])

            def add_rows(name, layer, half):
                projected(dve, name, layer)
                b = bank(name, layer)
                for t in (1, 0):
                    hh = h[:, t, half * 512:(half + 1) * 512]
                    V.tensor_tensor(hh, hh, pb[:, b + t, :], ALU.add).then_inc(lin_dve if t == 0 else (
                        rows_ready if half else half0_added), 1)

            dve.wait_ge(x_in, 16)
            normalise(h)
            dve.wait_ge(tables_in, 32)
            rawlb = par_("lb_raw")
            link(V.tensor_tensor(lb_s, rawlb[:, 0:2], rawlb[:, 2:4], ALU.max))
            for l in range(DEPTH):
                ins = V.tensor_tensor(lbe[:, 2 * l:2 * l + 2], rawlb[:, 2 * l:2 * l + 2], lb_s, ALU.subtract)
            ins.then_inc(lbx_ready, 1)
            dve.wait_ge(lbx_ready, 2)
            link(V.tensor_tensor(lb_s, lbe[:, 0:2], lbe[:, 2:4], ALU.add))
            link(V.reciprocal(lb_s, lb_s))
            for l in range(DEPTH):
                ins = V.tensor_tensor(lbe[:, 2 * l:2 * l + 2], lbe[:, 2 * l:2 * l + 2], lb_s, ALU.mult)
            link(ins)
            V.tensor_tensor(lb[:, 0:2], lbe[:, 0:2], lbe[:, 0:2], ALU.subtract)
            link(V.tensor_tensor(lb[:, 2:4], lbe[:, 0:2], lbe[:, 2:4], ALU.add))
            link(V.tensor_tensor(lb[:, 2:4], lb[:, 2:4], lbe[:, 0:2], ALU.subtract))
            V.tensor_scalar(lb1m, lb, -1.0, 1.0, ALU.mult, ALU.add)
            link(V.tensor_scalar(lbfl, lb, FLOOR, None, ALU.max))

            for layer in range(DEPTH):
                if layer == 0:
                    split_to(0)
                else:
                    normalise(h)
                turn_out(norm_no(layer, "mix"), xTh, xTl, par_("mix_w", layer))
                split_to(chunk0(layer, PROJ[0][0]) - 1 + HRING)
                dve.wait_ge(mem_in, 16 * (layer + 1))
                normalise(memrows)
                V.memset(xraw[:, :, 0:3], 0.0)
                after("gate_small", layer)
                dve.wait_ge(lin_act, evac_count(("gate_small", layer)))
                for t in range(NT):
                    V.scalar_tensor_tensor(out=X12[:, t, 0:4], in0=raw12[:, t, 0:4], scalar=-1.0,
                                           in1=par_("fox_b", layer), op0=ALU.mult, op1=ALU.subtract)
                    ins = V.tensor_tensor(X12[:, t, 4:12], raw12[:, t, 4:12], par_("dt_b", layer), ALU.add)
                link(ins)
                V.scalar_tensor_tensor(out=AX12, in0=X12, scalar=-1.0, in1=X12, op0=ALU.mult,
                                       op1=ALU.max).then_inc(x12_ready, 1)
                cw, cb = par_("conv_w", layer), par_("conv_b", layer)

                def convolve(half):
                    after(f"xbc{half}", layer)
                    dve.wait_ge(lin_act, evac_count((f"xbc{half}", layer)))
                    for tap in (3, 2, 1, 0):
                        for c in range(4 * half, 4 * half + 4):
                            if tap == 3:
                                ins = V.tensor_scalar(xcv[:, c, :], xraw[:, c, 3:3 + S], cw[:, 4 * c + 3:4 * c + 4],
                                                      cb[:, c:c + 1], ALU.mult, ALU.add)
                            else:
                                dve.wait_ge(dve_c, chain[0] - 3)
                                ins = V.scalar_tensor_tensor(out=xcv[:, c, :], in0=xraw[:, c, tap:tap + S],
                                                             scalar=cw[:, 4 * c + tap:4 * c + tap + 1],
                                                             in1=xcv[:, c, :], op0=ALU.mult, op1=ALU.add)
                            chain[0] += 1
                            if half == 1 and tap == 0 and c == 7:
                                chain[0] -= 1
                                ins.then_inc(conv_ready, 1)
                            else:
                                ins.then_inc(dve_c, 1)

                dve.wait_ge(e12_ready, layer + 1)
                link(V.tensor_scalar(Z12, EX12, 2.0, None, ALU.add))
                link(V.reciprocal(Z12, Z12))
                link(V.tensor_tensor(Z12, Z12, EX12, ALU.mult))
                link(V.tensor_tensor(ZZ12, Z12, Z12, ALU.mult))
                link(V.tensor_scalar(PO12, ZZ12, 1.0 / 15, None, ALU.mult))
                for d in (13, 11, 9, 7, 5, 3):
                    link(V.scalar_tensor_tensor(out=PO12, in0=PO12, scalar=1.0 / d, in1=ZZ12, op0=ALU.add, op1=ALU.mult))
                link(V.scalar_tensor_tensor(out=PO12, in0=PO12, scalar=1.0, in1=Z12, op0=ALU.add, op1=ALU.mult))
                link(V.tensor_scalar(X12, X12, 0.0, None, ALU.max))
                link(V.scalar_tensor_tensor(out=SP12, in0=PO12, scalar=2.0, in1=X12, op0=ALU.mult, op1=ALU.add))
                for t in range(NT):
                    V.tensor_scalar(A12[:, t, 0:4], SP12[:, t, 0:4], -1.0, None, ALU.mult)
                    ins = V.scalar_tensor_tensor(out=A12[:, t, 4:12], in0=SP12[:, t, 4:12], scalar=-1.0, in1=aexp,
                                                 op0=ALU.mult, op1=ALU.mult)
                link(ins)
                for t in range(NT):
                    V.tensor_tensor(AUf[:, t, :, :], const("upto").unsqueeze(1).to_broadcast([P, FOX_H, P]),
                                    bc(A12[:, t, 0:4], P), ALU.mult)
                V.tensor_copy(ABf, bc(A12[:, 0, 0:4], P)).then_inc(fa_ready, 1)
                after("fq_fk", layer)
                turn_out(norm_no(layer, "mem"), memTh, memTl, par_("mem_w", layer))
                dve.wait_ge(hg_e, layer + 1)
                link(V.tensor_scalar(he, hr, 1e37, None, ALU.min))
                link(V.tensor_scalar(hr, he, 1.0, None, ALU.add))
                link(V.reciprocal(hr, hr))
                for a in range(2):
                    i = 2 * layer + a
                    c = slice(a * S, (a + 1) * S)
                    V.scalar_tensor_tensor(out=hk[:, c], in0=he[:, c], scalar=lb1m[:, i:i + 1], in1=hr[:, c],
                                           op0=ALU.mult, op1=ALU.mult)
                    ins = V.tensor_scalar(hl[:, c], hr[:, c], lb1m[:, i:i + 1], lbfl[:, i:i + 1], ALU.mult, ALU.add)
                link(ins)
                link(V.tensor_scalar(hc, hl, 2.0 ** -40, 2.0 ** 60, ALU.is_lt, ALU.mult))
                V.scalar_tensor_tensor(out=hl, in0=hc, scalar=1.0, in1=hl, op0=ALU.max,
                                       op1=ALU.mult).then_inc(hg_f, 1)
                hq = hqT.rearrange("p a s -> p (a s)")
                V.tensor_scalar(hq, hq, DH ** -0.5, None, ALU.mult)
                V.memset(ScT, 0.0).then_inc(hg_qk, 1)
                after("fv_hi", layer)
                dve.wait_ge(fox_lg, layer + 1)
                V.tensor_reduce(nmax[:, 0:4], pb[:, 4:8, 0:P], AX.X, ALU.max, negate=True)
                V.tensor_reduce(nmax[:, 4:8], pb[:, 4:8, P:3 * P], AX.X, ALU.max, negate=True).then_inc(fox_max, 1)
                dve.wait_ge(hg_l, layer + 1)
                link(V.scalar_tensor_tensor(out=hl, in0=hc, scalar=-60.0 * float(np.log(2.0)) / 2.0 ** 60, in1=hl,
                                            op0=ALU.mult, op1=ALU.add))
                link(V.tensor_tensor_scan(hc, const("restart"), hl, 0.0, ALU.mult, ALU.add))
                dve.wait_ge(fox_pt, layer + 1)
                V.tensor_copy(PTf.rearrange("p h i q -> p (h i q)"),
                              pb[:, 4:7, :].rearrange("p b q -> p (b q)")).then_inc(fox_ptc, 1)
                link(V.reciprocal(rinv, rsum))
                convolve(0)
                split_to(chunk0(layer, "xbc1") + HRING)
                dve.wait_ge(fox_o, layer + 1)
                V.tensor_tensor(xn[:, :, 0:256].rearrange("p t (h d) -> p t h d", d=DH),
                                pb[:, 7, :].rearrange("p (t h d) -> p t h d", t=NT, h=FOX_H),
                                rinv.rearrange("p (t h) -> p t h", t=NT).unsqueeze(3).to_broadcast([P, NT, FOX_H, DH]),
                                ALU.mult).then_inc(fox_ok, 1)
                NL = len(LEVELS) + 2

                def exponents(lv):
                    n = layer * (NL - 1) + lv - 1
                    if lv >= 3:
                        dve.wait_ge(hg_x, n - 1)
                    if lv < NL - 1:
                        half = LEVELS[lv - 1]
                        c = hc.rearrange("p (b x i) -> p b x i", x=2, i=half)
                        d = Dl[:, (lv - 1) % 2, :].rearrange("p (b x i) -> p b x i", x=2, i=half)
                        nb = 2 * S // (2 * half)
                        mid = c[:, :, 0, half - 1:half].to_broadcast([P, nb, half])
                        V.tensor_tensor(d[:, :, 0, :], mid, c[:, :, 0, :], ALU.subtract)
                        if half == 64:
                            ins = V.tensor_copy(d[:, :, 1, :], c[:, :, 1, :])
                        else:
                            ins = V.tensor_tensor(d[:, :, 1, :], c[:, :, 1, :], mid, ALU.subtract)
                        ins.then_inc(hg_d, 1)
                        return
                    e = Dl[:, (lv - 1) % 2, :].rearrange("p (a t i) -> p a t i", a=2, t=NT)
                    c = hc.rearrange("p (a t i) -> p a t i", a=2, t=NT)
                    mid, end = ([c[:, :, 0, i:i + 1].to_broadcast([P, 2, 64]) for i in (63, 127)])
                    V.tensor_tensor(e[:, :, 0, 0:64], mid, c[:, :, 0, 0:64], ALU.subtract)
                    V.tensor_tensor(e[:, :, 0, 64:P], end, c[:, :, 0, 64:P], ALU.subtract)
                    V.tensor_copy(e[:, :, 1, 0:64], c[:, :, 1, 0:64])
                    link(V.tensor_tensor(e[:, :, 1, 64:P], c[:, :, 1, 64:P],
                                         c[:, :, 1, 63:64].to_broadcast([P, 2, 64]), ALU.add))
                    V.tensor_tensor(e[:, :, 0, 0:64], e[:, :, 0, 0:64], end, ALU.add).then_inc(hg_d, 1)

                def operands(lv):
                    dve.wait_ge(hg_x, layer * (NL - 1) + lv)
                    if lv >= 3:
                        dve.wait_ge(hg_s, layer * NL + lv - 1)
                    V.tensor_tensor(Ql[:, lv % 2, :], hq, El[:, (lv - 1) % 2, :], ALU.mult)
                    V.tensor_tensor(Kl[:, lv % 2, :], hk, El[:, (lv - 1) % 2, :], ALU.mult).then_inc(hg_qk, 1)

                def select(lv):
                    n = layer * NL + lv
                    if n == 0:
                        dve.wait_ge(masks_in, 16)
                    dve.wait_ge(hg_s, n + 1)
                    b = 4 + 2 * (lv % 2)
                    if lv == NL - 1:
                        V.tensor_copy(ScO.rearrange("p (b h) q -> p b (h q)", b=2),
                                      pb[:, b:b + 2, 0:2 * P]).then_inc(hg_sel, 1)
                    else:
                        if n:
                            dve.wait_ge(hg_sel, n)
                        V.copy_predicated(ScT, lmask[:, lv, :].unsqueeze(1).to_broadcast([P, 8, P]),
                                          pb[:, b:b + 2, :].rearrange("p b (i q) -> p (b i) q", q=P)
                                          ).then_inc(hg_sel, 1)

                exponents(1)
                for lv in range(1, NL):
                    if lv + 1 < NL:
                        exponents(lv + 1)
                    operands(lv)
                    if lv == 3:
                        convolve(1)
                    select(lv - 1)
                select(NL - 1)
                split_to(chunk0(layer, "z") + HRING)
                V.tensor_copy(ABm, bc(A12[:, 1, 4:12], P))
                for t in range(NT):
                    ins = V.tensor_tensor(ALm[:, t, :, :], const("after").unsqueeze(1).to_broadcast([P, M2_H, P]),
                                          bc(A12[:, t, 4:12], P), ALU.mult)
                ins.then_inc(m2_a, 1)
                dve.wait_ge(hg_o, layer + 1)
                V.tensor_copy(xn[:, :, 256:512], pb[:, 7, :].rearrange("p (t c) -> p t c", t=NT)).then_inc(hg_ok, 1)
                ss = ssq.rearrange("p (t c) -> p t c", c=10)
                rs = rstd.rearrange("p (t c) -> p t c", c=10)
                after("z", layer)
                dve.wait_ge(m2_t, layer + 1)
                V.tensor_tensor(CBs, pb[:, 4:6, 0:3 * P], const("m2mask").unsqueeze(1).to_broadcast([P, 2, 3 * P]),
                                ALU.mult).then_inc(m2_cb, 1)
                after("xk0", layer)
                dve.wait_ge(m2_xs, layer + 1)
                for t in range(NT):
                    heads = xs[:, t, :].rearrange("p (h d) -> p h d", d=DH)
                    V.tensor_tensor(xcd[:, t, :].rearrange("p (h d) -> p h d", d=DH), heads, bc(SP12[:, t, 4:12], DH),
                                    ALU.mult)
                    V.tensor_tensor(ytmp[:, t, :].rearrange("p (h d) -> p h d", d=DH), heads,
                                    bc(par_("m2_d", layer), DH), ALU.mult)
                dve.wait_ge(m2_cb, layer + 1)
                for rnd in range(2):
                    dve.wait_ge(m2_e, 2 * layer + rnd + 1)
                    m = Mm[:, 4 * rnd:4 * rnd + 4, :]
                    V.tensor_tensor(m, m, CBs[:, rnd, :].unsqueeze(1).to_broadcast([P, 4, 3 * P]),
                                    ALU.mult).then_inc(m2_m, 1)
                split_to(chunk0(layer, "xk1") + HRING)
                dve.wait_ge(m2_y, layer + 1)
                om = xn[:, :, 512:1024]
                link(V.tensor_tensor(om, ytmp, pb[:, 4:6, :], ALU.add))
                link(V.tensor_tensor(om, om, zs, ALU.mult))
                link(V.tensor_tensor(sq, xn, xn, ALU.mult))
                ss = ssq.rearrange("p (t c) -> p t c", c=10)
                V.tensor_reduce(ss[:, :, 0:8], sq[:, :, 0:512].rearrange("p t (h d) -> p t h d", d=DH), AX.X, ALU.add)
                link(V.tensor_reduce(ss[:, :, 8:10], sq[:, :, 512:1024].rearrange("p t (h d) -> p t h d", d=256),
                                     AX.X, ALU.add))
                V.tensor_scalar(ss[:, :, 0:8], ss[:, :, 0:8], 1.0 / DH, EPS, ALU.mult, ALU.add)
                V.tensor_scalar(ss[:, :, 8:10], ss[:, :, 8:10], 1.0 / 256, EPS, ALU.mult, ALU.add).then_inc(ss_ready, 1)
                after("xk1", layer)
                root()
                rs = rstd.rearrange("p (t c) -> p t c", c=10)
                for t in range(NT):
                    a = xn[:, t, 0:512].rearrange("p (h d) -> p h d", d=DH)
                    V.tensor_tensor(a, a, bc(rs[:, t, 0:8], DH), ALU.mult)
                    a = xn[:, t, 512:1024].rearrange("p (h d) -> p h d", d=256)
                    ins = V.tensor_tensor(a, a, bc(rs[:, t, 8:10], 256), ALU.mult)
                link(ins)
                V.tensor_tensor(xn[:, :, 256:512], xn[:, :, 256:512], gate, ALU.mult).then_inc(xn_ready, 1)
                split_to(chunk0(layer, "xv0") + HRING)
                turn_out(norm_no(layer, "mixed"), xTh, xTl, par_("out_w", layer))
                after("xv0", layer)
                add_rows("out0", layer, 0)
                after("out0", layer)
                add_rows("out1", layer, 1)
                dve.wait_ge(lin_dve, evac_count(("out1", layer)))
                normalise(h)
                after("out1", layer)
                split_to(chunk0(layer, "xv1") + HRING)
                turn_out(norm_no(layer, "xa"), xTh, xTl, par_("xa_w", layer))
                after("xv1", layer)
                after("xq1", layer)
                for i in range(2):
                    dve.wait_ge(xa_lg, 2 * layer + i + 1)
                    V.tensor_reduce(nmax[:, 4 * i:4 * i + 4],
                                    pb[:, 4 + 2 * i:6 + 2 * i, :].rearrange("p b (t m) -> p (b t) m", t=NT), AX.X,
                                    ALU.max, negate=True).then_inc(xa_max, 1)
                for i in range(2):
                    c = slice(4 * i, 4 * i + 4)
                    dve.wait_ge(xa_p, 2 * layer + i + 1)
                    link(V.reciprocal(rinv[:, c], rsum[:, c]))
                    V.tensor_tensor(Px[:, c, :], Px[:, c, :], bc(rinv[:, c], S), ALU.mult).then_inc(xa_pn, 1)
                dve.wait_ge(xa_pt, 2 * layer + 2)
                V.tensor_copy(PTx[:, 2:4, :, :].rearrange("p h m s -> p h (m s)"), pb[:, 6:8, :]).then_inc(xa_ptd, 1)
                for i in range(2):
                    dve.wait_ge(xa_oh, 2 * layer + i + 1)
                    V.tensor_tensor(xTl[:, 4 * i:4 * i + 4, :].rearrange("p (b a) s -> p b (a s)", a=2),
                                    pb[:, 4 + 2 * i:6 + 2 * i, :],
                                    xTh[:, 4 * i:4 * i + 4, :].rearrange("p (b a) s -> p b (a s)", a=2).bitcast(F32),
                                    ALU.subtract).then_inc(xa_ol, 1)
                after("xq1", layer)
                add_rows("xo0", layer, 0)
                after("xo0", layer)
                add_rows("xo1", layer, 1)
                dve.wait_ge(lin_dve, evac_count(("xo1", layer)))
                normalise(h)
                after("xo1", layer)
                turn_out(norm_no(layer, "ffn"), xTh, xTl, par_("ffn_w", layer))
                if layer == 0:
                    for j in range(NF // 2):
                        split_to(chunk0(0) + 2 * j + 1 + HRING)
                        dve.wait_ge(silu_ready, j + 1)
                        b = 2 * (j % 2)
                        V.tensor_tensor(gated[:, j % 2, :, :], silu[:, j % 2, :, :], pb[:, b:b + 2, S:2 * S],
                                        ALU.mult).then_inc(g_ready, 1)
                        dve.wait_ge(g_ready, j + 1)
                        dve.wait_ge(hT_hi, j + 1)
                        V.tensor_tensor(hTl[:, 2 * j:2 * j + 2, :], gated[:, j % 2, :, :],
                                        hTh[:, 2 * j:2 * j + 2, :].bitcast(F32), ALU.subtract).then_inc(hT_lo, 1)
                    split_to(chunk0(0) + FFN_CHUNKS - 2 + HRING)
                    dve.wait_ge(w_used, chunk0(0) + FFN_CHUNKS)
                    for t in (1, 0):
                        hh = h[:, t, :].rearrange("p (n c) -> p n c", c=512)
                        V.tensor_tensor(hh, hh, pb[:, 4 + 2 * t:6 + 2 * t, :],
                                        ALU.add).then_inc(rows_ready if t else ffn_added, 1)
                    dve.wait_ge(ffn_added, 1)

            dve.wait_ge(xT_lo, 4 * norm_no(1, "ffn") + 4)
            V.tensor_tensor(xfull, xTh.bitcast(F32), xTl.bitcast(F32), ALU.add).then_inc(rt_sum, 1)
            def first_chunks(p):
                for c in range(HRING):
                    dve.wait_ge(hi_ready, moe_chunk(p) + c + 1)
                    V.tensor_tensor(xlo_slots[c], xraw_slots[c], whi[:, (MOE0 + c) % HRING, :].bitcast(F32),
                                    ALU.subtract).then_inc(lo_ready, 1)

            dve.wait_ge(xn_hi, 1)
            V.tensor_tensor(xnl, xn, xnh.bitcast(F32), ALU.subtract).then_inc(xn_lo, 1)
            dve.wait_ge(rt_lg, 1)
            link(V.tensor_copy(lg, pb[:, 4, 0:NT * NE].rearrange("p (t e) -> p t e", e=NE)))
            for t in range(NT):
                link(V.max(top8[:, t, :], lg[:, t, :]))
                link(V.max_index(idx8[:, t, :].bitcast(U32), top8[:, t, :], lg[:, t, :]))
                V.tensor_copy(idxf[:, t, :], idx8[:, t, :].bitcast(U32))
                ins = V.tensor_tensor(gd[:, t:t + 1], top8[:, t, 1:2], top8[:, t, 0:1], ALU.subtract)
            ins.then_inc(rt_d, 1)
            link(V.memset(gates, 0.0))
            iota8 = const("iota")[:, 0:NE]
            for t in range(NT):
                V.tensor_scalar(oh[:, t, :], iota8, idxf[:, t, 0:1], None, ALU.is_equal)
                ins = V.tensor_scalar(lg[:, t, :], iota8, idxf[:, t, 1:2], None, ALU.is_equal)
            link(ins)
            V.tensor_tensor(routed, oh, lg, ALU.add).then_inc(rt_sum, 1)
            first_chunks(0)
            dve.wait_ge(rt_e, 1)
            link(V.tensor_scalar(gs, ge, 1.0, None, ALU.add))
            link(V.reciprocal(g12[:, 0, :], gs))
            link(V.tensor_tensor(g12[:, 1, :], g12[:, 0, :], ge, ALU.mult))
            for t in range(NT):
                V.tensor_scalar(oh[:, t, :], oh[:, t, :], g12[:, 0, t:t + 1], None, ALU.mult)
            link(V.tensor_scalar(lg[:, 0, :], lg[:, 0, :], g12[:, 1, 0:1], None, ALU.mult))
            link(V.tensor_scalar(lg[:, 1, :], lg[:, 1, :], g12[:, 1, 1:2], None, ALU.mult))
            link(V.tensor_tensor(gates[:, :, 1:NE + 1], oh, lg, ALU.add))
            dve.wait_ge(rt_rank, 1)
            link(V.memset(pos, 4.0 * S))
            link(V.tensor_scalar(oh, routed, -4.0 * S, 4.0 * S, ALU.mult, ALU.add))
            link(V.tensor_tensor(pos[:, 0, :, 0:NE], oh, pb[:, 5, 0:NT * NE].rearrange("p (t e) -> p t e", e=NE), ALU.add))
            link(V.tensor_scalar(pos[:, 1, :, 0:NE], pos[:, 0, :, 0:NE], -float(P), None, ALU.add))
            link(V.tensor_reduce(most, pb[:, 5, 2 * NE:3 * NE], AX.X, ALU.max))
            V.tensor_scalar(over_flag.bitcast(U32), most, float(P), None, ALU.is_gt).then_inc(routed_ok, 1)
            dve.wait_ge(routed_ok, 1)

            def experts(p):
                def select_tokens(col, e):
                    for t in range(NT):
                        ins = V.tensor_scalar(sel[:, e, t, :], const("iota"), pos[:, p, t, bass.ds(col, 1)], None,
                                              ALU.is_equal)
                    ins.then_inc(sel_ready, 1)

                def gathered_lo(count, e):
                    dve.wait_ge(xg_hi, count + 1)
                    w = par_("ffn_w", 1)
                    for k in range(KT):
                        ins = V.scalar_tensor_tensor(
                            out=xgl[:, e, k, :], in0=pb[:, 6 + k // 4, (k % 4) * P:(k % 4 + 1) * P],
                            scalar=w[:, k:k + 1], in1=xgh[:, e, k, :].bitcast(F32), op0=ALU.mult, op1=ALU.subtract)
                    ins.then_inc(xg_lo, 1)

                def outputs_lo(count):
                    dve.wait_ge(y_hi, count + 1)
                    V.tensor_tensor(yl.rearrange("p (a c) -> p a c", a=2), pb[:, 2:4, :],
                                    yh.rearrange("p (a c) -> p a c", a=2).bitcast(F32),
                                    ALU.subtract).then_inc(y_lo, 1)

                def add_outputs(count, col, t):
                    dve.wait_ge(spread, count * 2 + (t + 1))
                    for half in range(2):
                        hh = h[:, t, half * 512:(half + 1) * 512]
                        ins = V.scalar_tensor_tensor(out=hh, in0=pb[:, 6 + half, :],
                                                     scalar=gates[:, t, bass.ds(col, 1)], in1=hh,
                                                     op0=ALU.mult, op1=ALU.add)
                    ins.then_inc(ffn_added, 1)

                V.memset(sel[:, 1, :, :].bitcast(F32), 0.0)
                select_tokens(0, 0)
                gathered_lo(p * (NE + 1), 0)

                def two_experts(pair, last):
                    for e in range(2):
                        expert = pair * 2 + (e + p * NE)
                        lag = pair * 2 + (e + p * (NE + 1))
                        done = [HRING]

                        def split_experts(m):
                            while done[0] <= m and not (last and e * FFN_CHUNKS + done[0] >= 2 * FFN_CHUNKS):
                                c = e * FFN_CHUNKS + done[0]
                                dve.wait_ge(hi_ready, pair * (2 * FFN_CHUNKS) + (moe_chunk(p) + c + 1))
                                V.tensor_tensor(xlo_slots[c % XRING], xraw_slots[c % XRING], whi[:, (MOE0 + c) % HRING, :].bitcast(F32),
                                                ALU.subtract).then_inc(lo_ready, 1)
                                done[0] += 1

                        def hidden_lo(j):
                            dve.wait_ge(hT_hi, expert * (NF // 2) + (NF // 2 + j + 1))
                            V.tensor_tensor(hTl[:, 2 * j:2 * j + 2, 0:P],
                                            pb[:, 4 + j % 2, 0:2 * P].rearrange("p (f s) -> p f s", f=2),
                                            hTh[:, 2 * j:2 * j + 2, 0:P].bitcast(F32),
                                            ALU.subtract).then_inc(hT_lo, 1)

                        outputs_lo(lag)
                        for j in range(NF // 2):
                            split_experts(2 * j + 1 + HRING)
                            dve.wait_ge(silu_ready, expert * (NF // 2) + (NF // 2 + j + 1))
                            V.tensor_tensor(xgated[:, j % 2, :], xsilu[:, j % 2, :], pb[:, j % 2, S:2 * S],
                                            ALU.mult).then_inc(g_ready, 1)
                            if j >= 1:
                                hidden_lo(j - 1)
                            if j == 3:
                                add_outputs(lag, pair * 2 + e, 0)
                            if j == 4:
                                dve.wait_ge(selT_psum, lag + 1)
                                select_tokens(pair * 2 + (e + 1), 1 - e)
                            if j == 6:
                                add_outputs(lag, pair * 2 + e, 1)
                            if j == 8:
                                gathered_lo(lag + 1, 1 - e)
                        split_experts(W1_CHUNKS + HRING)
                        hidden_lo(NF // 2 - 1)
                        split_experts(FFN_CHUNKS - 1 + HRING)

                with dve.Fori(0, NE // 2 - 1) as pair:
                    two_experts(pair, False)
                two_experts(NE // 2 - 1, True)
                count = p * (NE + 1) + NE
                outputs_lo(count)
                add_outputs(count, NE, 0)
                add_outputs(count, NE, 1)
                dve.wait_ge(ffn_added, 1 + 2 * (NE + 1) * (p + 1))

            experts(0)
            more = dve.value_load(over_flag[0:1, :].bitcast(U32), min_val=0, max_val=1)
            with dve.If(more):
                first_chunks(1)
                experts(1)
            V.memset(ssq[:, 1:2], 0.0).then_inc(rows_ready, 1)
            rstd_of(h)
            for t in range(NT):
                ins = V.scalar_tensor_tensor(out=xn[:, t, :], in0=h[:, t, :], scalar=rstd[:, t:t + 1],
                                             in1=par_("final_w"), op0=ALU.mult, op1=ALU.mult)
            ins.then_inc(fin_ready, 1)


def kernel(**inputs):
    import concourse.bacc as bacc
    from concourse.bass_utils import run_bass_kernel_spmd

    a = {k: np.asarray(v) for k, v in inputs.items()}

    def columns(w):
        return w.reshape(-1, P).T

    def rows(v):
        return np.broadcast_to(v[None, :], (P, v.shape[0]))

    par = []
    for l in range(DEPTH):
        heads = np.concatenate([a["fox_norm_w"][l], a["hg_norm_w"][l], a["m2_norm_w"][l]])
        par += [columns(a["mix_norm_w"][l]), columns(a["xa_norm_w"][l]), columns(a["xa_mem_norm_w"][l]),
                columns(a["ffn_norm_w"][l]), columns(heads),
                a["m2_conv_w"][l].reshape(4, 8, P).transpose(2, 1, 0).reshape(P, 32), columns(a["m2_conv_b"][l]),
                rows(a["fox_f_bias"][l]), rows(a["m2_dt_bias"][l]), rows(a["m2_a_log"][l]), rows(a["m2_d"][l])]
    par += [columns(a["hg_lb_raw"].reshape(-1)),
            a["moe_router"][0].reshape(KT, P, NE).transpose(1, 0, 2).reshape(P, KT * NE), rows(a["final_norm_w"])]
    par = np.ascontiguousarray(np.concatenate(par, axis=1))

    def projection(w, form):
        w = w.reshape(KT, P, 512)
        if form == "T":
            return [w[:, :, c * 256:(c + 1) * 256].transpose(1, 0, 2).reshape(P, CW) for c in range(2)]
        return [w[c * 4:(c + 1) * 4].transpose(1, 0, 2).reshape(P, CW) for c in range(2)]

    lin = []
    for l in range(DEPTH):
        w_in = a["w_in"][l]
        cut = np.cumsum([0, 256, 256, 256, FOX_H, 256, 256, 256, 256, 512, 1024, M2_H])
        fq, fk, fv, ff, hq, hf, hi, hg, z, xbc, dt = (w_in[:, i:j] for i, j in zip(cut[:-1], cut[1:]))
        pad = np.zeros((D, 512 - 256 - FOX_H - M2_H), w_in.dtype)
        w = {"hq_hf": np.concatenate([hq, hf], 1), "gate_small": np.concatenate([hg, ff, dt, pad], 1),
             "xbc0": xbc[:, :512], "xbc1": xbc[:, 512:], "fq_fk": np.concatenate([fq, fk], 1),
             "fv_hi": np.concatenate([fv, hi], 1), "z": z}
        for i in range(2):
            s = slice(512 * i, 512 * i + 512)
            w[f"xk{i}"], w[f"xv{i}"] = a["xa_w_kv"][l][:, :D][:, s], a["xa_w_kv"][l][:, D:][:, s]
            w[f"out{i}"], w[f"xq{i}"], w[f"xo{i}"] = a["w_out"][l][:, s], a["xa_w_q"][l][:, s], a["xa_w_o"][l][:, s]
        for name, form in PROJ:
            lin += projection(w[name], form)
    lin = np.stack(lin)

    def swiglu(w1, w2, expert):
        if expert:
            w1 = w1.reshape(2, KT // 2, P, 2, NF // 2, S).transpose(4, 0, 2, 1, 3, 5).reshape(NF, P, CW)
        else:
            w1 = w1.reshape(KT, P, 2, NF, P).transpose(3, 1, 0, 2, 4).reshape(NF, P, CW)
        w2 = w2.reshape(NF // 2, 2, P, D).transpose(0, 2, 1, 3).reshape(NF // 2, P, CW)
        return np.concatenate([w1, w2])

    ffn = np.stack([swiglu(a["ffn_w1"][0], a["ffn_w2"][0], False)] +
                   [swiglu(a["moe_w1"][0, e], a["moe_w2"][0, e], True) for e in range(NE)])
    arrays = {"x": a["x"], "mem": a["mem"], "par": par, "con": constants(), "lvl": level_masks(), "lin_w": lin,
              "ffn_w": ffn}
    nc = bacc.Bacc("TRN2", target_bir_lowering=False, num_devices=1)
    args = {}
    for name in list(arrays):
        arr = np.ascontiguousarray(arrays[name])
        arrays[f"in_{name}"] = arr
        del arrays[name]
        args[name] = nc.dram_tensor(f"in_{name}", arr.shape, mybir.dt.from_np(arr.dtype), kind="ExternalInput").ap()
    out = nc.dram_tensor("out_0", (1, S, D), F32, kind="ExternalOutput").ap()
    build(nc, out=out, **args)
    r = run_bass_kernel_spmd(nc, [arrays], core_ids=[0])
    return r.results[0]["out_0"]
```
